# Optimizing a Trainium2 kernel written in Bass

```python
import math
import jax
import jax.numpy as jnp
from jax import lax
import numpy as np

D_MODEL = 1024
BATCH = 1
SEQ = 1024
DEPTH = 2

CHUNK = 64
N_META = 16
Q_BLOCK = 128

A_HEADS = 4
A_DH = 64
A_DV = 2 * A_DH
A_QK = A_HEADS * 2 * A_DH
A_W = A_HEADS * A_DV
B_HEADS = 8
B_DH = 64
B_W = B_HEADS * B_DH
EVEN_W = A_W + B_W
EVEN_SPLITS = (A_QK, A_QK, A_W, A_W, B_W, B_W, B_W, B_W)
EVEN_IN = 2 * A_QK + 2 * A_W + 4 * B_W

C_HEADS = 8
C_NOPE = 128
C_ROPE = 64
C_DV = 128
C_QK = C_NOPE + C_ROPE
Q_LORA = 512
KV_LORA = 256
C_W = C_HEADS * C_DV
ODD_SPLITS = (Q_LORA, KV_LORA, C_ROPE, C_W)
ODD_IN = Q_LORA + KV_LORA + C_ROPE + C_W

ROPE_THETA = 10000.0
LN_EPS = 1e-5
RMS_EPS = 1e-6
ALPHA = (2.0 * DEPTH) ** 0.25
BETA = (8.0 * DEPTH) ** -0.25
N_EVEN = (DEPTH + 1) // 2
N_ODD = DEPTH // 2

kernel_name = "hybrid_diff_stickbreak_mla_streaming"

def layer_norm(x, g, b):
    xf = x.astype(jnp.float32)
    mu = jnp.mean(xf, axis=-1, keepdims=True)
    var = jnp.mean(jnp.square(xf - mu), axis=-1, keepdims=True)
    return ((xf - mu) * lax.rsqrt(var + LN_EPS) * g.astype(jnp.float32) + b.astype(jnp.float32)).astype(x.dtype)

def rms_norm(x, g):
    xf = x.astype(jnp.float32)
    return (xf * lax.rsqrt(jnp.mean(xf * xf, axis=-1, keepdims=True) + RMS_EPS) * g.astype(jnp.float32)).astype(x.dtype)

def chunk_id(pos):
    return jnp.where(pos < N_META, 0, 1 + (pos - N_META) // CHUNK)

def split_cols(h, sizes):
    idx = np.cumsum(sizes)[:-1].tolist()
    return jnp.split(h, idx, axis=-1)

def rope(x, pos):
    half = x.shape[-1] // 2
    inv_freq = ROPE_THETA ** (-jnp.arange(half, dtype=jnp.float32) / half)
    ang = pos.astype(jnp.float32)[:, None] * inv_freq[None, :]
    cos = jnp.cos(ang)[None, :, None, :]
    sin = jnp.sin(ang)[None, :, None, :]
    x1 = x[..., :half].astype(jnp.float32)
    x2 = x[..., half:].astype(jnp.float32)
    return jnp.concatenate([x1 * cos - x2 * sin, x2 * cos + x1 * sin], axis=-1).astype(x.dtype)

def sweep_query_blocks(fn, q):
    L = q.shape[1]
    n_blocks = L // Q_BLOCK

    def body(i):
        q0 = i * Q_BLOCK
        return fn(q0, lax.dynamic_slice_in_dim(q, q0, Q_BLOCK, axis=1))

    out = lax.map(body, jnp.arange(n_blocks))
    out = jnp.moveaxis(out, 0, 1)
    return out.reshape((out.shape[0], L) + out.shape[3:])

def even_layer(x, pos, cid, layer_idx, w_in, w_out, lam_q1, lam_k1, lam_q2, lam_k2, subln_g):
    bsz, L, _ = x.shape
    qa, ka, va, ga, qs, ks, vs, gs = split_cols(x @ w_in, EVEN_SPLITS)

    qa = qa.reshape(bsz, L, A_HEADS, 2, A_DH)
    ka = ka.reshape(bsz, L, A_HEADS, 2, A_DH)
    va = va.reshape(bsz, L, A_HEADS, A_DV)
    lam_init = 0.8 - 0.6 * math.exp(-0.3 * layer_idx)
    lam = (jnp.exp(jnp.sum(lam_q1.astype(jnp.float32) * lam_k1.astype(jnp.float32)))
           - jnp.exp(jnp.sum(lam_q2.astype(jnp.float32) * lam_k2.astype(jnp.float32)))
           + lam_init)
    slopes = jnp.asarray(2.0 ** (-8.0 * np.arange(1, A_HEADS + 1) / A_HEADS), dtype=jnp.float32)

    def diff_block(q0, qb):
        tq = q0 + jnp.arange(Q_BLOCK)
        s = jnp.einsum('bqhmd,bkhmd->bhmqk', qb, ka).astype(jnp.float32) * (A_DH ** -0.5)
        dist = jnp.abs(tq[:, None] - pos[None, :]).astype(jnp.float32)
        s = s - slopes[None, :, None, None, None] * dist
        visible = cid[None, :] <= chunk_id(tq)[:, None]
        p = jax.nn.softmax(jnp.where(visible, s, -jnp.inf), axis=-1)
        w = p[:, :, 0] - lam * p[:, :, 1]
        return jnp.einsum('bhqk,bkhd->bqhd', w.astype(va.dtype), va)

    oa = sweep_query_blocks(diff_block, qa)
    oa = rms_norm(oa, subln_g) * (1.0 - lam_init)
    ya = oa.reshape(bsz, L, A_W) * jax.nn.silu(ga)

    qs = qs.reshape(bsz, L, B_HEADS, B_DH)
    ks = ks.reshape(bsz, L, B_HEADS, B_DH)
    vs = vs.reshape(bsz, L, B_HEADS, B_DH)

    def sb_block(q0, qb):
        tq = q0 + jnp.arange(Q_BLOCK)
        z = jnp.einsum('bqhd,bkhd->bhqk', qb, ks).astype(jnp.float32) * (B_DH ** -0.5)
        earlier = pos[None, :] < tq[:, None]
        log_skip = jnp.where(earlier, jax.nn.log_sigmoid(-z), 0.0)
        log_pass = lax.cumsum(log_skip, axis=3, reverse=True) - log_skip
        a = jnp.where(earlier, jnp.exp(jax.nn.log_sigmoid(z) + log_pass), 0.0)
        return jnp.einsum('bhqk,bkhd->bqhd', a.astype(vs.dtype), vs)

    ys = sweep_query_blocks(sb_block, qs).reshape(bsz, L, B_W) * jax.nn.silu(gs)

    return jnp.concatenate([ya, ys], axis=-1) @ w_out

def odd_layer(x, pos, cid, w_in, q_norm, w_uq, kv_norm, w_ukv, w_out):
    bsz, L, _ = x.shape
    cq, ckv, k_pe, g = split_cols(x @ w_in, ODD_SPLITS)

    q = (rms_norm(cq, q_norm) @ w_uq).reshape(bsz, L, C_HEADS, C_QK)
    q = jnp.concatenate([q[..., :C_NOPE], rope(q[..., C_NOPE:], pos)], axis=-1)
    kv = (rms_norm(ckv, kv_norm) @ w_ukv).reshape(bsz, L, C_HEADS, C_NOPE + C_DV)
    k_pe = rope(k_pe[:, :, None, :], pos)
    k = jnp.concatenate([kv[..., :C_NOPE], jnp.broadcast_to(k_pe, (bsz, L, C_HEADS, C_ROPE))], axis=-1)
    v = kv[..., C_NOPE:]

    def mla_block(q0, qb):
        tq = q0 + jnp.arange(Q_BLOCK)
        s = jnp.einsum('bqhd,bkhd->bhqk', qb, k).astype(jnp.float32) * (C_QK ** -0.5)
        visible = cid[None, :] <= chunk_id(tq)[:, None]
        p = jax.nn.softmax(jnp.where(visible, s, -jnp.inf), axis=-1)
        return jnp.einsum('bhqk,bkhd->bqhd', p.astype(v.dtype), v)

    o = sweep_query_blocks(mla_block, q).reshape(bsz, L, C_W) * jax.nn.silu(g)
    return o @ w_out

def setup_inputs(seed: int = 0) -> dict:
    key = jax.random.key(seed)
    k = jax.random.split(key, 18)
    n = jax.random.normal
    f32 = jnp.float32
    return {
        "x": n(k[0], (BATCH, SEQ, D_MODEL), f32),
        "meta": n(k[1], (N_META, D_MODEL), f32),
        "ln_g": 1.0 + 0.02 * n(k[2], (DEPTH, D_MODEL), f32),
        "ln_b": 0.02 * n(k[3], (DEPTH, D_MODEL), f32),
        "ev_w_in": n(k[4], (N_EVEN, D_MODEL, EVEN_IN), f32) * D_MODEL ** -0.5,
        "ev_w_out": n(k[5], (N_EVEN, EVEN_W, D_MODEL), f32) * (EVEN_W ** -0.5 * BETA),
        "ev_lam_q1": 0.1 * n(k[6], (N_EVEN, A_DH), f32),
        "ev_lam_k1": 0.1 * n(k[7], (N_EVEN, A_DH), f32),
        "ev_lam_q2": 0.1 * n(k[8], (N_EVEN, A_DH), f32),
        "ev_lam_k2": 0.1 * n(k[9], (N_EVEN, A_DH), f32),
        "ev_subln": 1.0 + 0.02 * n(k[10], (N_EVEN, A_DV), f32),
        "od_w_in": n(k[11], (N_ODD, D_MODEL, ODD_IN), f32) * D_MODEL ** -0.5,
        "od_q_norm": 1.0 + 0.02 * n(k[12], (N_ODD, Q_LORA), f32),
        "od_w_uq": n(k[13], (N_ODD, Q_LORA, C_HEADS * C_QK), f32) * Q_LORA ** -0.5,
        "od_kv_norm": 1.0 + 0.02 * n(k[14], (N_ODD, KV_LORA), f32),
        "od_w_ukv": n(k[15], (N_ODD, KV_LORA, C_HEADS * (C_NOPE + C_DV)), f32) * KV_LORA ** -0.5,
        "od_w_out": n(k[16], (N_ODD, C_W, D_MODEL), f32) * (C_W ** -0.5 * BETA),
    }

def reference(x, meta, ln_g, ln_b, ev_w_in, ev_w_out, ev_lam_q1, ev_lam_k1, ev_lam_q2, ev_lam_k2,
              ev_subln, od_w_in, od_q_norm, od_w_uq, od_kv_norm, od_w_ukv, od_w_out):
    bsz, seq, d = x.shape
    L = N_META + seq
    L_pad = -(-L // Q_BLOCK) * Q_BLOCK
    h = jnp.concatenate([
        jnp.broadcast_to(meta.astype(x.dtype)[None], (bsz, N_META, d)),
        x,
        jnp.zeros((bsz, L_pad - L, d), x.dtype),
    ], axis=1)
    pos = jnp.arange(L_pad)
    cid = chunk_id(pos)

    for i in range(DEPTH):
        j = i // 2
        if i % 2 == 0:
            y = even_layer(h, pos, cid, i, ev_w_in[j], ev_w_out[j], ev_lam_q1[j], ev_lam_k1[j],
                           ev_lam_q2[j], ev_lam_k2[j], ev_subln[j])
        else:
            y = odd_layer(h, pos, cid, od_w_in[j], od_q_norm[j], od_w_uq[j], od_kv_norm[j],
                          od_w_ukv[j], od_w_out[j])
        h = layer_norm(ALPHA * h + y, ln_g[i], ln_b[i])

    return h[:, N_META:N_META + seq]


_drawn_inputs = setup_inputs


def setup_inputs(seed=0):
    import zlib

    import numpy as np

    out = dict(_drawn_inputs(seed))
    spreads = {}
    factors = {'meta': 4.227,
     'ev_lam_q1': 64.0,
     'ev_lam_k1': 6.28,
     'ev_lam_q2': 4.479,
     'ev_lam_k2': 8.0,
     'ev_subln': 8.0,
     'od_q_norm': 8.0,
     'od_w_uq': 2.98,
     'od_kv_norm': 8.0}
    for name, (base, spread) in spreads.items():
        noise = np.random.default_rng([zlib.crc32(name.encode()), seed]).standard_normal(out[name].shape)
        drawn = base * np.exp(spread * noise) if base else spread * noise
        out[name] = jnp.asarray(drawn.astype(out[name].dtype))
    for name, factor in factors.items():
        out[name] = (out[name] * factor).astype(out[name].dtype)
    return out
```

```python
import concourse.bass as bass
from concourse import mybir
from contextlib import ExitStack
import math
import numpy as np

F32 = mybir.dt.float32
F32R = mybir.dt.float32r
BF16 = mybir.dt.bfloat16
F16 = mybir.dt.float16
ALU = mybir.AluOpType
ACT = mybir.ActivationFunctionType
AX_X = mybir.AxisListType.X

META, SEQ, D = 16, 1024, 1024
TOK = META + SEQ
KD = D // 128
CHUNK = 64
CHUNKS = [(0, 352), (352, 344), (696, 344)]
NB = SEQ // 128
A_UNITS, B_UNITS, HEADS = 4, 4, 8
UNITS = A_UNITS + B_UNITS
DH = 64
SCALE64 = DH ** -0.5
SLOPES = [2.0 ** (-8.0 * (h + 1) / A_UNITS) for h in range(A_UNITS)]
SCALE192 = 192 ** -0.5
LAM_INIT = 0.8 - 0.6 * math.exp(0.0)
ALPHA = 4.0 ** 0.25
LN_EPS, RMS_EPS = 1e-5, 1e-6
QL_T, KVL_T = 4, 2
MASKED = -1.0e30
NRING = 3
SBANKS = 3
META_Q = NB


def keys_of(i):
    return META if i == META_Q else META + 128 * (i + 1)


def score_chunks(i):
    n = keys_of(i)
    if n <= 512:
        return [(0, n)]
    if n <= 1024:
        return [(0, n // 2), (n // 2, n // 2)]
    return list(CHUNKS)


def query_cols(i):
    return (0, META) if i == META_Q else (META + 128 * i, 128)


def turns_of(blocks):
    if blocks == [META_Q]:
        return [[0]]
    top = blocks[-1] + 1
    return [[0]] + [[a, a + 1] for a in range(1, top, 2)]


def make_plan():
    plan = []
    groups = []
    tsteps = []

    def group_list(layer, u):
        x = [[2 * j, 2 * j + 1] for j in range(NB // 2)]
        if layer == 1:
            return [(1, "C", u, 0, b) for b in x]
        if u < A_UNITS:
            return [(0, "A", u, 0, b) for b in x + [[META_Q]]]
        return [(0, "B", u, m, b) for m in range(2) for b in x + [[META_Q]]]

    def proj(kind, u):
        return [("P", kind, u, c) for c in range(len(CHUNKS))]

    pending = [None]
    final = [None]

    def finish():
        if final[0] is not None:
            layer, u = final[0]
            if layer == 0 and u < A_UNITS:
                plan.append(("SQ", u))
                plan.extend(proj("rms0", u))
            plan.append(("F", layer, u))
            final[0] = None

    def value(last):
        if pending[0] is not None:
            plan.append(("V", pending[0]))
            layer, _, u, _, _ = groups[pending[0]]
            if last:
                final[0] = (layer, u)
            pending[0] = None

    def run_layer(layer, fills, q_next):
        for u in range(UNITS):
            gl = group_list(layer, u)
            total = sum(keys_of(i) for g in gl for i in g[4])
            fill, done, placed = list(fills(u)), 0, 0
            count = len(fill)
            for gi, g in enumerate(gl):
                gid = len(groups)
                groups.append(g)
                ts = []
                for slot, i in enumerate(g[4]):
                    t = len(tsteps)
                    tsteps.append((gid, i, slot))
                    ts.append(t)
                    plan.append(("S", t))
                    if slot == 1:
                        plan.append(("C", ts[0]))
                    if gi == 0 and slot == 0:
                        value(True)
                        finish()
                    done += keys_of(i)
                    want = math.ceil(count * min(1.0, done * 1.15 / total))
                    while placed < want:
                        plan.append(fill[placed])
                        placed += 1
                if gi > 0:
                    value(False)
                if gi == len(gl) - 1:
                    plan.extend(q_next(u))
                plan.append(("C", ts[-1]))
                pending[0] = gid
        value(True)
        finish()

    for kind in ("k0", "v0", "q0"):
        plan.extend(proj(kind, 0))
    plan.append(("VT", 0, 0))

    def fills0(u):
        out = proj("g0", u)
        if u + 1 == UNITS:
            out += [("WO", 0)]
        else:
            out += proj("k0", u + 1) + proj("v0", u + 1) + [("VT", 0, u + 1)]
        return out

    run_layer(0, fills0, lambda u: proj("q0", u + 1) if u + 1 < UNITS else [])
    for b in range(NB + 1):
        plan.append(("O", 0, b))
    plan.append(("OT", 0))
    for j in range(QL_T):
        plan.extend(proj("cq", j))
    for j in range(KVL_T):
        plan.extend(proj("ckv", j))
    plan.extend(proj("kpe", 0))
    plan.extend(proj("g1", 0))
    plan.extend(proj("ncq", 0))
    plan.extend(proj("g1", 1))
    plan.extend(proj("nckv", 0))
    for h in range(2, HEADS):
        plan.extend(proj("g1", h))
    plan.append(("NEXT",))
    for kind in ("kn", "vn", "qr", "qn"):
        plan.extend(proj(kind, 0))
    plan.append(("VT", 1, 0))

    def fills1(u):
        out = [("L", u)]
        if u + 1 < HEADS:
            out += proj("kn", u + 1) + proj("vn", u + 1) + [("VT", 1, u + 1)]
        else:
            out += [("WO", 1)]
        return out

    run_layer(1, fills1, lambda u: (proj("qr", u + 1) if (u + 1) % 2 == 0 else []) + proj("qn", u + 1)
              if u + 1 < HEADS else [])
    for b in range(NB):
        plan.append(("O", 1, b))
    return plan, groups, tsteps


PLAN, GROUPS, TSTEPS = make_plan()
NORMS = ("rms0", "ncq", "nckv")
KT_OF = {"q0": KD, "k0": KD, "v0": KD, "g0": KD, "cq": KD, "ckv": KD, "kpe": KD, "g1": KD,
         "kn": KVL_T, "vn": KVL_T, "qn": QL_T, "qr": QL_T}
PROJ = [s for s in PLAN if s[0] == "P"]
PTURN = {s: n for n, s in enumerate(PROJ)}
N_CONSTS = 7
TILES = []
for _s in PROJ:
    if _s[1] not in NORMS and _s[3] == 0:
        TILES.append(_s[1:3])
TILE_AT = {s: n for n, s in enumerate(TILES)}
_l0 = sum(1 for k, _ in TILES if k[1] == "0")
WEIGHTS = TILES[:_l0] + [("wo0", k) for k in range(KD)] + TILES[_l0:] + [("wo1", k) for k in range(KD)]
WEIGHT_AT = {s: n for n, s in enumerate(WEIGHTS)}
NO_HI = ("v0", "vn", "cq", "ckv")


def count_before(items, good):
    out, n = {}, 0
    for s in items:
        n += bool(good(s))
        out[s] = n
    return out


HI_COUNT = count_before(PROJ, lambda s: s[1] not in NO_HI)
S_CHUNK, _n = {}, 0
S_OWNER = []
for _t, (_g, _i, _) in enumerate(TSTEPS):
    for _m in range(2 if GROUPS[_g][1] == "A" else 1):
        for _c in range(len(score_chunks(_i))):
            S_CHUNK[_t, _m, _c] = len(S_OWNER)
            S_OWNER.append("dve" if GROUPS[_g][1] == "A" else "act")
S_FREED = [S_OWNER[:n + 1].count(S_OWNER[n]) for n in range(len(S_OWNER))]
MAPS_DONE, _n = {}, 0
for _t, (_g, _i, _) in enumerate(TSTEPS):
    for _m in range(2 if GROUPS[_g][1] == "A" else 1):
        _n += 1
        MAPS_DONE[_t, _m] = _n
STATS_DONE = {}
_n = 0
for _t, (_g, _i, _) in enumerate(TSTEPS):
    if GROUPS[_g][1] != "B":
        for _m in range(2 if GROUPS[_g][1] == "A" else 1):
            _n += 1
            STATS_DONE[_t, _m] = _n
T_TURN, RING, _t, _r = {}, {}, 0, 0
for _s in PLAN:
    if _s[0] == "VT":
        for _k in range(3):
            T_TURN[_s, _k] = _t
            _t += 1
    if _s[0] == "V":
        for _k in range(len(turns_of(GROUPS[_s[1]][4]))):
            T_TURN[_s, _k] = _t
            RING[_s[1], _k] = _r
            _t, _r = _t + 1, _r + 1
    if _s[0] == "O" and _s[1] == 0:
        for _k in range(2):
            T_TURN[_s, _k] = _t
            _t += 1
B_GROUPS = [g for g in range(len(GROUPS)) if GROUPS[g][1] == "B"]
GROUP_STEPS = {g: [t for t in range(len(TSTEPS)) if TSTEPS[t][0] == g] for g in range(len(GROUPS))}
LAST_T = {g: T_TURN[("V", g), len(turns_of(GROUPS[g][4])) - 1] for g in range(len(GROUPS))}
V_TILES = [[0, 1, 2], [3, 4, 5], [6, 7, 8]]
FINALS = [s for s in PLAN if s[0] == "F"]
F_AT = {s: n for n, s in enumerate(FINALS)}
O_STEPS = [s for s in PLAN if s[0] == "O"]
O_AT = {s: n for n, s in enumerate(O_STEPS)}
G1_STORES = HEADS


def square_at(kind, c, j):
    return QL_T * c + j if kind == "ncq" else QL_T * len(CHUNKS) + KVL_T * c + j


def square_used(k):
    n_cq = QL_T * len(CHUNKS)
    kind, nt, c, j = ("ncq", QL_T, *divmod(k, QL_T)) if k < n_cq else ("nckv", KVL_T, *divmod(k - n_cq, KVL_T))
    if j == nt - 1:
        return "proj_done", PTURN[("P", kind, 0, c)] + 1
    before = c * (nt - 1) + (0 if kind == "ncq" else len(CHUNKS) * (QL_T - 1))
    return "lsq_used", before + j + 1


def unit_groups(layer, u):
    return [g for g in range(len(GROUPS)) if GROUPS[g][0] == layer and GROUPS[g][2] == u]


def q_scale(u):
    return SCALE64 / SLOPES[u] if u < A_UNITS else 1.0


def last_turn(kind, u):
    return PTURN[("P", kind, u, len(CHUNKS) - 1)]


def trunk_kernel(nc, ht, x, meta, w0, wo0, w1, wuq_n, wuq_r, wukv, wo1, lng, lnb, lam, subln,
                 qnorm, kvnorm, dist, masks, eyeb, rope, out):
    yd = nc.dram_tensor("y_scratch", (2, UNITS, 128, TOK), F32, kind="Internal").ap()
    gd = nc.dram_tensor("gate_scratch", (HEADS, 128, TOK), F32, kind="Internal").ap()
    hd = nc.dram_tensor("h1_scratch", (SEQ, D), F32, kind="Internal").ap()

    ctx = ExitStack()
    with ctx:
        def sem(name):
            return ctx.enter_context(nc.semaphore(name))

        def sb(name, shape, dt, where=ctx):
            return where.enter_context(nc.sbuf_tensor(name, shape, dt))

        big = sb("big", [128, 2, KD, TOK], F32R)
        wraw = sb("wraw", [128, 2, KD * 128], F32)
        wsp = sb("wsp", [128, 2, 2, KD, 128], F32R)
        eye = sb("eye", [128, 128], F32)
        ones = sb("ones", [128, 128], F32)
        eyebf = sb("eyebf", [128, 128], BF16)
        mask = sb("mask", [128, 2, 128], BF16)
        stat = sb("stat", [128, 4, 16], F32)
        small = sb("small", [128, 64], F32)
        lamv = sb("lamv", [128, 4, DH], F32)
        eps = sb("eps", [128, 2], F32)
        rmsg = sb("rmsg", [128, 8], F32)
        wok = big[:, :, :, 0:D]

        st = ExitStack()
        xin = sb("xin", [128, 2, TOK], F32, st)
        st.close()
        st = ExitStack()
        kst = sb("kst", [128, 2, 2, TOK], F32R, st)
        qst = sb("qst", [128, 2, 2, TOK], F32R, st)
        vtok = sb("vtok", [128, 2, 2, 9, 128], F32R, st)
        vt = sb("vt", [128, TOK], F32, st)
        gate = sb("gate", [128, TOK], F32, st)
        ot = sb("ot", [128, TOK], F32, st)
        ring = sb("ring", [128, NRING, 2, 512], F32R, st)
        tb = sb("tb", [128, 2, 2, TOK], F32, st)
        pb = sb("pb", [128, 2, 2, TOK], F32, st)
        sq = sb("sq", [128, TOK], F32, st)
        otmp = sb("otmp", [64, 256], F32, st)
        distt = sb("distt", [128, TOK], F16, st)
        st.close()
        st = ExitStack()
        h1t = sb("h1t", [128, 2, KD, TOK], F32R, st)
        st2 = ExitStack()
        yraw = sb("yraw", [128, 2, KD, 128], F32, st2)
        ysp = sb("ysp", [128, 2, 2, KD, 128], F32R, st2)
        xres = sb("xres", [128, 2, D], F32, st2)
        res = sb("res", [128, 2, D], F32, st2)
        lngb = sb("lngb", [128, 2, D], F32, st2)
        st2.close()
        st2 = ExitStack()
        lraw = sb("lraw", [128, QL_T + KVL_T, TOK], F32, st2)
        gtmp = sb("gtmp", [128, 2, TOK], F32, st2)
        st2.close()
        st.close()
        st = ExitStack()
        kh = sb("kh", [128, 2, 2, TOK], F32R, st)
        qh = sb("qh", [128, 2, TOK], F32R, st)
        qpe = sb("qpe", [128, 2, 2, TOK], F32R, st)
        vtok1 = sb("vtok1", [128, 2, 2, 9, 128], F32R, st)
        vt1 = sb("vt1", [128, TOK], F32, st)
        gate1 = sb("gate1", [128, TOK], F32, st)
        ot1 = sb("ot1", [128, TOK], F32, st)
        ring1 = sb("ring1", [128, NRING, 2, 512], F32R, st)
        pb1 = sb("pb1", [128, 2, 2, TOK], F32, st)
        ropet = sb("ropet", [128, 2, TOK], F32, st)
        kpe = sb("kpe", [128, TOK], F32R, st)
        rtmp = sb("rtmp", [128, 2, 352], F32, st)
        lsq = rtmp
        st.close()
        st = ExitStack()
        yraw1 = sb("yraw1", [128, 2, KD, 128], F32, st)
        ysp1 = sb("ysp1", [128, 2, 2, KD, 128], F32R, st)
        xres1 = sb("xres1", [128, 2, D], F32, st)
        res1 = sb("res1", [128, 2, D], F32, st)
        lngb1 = sb("lngb1", [128, 2, D], F32, st)
        st.close()

        bank = [ctx.enter_context(nc.psum_tensor(f"bank{n}", [128, 512], F32)) for n in range(8)]
        PJ, SC, TR, PO = bank[0:2], bank[2:5], bank[5:7], bank[7]

        lat = {"ncq": (0, QL_T, 1), "nckv": (QL_T, KVL_T, 1 + QL_T)}
        L0T = dict(ring=ring, pb=pb, vtok=vtok, vt=vt, gate=gate, ot=ot)
        L1T = dict(ring=ring1, pb=pb1, vtok=vtok1, vt=vt1, gate=gate1, ot=ot1)

        def bufs(layer):
            return L1T if layer else L0T

        names = """consts const_dve const_pool x_in_0 x_in_1 x_split w_raw_0 w_raw_1 w_ready w_used proj_done proj_hi
            proj_evac s_done s_free_dve s_free_act max_ready exp_done p_ready tr_done tr_hi tr_lo
            pv_done o_done o_tmp o_evac sq_done unit_done y_stored act_step dve_step pool_step
            g_done g_stored_0 g_stored_1 g_loaded y_in_0 y_in_1 res_in_0 res_in_1 y_split y_done y_evac
            res_used ln_mid ln_mid2 ln_norm ln_scaled h_ready h_stored_0 h_stored_1 lnp_in lam_exp rope_in
            lat_sq lsq_used x_hi ln_stats ln_rstd""".split()
        S = {n: sem(n) for n in names}

        def slot(name, n):
            return S[f"{name}_{n % 2}"]

        def arrived(eng, name, n):
            eng.wait_ge(slot(name, n), 16 * (n // 2 + 1))

        def all_arrived(eng, name, count):
            for n in range(max(count - 2, 0), count):
                arrived(eng, name, n)

        block = ctx.enter_context(nc.Block())
        lo_hi = lambda ap: ap.bitcast(F32)

        def rhs_of(kind):
            if kind in ("q0", "k0", "v0", "g0"):
                return big, 0
            if kind in ("cq", "ckv", "kpe", "g1"):
                return h1t, 0
            return (big, 0) if kind in ("qn", "qr") else (big, QL_T)

        def w_src(kind, u):
            if kind in ("q0", "k0", "v0", "g0"):
                return w0[u, "qkvg".index(kind[0])]
            if kind == "cq":
                return w1[u]
            if kind == "ckv":
                return w1[QL_T + u]
            if kind == "kpe":
                return w1[QL_T + KVL_T]
            if kind == "g1":
                return w1[QL_T + KVL_T + 1 + u]
            if kind == "qn":
                return wuq_n[u]
            if kind == "qr":
                return wuq_r[u // 2]
            return wukv[u, 0 if kind == "kn" else 1]

        LAST0 = last_turn("g0", UNITS - 1)
        LAST_IN1 = last_turn("g1", HEADS - 1)
        LAST1 = last_turn("qn", HEADS - 1)
        F_L0 = sum(1 for s in FINALS if s[1] == 0)

        @block.sync
        def _(sp):
            sp.dma_start(eyebf[:, :], eyeb).then_inc(S["consts"], 16)
            sp.dma_start(mask[:, :, :], masks).then_inc(S["consts"], 16)
            sp.dma_start(distt[:, :], dist).then_inc(S["consts"], 16)
            sp.dma_start(lamv[:, :, :], lam).then_inc(S["consts"], 16)
            sp.dma_start(rmsg[:, 0:1], subln).then_inc(S["consts"], 16)
            sp.dma_start(rmsg[:, 1:5], qnorm).then_inc(S["consts"], 16)
            sp.dma_start(rmsg[:, 5:7], kvnorm).then_inc(S["consts"], 16)

            def weights(upto):
                while issued[0] <= min(upto, len(WEIGHTS) - 1):
                    n = issued[0]
                    kind, u = WEIGHTS[n]
                    if n >= 2:
                        sp.wait_ge(S["w_ready"], n - 1)
                    if kind in ("wo0", "wo1"):
                        dst, src = wraw[:, n % 2, :], (wo1 if kind == "wo1" else wo0)[:, u, :]
                    else:
                        dst, src = wraw[:, n % 2, 0:KT_OF[kind] * 128], w_src(kind, u)
                    sp.dma_start(dst, src).then_inc(slot("w_raw", n), 16)
                    issued[0] += 1

            issued = [0]
            weights(0)
            for k in range(KD):
                if k >= 2:
                    sp.wait_ge(S["x_split"], k - 1)
                sp.dma_start(xin[:, k % 2, :], ht[:, k, :]).then_inc(slot("x_in", k), 16)
            weights(1)
            for s in PLAN:
                if s[0] == "P":
                    if s[1] not in NORMS and s[3] == 0:
                        weights(WEIGHT_AT[s[1:3]] + 2)
                    if s == ("P", "cq", 0, 0):
                        sp.wait_ge(S["tr_lo"], T_TURN[("O", 0, NB), 1] + 1)
                        all_arrived(sp, "h_stored", NB)
                        sp.dma_start(ropet[:, :, :], rope).then_inc(S["rope_in"], 16)
                    if s[1] == "g1" and s[3] == len(CHUNKS) - 1:
                        sp.wait_ge(S["proj_evac"], PTURN[s] + 1)
                        sp.dma_start(gd[s[2]], gtmp[:, s[2] % 2, :]).then_inc(slot("g_stored", s[2]), 16)
                if s[0] == "F":
                    n = F_AT[s]
                    sp.wait_ge(S["unit_done"], n + 1)
                    a = META if s[1] else 0
                    sp.dma_start(yd[s[1], s[2], :, a:TOK], bufs(s[1])["ot"][:, a:TOK]).then_inc(S["y_stored"], 16)
                if s[0] == "L":
                    if s[1] == 0:
                        all_arrived(sp, "g_stored", HEADS)
                    else:
                        sp.wait_ge(S["unit_done"], F_L0 + s[1])
                    sp.dma_start(gate1[:, :], gd[s[1]]).then_inc(S["g_loaded"], 16)
                if s[0] == "WO":
                    weights(WEIGHT_AT[("wo1" if s[1] else "wo0"), KD - 1])
                if s[0] == "O" and s[2] == 0:
                    layer = s[1]
                    fins = len(FINALS) if layer else F_L0
                    sp.wait_ge(S["y_stored"], 16 * fins)
                    g_, b_ = (lngb1 if layer else lngb)[:, 0, :], (lngb1 if layer else lngb)[:, 1, :]
                    sp.dma_start(g_, lng[layer:layer + 1, :].to_broadcast([128, D])).then_inc(S["lnp_in"], 16)
                    sp.dma_start(b_, lnb[layer:layer + 1, :].to_broadcast([128, D])).then_inc(S["lnp_in"], 16)
                if s[0] == "O":
                    layer, b = s[1], s[2]
                    n = O_AT[s]
                    rows = META if b == META_Q else 128
                    c0, _ = query_cols(b)
                    base = (NB + 1) * layer
                    yr, xr = (yraw1, xres1) if layer else (yraw, xres)
                    if n - base >= 2:
                        sp.wait_ge(S["y_split"], n - 1)
                    sp.dma_start(yr[:, n % 2, :, :],
                                 yd[layer, :, :, c0:c0 + 128].rearrange("u p c -> p u c")).then_inc(slot("y_in", n), 16)
                    if n - base >= 2:
                        sp.wait_ge(S["y_evac"], n - 1)
                    if layer:
                        all_arrived(sp, "h_stored", NB)
                    src = (hd[128 * b:128 * b + 128, :] if layer else
                           meta[:, :] if b == META_Q else x[128 * b:128 * b + 128, :])
                    sp.dma_start(xr[0:rows, n % 2, :], src).then_inc(slot("res_in", n), 16)
            all_arrived(sp, "h_stored", 2 * NB)


        @block.gpsimd
        def _(pool):
            step = [0]

            def tick(ins):
                step[0] += 1
                ins.then_inc(S["pool_step"], 1)
                return step[0]

            nc.gpsimd.memset(ones[:, :], 1.0).then_inc(S["const_pool"], 1)
            nc.gpsimd.memset(eps[:, 0:1], RMS_EPS).then_inc(S["const_pool"], 1)
            nc.gpsimd.memset(eps[:, 1:2], LN_EPS).then_inc(S["const_pool"], 1)
            pool.wait_ge(S["pool_step"], tick(nc.gpsimd.memset(eye[:, :], 0.0)))
            nc.gpsimd.affine_select(out=eye[:, :], in_=eye[:, :], compare_op=ALU.not_equal, fill=1.0,
                                    base=0, pattern=[[-1, 128]], channel_multiplier=1)\
                .then_inc(S["const_pool"], 1)

            def split(hi, lo, raw):
                pool.wait_ge(S["pool_step"], tick(nc.gpsimd.tensor_scalar(hi, raw, 1.0, 1.0, ALU.mult, ALU.mult)))
                return nc.gpsimd.tensor_tensor(lo, raw, lo_hi(hi), ALU.subtract)

            def split_weights(upto):
                while split_[0] <= min(upto, len(WEIGHTS) - 1):
                    n = split_[0]
                    kind, u = WEIGHTS[n]
                    arrived(pool, "w_raw", n)
                    if kind in ("wo0", "wo1"):
                        if u == 0:
                            pool.wait_ge(S["proj_done"], (LAST1 if kind == "wo1" else LAST0) + 1)
                        split(wok[:, 0, u, :], wok[:, 1, u, :], wraw[:, n % 2, :]).then_inc(S["w_ready"], 1)
                    else:
                        kt, i = KT_OF[kind], TILE_AT[kind, u]
                        if i >= 2:
                            pool.wait_ge(S["proj_done"], last_turn(*TILES[i - 2]) + 1)
                        split(wsp[:, i % 2, 0, 0:kt, :], wsp[:, i % 2, 1, 0:kt, :],
                              wraw[:, n % 2, 0:kt * 128].rearrange("p (k c) -> p k c", k=kt)).then_inc(S["w_ready"], 1)
                    split_[0] += 1

            split_ = [0]
            split_weights(0)
            for s in PLAN:
                if s[0] == "P" and s[1] not in NORMS and s[3] == 0:
                    split_weights(WEIGHT_AT[s[1:3]] + 1)
                if s[0] == "WO":
                    split_weights(WEIGHT_AT[("wo1" if s[1] else "wo0"), KD - 1])
                if s[0] == "O":
                    layer, b = s[1], s[2]
                    n = O_AT[s]
                    base = (NB + 1) * layer
                    yr, ys = (yraw1, ysp1) if layer else (yraw, ysp)
                    rs = res1 if layer else res
                    lg = lngb1 if layer else lngb

                    def y_split(m):
                        arrived(pool, "y_in", m)
                        if m - base >= 2:
                            pool.wait_ge(S["y_done"], m - 1)
                        split(ys[:, m % 2, 0, :, :], ys[:, m % 2, 1, :, :], yr[:, m % 2, :, :])\
                            .then_inc(S["y_split"], 1)

                    if n == base:
                        y_split(n)
                    if n + 1 < base + (NB if layer else NB + 1):
                        y_split(n + 1)
                    rows = META if b == META_Q else 128
                    pool.wait_ge(S["ln_scaled"], n + 1)
                    nc.gpsimd.tensor_tensor(rs[0:rows, n % 2, :], rs[0:rows, n % 2, :], lg[0:rows, 1, :],
                                            ALU.add).then_inc(S["h_ready"], 1)

        def p_free(eng, g):
            if g >= 2:
                eng.wait_ge(S["tr_done"], LAST_T[g - 2] + 1)

        def turn_extent(g, k):
            blocks = GROUPS[g][4]
            tiles = turns_of(blocks)[k]
            if blocks == [META_Q]:
                return META, META
            if tiles == [0]:
                return META, 256
            return 128, (384 if tiles[-1] == blocks[-1] + 1 else 512)

        def v_parts(s, k, part):
            _, layer, u = s
            tiles = V_TILES[k]
            a, b = tiles[0], tiles[-1] + 1
            src = TR[T_TURN[s, k] % 2][:, 0:384].rearrange("p (t d) -> p t d", t=3)
            v = bufs(layer)["vtok"]
            if layer == 1 or u < A_UNITS:
                return [(v[:, u % 2, part, a:b, :], v[:, u % 2, 0, a:b, :], src)]
            return [(v[:, u % 2, m, a:b, DH * part:DH * part + DH], v[:, u % 2, m, a:b, 0:DH],
                     src[:, :, DH * m:DH * m + DH]) for m in range(2)]

        @block.scalar
        def _(act):
            A = nc.scalar.activation

            def split_x():
                for k in range(KD):
                    arrived(act, "x_in", k)
                    A(big[:, 0, k, :], xin[:, k % 2, :], ACT.Copy).then_inc(S["x_hi"], 1)

            def evacuate(s):
                _, kind, u, c = s
                if kind in NO_HI:
                    return
                turn = PTURN[s]
                c0, w = CHUNKS[c]
                cc = slice(c0, c0 + w)
                src = PJ[turn % 2]
                if kind in ("ncq", "nckv"):
                    t0, nt, _ = lat[kind]
                    if c == 0:
                        act.wait_ge(S["proj_evac"], last_turn(*(("cq", QL_T - 1) if kind == "ncq" else ("ckv", KVL_T - 1))) + 1)
                        act.wait_ge(S["proj_evac"], last_turn("kpe", 0) + 1)
                    for j in range(nt):
                        k = square_at(kind, c, j)
                        if k >= 2:
                            name, value = square_used(k - 2)
                            act.wait_ge(S[name], value)
                        A(lsq[:, k % 2, 0:w], lraw[:, t0 + j, cc], ACT.Square).then_inc(S["lat_sq"], 1)
                act.wait_ge(S["proj_done"], turn + 1)
                if kind == "k0":
                    for m in range(2):
                        ins = A(kst[0:64, u % 2, m, cc], src[64 * m:64 * m + 64, 0:w], ACT.Copy)
                elif kind == "q0":
                    for m in range(2):
                        for z in range(2):
                            ins = A(qst[64 * z:64 * z + 64, m, 0, cc], src[64 * m:64 * m + 64, 0:w],
                                    ACT.Copy, scale=q_scale(u))
                elif kind == "g0":
                    if c == 0 and u >= 1:
                        act.wait_ge(S["unit_done"], u)
                    ins = A(gate[:, cc], src[:, 0:w], ACT.Sigmoid)
                elif kind == "g1":
                    if c == 0 and u >= 2:
                        arrived(act, "g_stored", u - 2)
                    ins = A(gtmp[:, u % 2, cc], src[:, 0:w], ACT.Sigmoid)
                elif kind == "rms0":
                    ins = A(sq[:, cc], src[:, 0:w], ACT.Sqrt, bias=eps[:, 0:1], scale=1.0 / 128)
                elif kind in ("ncq", "nckv"):
                    ins = A(src[:, 0:w], src[:, 0:w], ACT.Sqrt, bias=eps[:, 0:1], scale=1.0 / (128 * lat[kind][1]))
                elif kind in ("kpe", "qr"):
                    if turn >= 1:
                        act.wait_ge(S["proj_evac"], turn)
                    for z in range(4):
                        a = 32 * (z ^ 1)
                        ins = A(rtmp[32 * z:32 * z + 32, 0, 0:w], src[a:a + 32, 0:w], ACT.Copy)
                elif kind == "kn":
                    ins = A(kh[:, u % 2, 0, cc], src[:, 0:w], ACT.Copy)
                elif kind == "qn":
                    ins = A(qh[:, 0, cc], src[:, 0:w], ACT.Copy)
                ins.then_inc(S["proj_hi"], 1)

            def turned_v(s):
                _, layer, u = s
                for k in range(3):
                    if k == 0 and u >= 2:
                        g = unit_groups(layer, u - 2)[-1]
                        act.wait_ge(S["pv_done"], RING[g, len(turns_of(GROUPS[g][4])) - 1] + 1)
                    act.wait_ge(S["tr_done"], T_TURN[s, k] + 1)
                    for dst, _, src in v_parts(s, k, 0):
                        ins = A(dst, src, ACT.Copy)
                    ins.then_inc(S["tr_hi"], 1)

            def softmax_scores(t):
                g, i, slot = TSTEPS[t]
                layer, kind, u, head, _ = GROUPS[g]
                n = keys_of(i)
                rows = META if i == META_Q else 128
                st_ = lambda a, b: stat[0:rows, t % 4, a:b]
                if kind == "A":
                    for m in range(2):
                        act.wait_ge(S["max_ready"], STATS_DONE[t, m])
                        A(tb[0:rows, t % 2, m, 0:n], tb[0:rows, t % 2, m, 0:n], ACT.Exp, bias=st_(6 + m, 7 + m),
                          scale=SLOPES[u], accum_out=st_(8 + m, 9 + m)).then_inc(S["exp_done"], 1)
                    return
                if kind == "B":
                    if t >= 2:
                        act.wait_ge(S["p_ready"], t - 1)
                    for c, (c0, w) in enumerate(score_chunks(i)):
                        b = S_CHUNK[t, 0, c]
                        act.wait_ge(S["s_done"], b + 1)
                        src = SC[b % SBANKS][0:rows, 0:w]
                        A(tb[0:rows, t % 2, 0, c0:c0 + w], src, ACT.Sigmoid, scale=-SCALE64)
                        A(tb[0:rows, t % 2, 1, c0:c0 + w], src, ACT.Sigmoid, scale=SCALE64)\
                            .then_inc(S["s_free_act"], 1)
                    return
                if t == TSTEPS.index((unit_groups(1, 0)[0], 0, 0)):
                    all_arrived(act, "g_stored", HEADS)
                p_free(act, g)
                act.wait_ge(S["max_ready"], STATS_DONE[t, 0])
                for c, (c0, w) in enumerate(score_chunks(i)):
                    b = S_CHUNK[t, 0, c]
                    A(pb1[:, g % 2, slot, c0:c0 + w], SC[b % SBANKS][:, 0:w], ACT.Exp, bias=st_(6, 7),
                      scale=SCALE192, accum_out=st_(8 + c, 9 + c)).then_inc(S["s_free_act"], 1)

            def turned_weights(s):
                g = s[1]
                layer, kind, u, head, blocks = GROUPS[g]
                R = bufs(layer)["ring"]
                turns = turns_of(blocks)
                for k in range(len(turns)):
                    t, r = T_TURN[s, k], RING[g, k]
                    rows, w = turn_extent(g, k)
                    if r >= NRING:
                        act.wait_ge(S["pv_done"], r - NRING + 1)
                    act.wait_ge(S["tr_done"], t + 1)
                    A(R[0:rows, r % NRING, 0, 0:w], TR[t % 2][0:rows, 0:w], ACT.Copy).then_inc(S["tr_hi"], 1)
                if kind == "B":
                    w = META if blocks == [META_Q] else 256
                    act.wait_ge(S["pv_done"], RING[g, len(turns) - 1] + 1)
                    if g >= 1:
                        act.wait_ge(S["o_evac"], g)
                    A(otmp[:, 0:w], PO[64:128, 0:w], ACT.Copy).then_inc(S["o_tmp"], 1)

            def norm_block(s):
                _, layer, b = s
                n = O_AT[s]
                rows = META if b == META_Q else 128
                o = 32 * (n % 2)
                rs = res1 if layer else res
                act.wait_ge(S["ln_stats"], n + 1)
                A(small[0:rows, o + 14:o + 15], small[0:rows, o + 13:o + 14], ACT.Sqrt, bias=eps[0:rows, 1:2])\
                    .then_inc(S["ln_mid"], 1)
                act.wait_ge(S["ln_rstd"], n + 1)
                A(rs[0:rows, n % 2, :], rs[0:rows, n % 2, :], ACT.Identity, scale=small[0:rows, o + 15:o + 16],
                  bias=small[0:rows, o + 16:o + 17]).then_inc(S["ln_norm"], 1)

            def store_block(s):
                _, layer, b = s
                if b == META_Q:
                    return
                n = O_AT[s]
                act.wait_ge(S["h_ready"], n + 1)
                dst = out if layer else hd
                act.dma_start(dst[128 * b:128 * b + 128, :], (res1 if layer else res)[:, n % 2, :])\
                    .then_inc(slot("h_stored", NB * layer + b), 16)

            def turned_h(s):
                b = s[2]
                c0, w = query_cols(b)
                for k in range(2):
                    t = T_TURN[s, k]
                    act.wait_ge(S["tr_done"], t + 1)
                    A(h1t[:, 0, 4 * k:4 * k + 4, c0:c0 + w],
                      TR[t % 2][:, :].rearrange("p (j c) -> p j c", j=4)[:, :, 0:w], ACT.Copy).then_inc(S["tr_hi"], 1)

            act.wait_ge(S["const_pool"], 4)
            split_x()
            act.wait_ge(S["lam_exp"], 1)
            A(small[:, 60:62], small[:, 62:64], ACT.Exp).then_inc(S["act_step"], 1)
            last = None
            for s in PLAN:
                if s[0] == "P":
                    evacuate(s)
                elif s[0] == "VT":
                    turned_v(s)
                elif s[0] == "S":
                    softmax_scores(s[1])
                elif s[0] == "V":
                    turned_weights(s)
                elif s[0] == "SQ":
                    act.wait_ge(S["o_evac"], unit_groups(0, s[1])[-1] + 1)
                    if s[1] >= 1:
                        act.wait_ge(S["proj_evac"], last_turn("rms0", s[1] - 1) + 1)
                    A(sq[:, :], ot[:, :], ACT.Square).then_inc(S["sq_done"], 1)
                elif s[0] == "O":
                    norm_block(s)
                    if last is not None:
                        store_block(last)
                        if s[1] == 0:
                            turned_h(last)
                    last = s
                elif s[0] == "OT":
                    store_block(last)
                    turned_h(last)
                    last = None
            store_block(last)

        @block.vector
        def _(dve):
            V = nc.vector
            step = [0]

            def then(ins):
                step[0] += 1
                ins.then_inc(S["dve_step"], 1)
                dve.wait_ge(S["dve_step"], step[0])

            def constants():
                dve.wait_ge(S["consts"], 16 * N_CONSTS)
                for j in range(2):
                    then(V.tensor_tensor_reduce(out=lamv[:, 2 * j, :], in0=lamv[:, 2 * j, :], in1=lamv[:, 2 * j + 1, :],
                                                scale=1.0, scalar=0.0, op0=ALU.mult, op1=ALU.add,
                                                accum_out=small[:, 62 + j:63 + j]))
                then(V.tensor_scalar(rmsg[:, 0:1], rmsg[:, 0:1], 1.0 - LAM_INIT, None, ALU.mult))
                V.tensor_scalar(rmsg[:, 7:8], rmsg[:, 0:1], 0.0, None, ALU.mult).then_inc(S["lam_exp"], 1)

            def negative_lambda():
                dve.wait_ge(S["act_step"], 1)
                then(V.tensor_tensor(small[:, 58:59], small[:, 61:62], small[:, 60:61], ALU.subtract))
                then(V.tensor_scalar(small[:, 59:60], small[:, 58:59], -LAM_INIT, None, ALU.add))

            def split_x():
                for k in range(KD):
                    dve.wait_ge(S["x_hi"], k + 1)
                    V.tensor_tensor(big[:, 1, k, :], xin[:, k % 2, :], lo_hi(big[:, 0, k, :]), ALU.subtract)\
                        .then_inc(S["x_split"], 1)

            def rotate(turn, cc, w):
                src = PJ[turn % 2][:, 0:w]
                dve.wait_ge(S["rope_in"], 16)
                V.tensor_tensor(rtmp[:, 1, 0:w], src, ropet[:, 0, cc], ALU.mult)
                then(V.tensor_tensor(rtmp[:, 0, 0:w], rtmp[:, 0, 0:w], ropet[:, 1, cc], ALU.mult))
                then(V.tensor_tensor(rtmp[:, 1, 0:w], rtmp[:, 0, 0:w], rtmp[:, 1, 0:w], ALU.add))

            def evacuate(s):
                _, kind, u, c = s
                turn = PTURN[s]
                c0, w = CHUNKS[c]
                cc = slice(c0, c0 + w)
                src = PJ[turn % 2]
                if kind in NO_HI:
                    dve.wait_ge(S["proj_done"], turn + 1)
                else:
                    dve.wait_ge(S["proj_hi"], HI_COUNT[s])
                if kind == "k0":
                    for m in range(2):
                        ins = V.tensor_tensor(kst[64:128, u % 2, m, cc], src[64 * m:64 * m + 64, 0:w],
                                              lo_hi(kst[0:64, u % 2, m, cc]), ALU.subtract)
                elif kind == "q0":
                    for m in range(2):
                        for z in range(2):
                            ins = V.scalar_tensor_tensor(
                                out=qst[64 * z:64 * z + 64, m, 1, cc], in0=src[64 * m:64 * m + 64, 0:w],
                                scalar=q_scale(u), in1=lo_hi(qst[0:64, m, 0, cc]), op0=ALU.mult, op1=ALU.subtract)
                elif kind in ("v0", "vn"):
                    ins = V.tensor_copy((vt1 if kind == "vn" else vt)[:, cc], src[:, 0:w])
                elif kind == "g0":
                    ins = V.tensor_tensor(gate[:, cc], src[:, 0:w], gate[:, cc], ALU.mult)
                elif kind == "g1":
                    ins = V.tensor_tensor(gtmp[:, u % 2, cc], src[:, 0:w], gtmp[:, u % 2, cc], ALU.mult)
                elif kind == "rms0":
                    then(V.reciprocal(sq[:, cc], sq[:, cc]))
                    ins = V.scalar_tensor_tensor(out=ot[:, cc], in0=ot[:, cc], scalar=rmsg[:, 0:1], in1=sq[:, cc],
                                                 op0=ALU.mult, op1=ALU.mult)
                elif kind in ("cq", "ckv"):
                    if (kind, u, c) == ("cq", 0, 0):
                        all_arrived(dve, "h_stored", NB)
                    ins = V.tensor_copy(lraw[:, u + (QL_T if kind == "ckv" else 0), cc], src[:, 0:w])
                elif kind in ("ncq", "nckv"):
                    t0, nt, gain = lat[kind]
                    then(V.reciprocal(src[:, 0:w], src[:, 0:w]))
                    for j in range(t0, t0 + nt):
                        last = V.scalar_tensor_tensor(out=lraw[:, j, cc], in0=lraw[:, j, cc],
                                                      scalar=rmsg[:, 1 + j:2 + j], in1=src[:, 0:w],
                                                      op0=ALU.mult, op1=ALU.mult)
                    then(last)
                    for j in range(t0, t0 + nt):
                        last = V.tensor_copy(big[:, 0, j, cc], lraw[:, j, cc])
                    then(last)
                    for j in range(t0, t0 + nt):
                        ins = V.tensor_tensor(big[:, 1, j, cc], lraw[:, j, cc], lo_hi(big[:, 0, j, cc]), ALU.subtract)
                elif kind == "kpe":
                    rotate(turn, cc, w)
                    then(V.tensor_copy(kpe[:, cc], rtmp[:, 1, 0:w]))
                    ins = V.tensor_tensor(kpe[64:128, cc], rtmp[64:128, 1, 0:w], lo_hi(kpe[64:128, cc]), ALU.subtract)
                elif kind == "qr":
                    rotate(turn, cc, w)
                    for h in range(2):
                        for z in range(2):
                            last = V.tensor_copy(qpe[64 * z:64 * z + 64, h, 0, cc], rtmp[64 * h:64 * h + 64, 1, 0:w])
                    then(last)
                    for h in range(2):
                        for z in range(2):
                            ins = V.tensor_tensor(qpe[64 * z:64 * z + 64, h, 1, cc], rtmp[64 * h:64 * h + 64, 1, 0:w],
                                                  lo_hi(qpe[64 * h:64 * h + 64, h, 0, cc]), ALU.subtract)
                elif kind == "kn":
                    ins = V.tensor_tensor(kh[:, u % 2, 1, cc], src[:, 0:w], lo_hi(kh[:, u % 2, 0, cc]), ALU.subtract)
                elif kind == "qn":
                    ins = V.tensor_tensor(qh[:, 1, cc], src[:, 0:w], lo_hi(qh[:, 0, cc]), ALU.subtract)
                ins.then_inc(S["proj_evac"], 1)

            def turned_v(s):
                for k in range(3):
                    dve.wait_ge(S["tr_hi"], T_TURN[s, k] + 1)
                    for dst, hi, src in v_parts(s, k, 1):
                        ins = V.tensor_tensor(dst, src, lo_hi(hi), ALU.subtract)
                    ins.then_inc(S["tr_lo"], 1)

            def scores(t):
                g, i, slot = TSTEPS[t]
                layer, kind, u, head, _ = GROUPS[g]
                if kind == "B":
                    return
                rows = META if i == META_Q else 128
                st_ = lambda a, b: stat[0:rows, t % 4, a:b]
                chunks = score_chunks(i)
                d0 = 128 * (NB - 1 - i) if i != META_Q else 128 * (NB - 1) + META
                if kind == "A" and t >= 2:
                    dve.wait_ge(S["p_ready"], t - 1)
                for m in range(2 if kind == "A" else 1):
                    for c, (c0, w) in enumerate(chunks):
                        b = S_CHUNK[t, m, c]
                        dve.wait_ge(S["s_done"], b + 1)
                        src = SC[b % SBANKS][0:rows, 0:w]
                        mx = st_(3 * m + c, 3 * m + c + 1)
                        if kind == "A":
                            ins = V.tensor_tensor_reduce(out=tb[0:rows, t % 2, m, c0:c0 + w], in0=src,
                                                         in1=distt[0:rows, d0 + c0:d0 + c0 + w], scale=1.0, scalar=-3.0e38,
                                                         op0=ALU.add, op1=ALU.max, accum_out=mx)
                            ins.then_inc(S["s_free_dve"], 1)
                            last_freed = S_FREED[b]
                        else:
                            ins = V.reduce_max(mx, src, AX_X)
                            if c == len(chunks) - 1:
                                then(ins)
                    if kind == "A":
                        dve.wait_ge(S["s_free_dve"], last_freed)
                    nm = st_(6 + m, 7 + m)
                    scale = -(SLOPES[u] if kind == "A" else SCALE192)
                    if len(chunks) > 1:
                        then(V.reduce_max(nm, st_(3 * m, 3 * m + len(chunks)), AX_X))
                        V.tensor_scalar(nm, nm, scale, None, ALU.mult).then_inc(S["max_ready"], 1)
                    else:
                        V.tensor_scalar(nm, st_(3 * m, 3 * m + 1), scale, None, ALU.mult).then_inc(S["max_ready"], 1)

            def weights(t):
                g, i, slot = TSTEPS[t]
                layer, kind, u, head, _ = GROUPS[g]
                n = keys_of(i)
                rows = META if i == META_Q else 128
                st_ = lambda a, b: stat[0:rows, t % 4, a:b]
                P = bufs(layer)["pb"][0:rows, g % 2, slot, :]
                chunks = score_chunks(i)
                if kind != "C":
                    p_free(dve, g)
                if kind == "A":
                    dve.wait_ge(S["exp_done"], MAPS_DONE[t, 1])
                    then(V.reciprocal(st_(12, 14), st_(8, 10)))
                    V.tensor_scalar(P[:, 0:n], tb[0:rows, t % 2, 0, 0:n], st_(12, 13), None, ALU.mult)
                    then(V.tensor_scalar(st_(14, 15), st_(13, 14), small[0:rows, 59:60], None, ALU.mult))
                    V.scalar_tensor_tensor(out=P[:, 0:n], in0=tb[0:rows, t % 2, 1, 0:n], scalar=st_(14, 15), in1=P[:, 0:n],
                                           op0=ALU.mult, op1=ALU.add).then_inc(S["p_ready"], 1)
                elif kind == "B":
                    dve.wait_ge(S["s_free_act"], S_FREED[S_CHUNK[t, 0, len(chunks) - 1]])
                    skip = tb[0:rows, t % 2, 0, :]
                    V.memset(P[:, n - 1:n], 1.0)
                    then(V.tensor_tensor_scan(P[:, 0:n - 1][:, ::-1], skip[:, 1:n][:, ::-1], skip[:, 1:n][:, ::-1], 1.0,
                                              ALU.mult, ALU.bypass))
                    V.tensor_tensor(P[:, 0:n], P[:, 0:n], tb[0:rows, t % 2, 1, 0:n], ALU.mult).then_inc(S["p_ready"], 1)
                else:
                    dve.wait_ge(S["s_free_act"], S_FREED[S_CHUNK[t, 0, len(chunks) - 1]])
                    if len(chunks) > 1:
                        then(V.reduce_sum(st_(12, 13), st_(8, 8 + len(chunks)), AX_X))
                        then(V.reciprocal(st_(13, 14), st_(12, 13)))
                    else:
                        then(V.reciprocal(st_(13, 14), st_(8, 9)))
                    V.tensor_scalar(P[:, 0:n], P[:, 0:n], st_(13, 14), None, ALU.mult).then_inc(S["p_ready"], 1)

            def turned_weights(s):
                g = s[1]
                layer, kind, u, head, blocks = GROUPS[g]
                B = bufs(layer)
                turns = turns_of(blocks)
                for k in range(len(turns)):
                    t, r = T_TURN[s, k], RING[g, k]
                    rows, w = turn_extent(g, k)
                    dve.wait_ge(S["tr_hi"], t + 1)
                    R = B["ring"]
                    V.tensor_tensor(R[0:rows, r % NRING, 1, 0:w], TR[t % 2][0:rows, 0:w],
                                    lo_hi(R[0:rows, r % NRING, 0, 0:w]), ALU.subtract).then_inc(S["tr_lo"], 1)
                if blocks == [META_Q]:
                    c0, w = 0, META
                else:
                    c0, w = META + 128 * blocks[0], 256
                first = g == unit_groups(layer, u)[0]
                done = F_AT[("F", layer, u)]
                if first and done > 0:
                    dve.wait_ge(S["y_stored"], 16 * done)
                if kind == "B":
                    dve.wait_ge(S["o_tmp"], B_GROUPS.index(g) + 1)
                    V.tensor_tensor(B["ot"][64 * head:64 * head + 64, c0:c0 + w], PO[0:64, 0:w], otmp[:, 0:w], ALU.add)\
                        .then_inc(S["o_evac"], 1)
                else:
                    dve.wait_ge(S["pv_done"], RING[g, len(turns) - 1] + 1)
                    V.tensor_copy(B["ot"][:, c0:c0 + w], PO[:, 0:w]).then_inc(S["o_evac"], 1)

            def gated(s):
                _, layer, u = s
                B = bufs(layer)
                a = META if layer else 0
                if layer:
                    dve.wait_ge(S["g_loaded"], 16 * (u + 1))
                elif u < A_UNITS:
                    dve.wait_ge(S["proj_evac"], last_turn("rms0", u) + 1)
                dve.wait_ge(S["o_evac"], unit_groups(layer, u)[-1] + 1)
                V.tensor_tensor(B["ot"][:, a:TOK], B["ot"][:, a:TOK], B["gate"][:, a:TOK], ALU.mult)\
                    .then_inc(S["unit_done"], 1)

            def norm_block(s):
                _, layer, b = s
                n = O_AT[s]
                rows = META if b == META_Q else 128
                o = 32 * (n % 2)
                rs, xr, lg = (res1, xres1, lngb1) if layer else (res, xres, lngb)
                base = (NB + 1) * layer
                arrived(dve, "res_in", n)
                dve.wait_ge(S["y_done"], n + 1)
                if n - base >= 2:
                    arrived(dve, "h_stored", NB * layer + b - 2)
                    if layer == 0:
                        dve.wait_ge(S["tr_done"], T_TURN[("O", 0, b - 2), 1] + 1)
                for half in range(2):
                    hs = slice(512 * half, 512 * half + 512)
                    ins = V.scalar_tensor_tensor(out=rs[0:rows, n % 2, hs], in0=xr[0:rows, n % 2, hs], scalar=ALPHA,
                                                 in1=bank[2 * (n % 2) + half][0:rows, :], op0=ALU.mult, op1=ALU.add)
                ins.then_inc(S["y_evac"], 1)
                dve.wait_ge(S["y_evac"], n + 1)
                for half in range(2):
                    ins = V.bn_stats(small[0:rows, o + 6 * half:o + 6 * half + 6], rs[0:rows, n % 2, 512 * half:512 * half + 512])
                then(ins)
                V.bn_aggr(small[0:rows, o + 12:o + 14], small[0:rows, o:o + 12]).then_inc(S["ln_stats"], 1)
                dve.wait_ge(S["ln_mid"], n + 1)
                then(V.reciprocal(small[0:rows, o + 15:o + 16], small[0:rows, o + 14:o + 15]))
                V.scalar_tensor_tensor(out=small[0:rows, o + 16:o + 17], in0=small[0:rows, o + 12:o + 13], scalar=-1.0,
                                       in1=small[0:rows, o + 15:o + 16], op0=ALU.mult, op1=ALU.mult).then_inc(S["ln_rstd"], 1)
                dve.wait_ge(S["ln_norm"], n + 1)
                dve.wait_ge(S["lnp_in"], 32 * (layer + 1))
                V.tensor_tensor(rs[0:rows, n % 2, :], rs[0:rows, n % 2, :], lg[0:rows, 0, :], ALU.mult)\
                    .then_inc(S["ln_scaled"], 1)

            def turned_h(s):
                b = s[2]
                c0, w = query_cols(b)
                for k in range(2):
                    t = T_TURN[s, k]
                    dve.wait_ge(S["tr_hi"], t + 1)
                    V.tensor_tensor(h1t[:, 1, 4 * k:4 * k + 4, c0:c0 + w],
                                    TR[t % 2][:, :].rearrange("p (j c) -> p j c", j=4)[:, :, 0:w],
                                    lo_hi(h1t[:, 0, 4 * k:4 * k + 4, c0:c0 + w]), ALU.subtract).then_inc(S["tr_lo"], 1)

            constants()
            split_x()
            negative_lambda()
            last = None
            for s in PLAN:
                if s[0] == "P":
                    evacuate(s)
                elif s[0] == "VT":
                    turned_v(s)
                elif s[0] == "S":
                    scores(s[1])
                elif s[0] == "C":
                    weights(s[1])
                elif s[0] == "V":
                    turned_weights(s)
                elif s[0] == "F":
                    gated(s)
                elif s[0] == "O":
                    norm_block(s)
                    if s[1] == 0 and last is not None:
                        turned_h(last)
                    last = s
                elif s[0] == "OT":
                    turned_h(last)
                    last = None

        @block.tensor
        def _(pe):
            mm = nc.tensor.matmul

            def project(s):
                _, kind, u, c = s
                n, turn = TILE_AT[kind, u], PTURN[s]
                kt = KT_OF[kind]
                c0, w = CHUNKS[c]
                rhs, k0 = rhs_of(kind)
                if c == 0:
                    pe.wait_ge(S["w_ready"], WEIGHT_AT[kind, u] + 1)
                if turn == 0:
                    pe.wait_ge(S["x_split"], KD)
                if kind == "cq" and u == 0 and c == 0:
                    pe.wait_ge(S["tr_lo"], T_TURN[("O", 0, NB), 1] + 1)
                if turn >= 2:
                    pe.wait_ge(S["proj_evac"], turn - 1)
                if (kind, u, c) in (("kn", 0, 0), ("qr", 0, 0)):
                    pe.wait_ge(S["proj_evac"], last_turn("nckv" if kind == "kn" else "ncq", 0) + 1)
                dst = PJ[turn % 2][:, 0:w]
                first = True
                for k in range(kt):
                    for a, b in ((0, 0), (0, 1), (1, 0)):
                        ins = mm(dst, wsp[:, n % 2, a, k, :], rhs[:, b, k0 + k, c0:c0 + w], start=first,
                                 stop=(k == kt - 1 and a == 1))
                        first = False
                ins.then_inc(S["proj_done"], 1)

            def norm_sum(s):
                _, kind, u, c = s
                turn = PTURN[s]
                c0, w = CHUNKS[c]
                if turn >= 2:
                    pe.wait_ge(S["proj_evac"], turn - 1)
                dst = PJ[turn % 2][:, 0:w]
                if kind == "rms0":
                    pe.wait_ge(S["sq_done"], u + 1)
                    ins = mm(dst, ones[:, :], sq[:, c0:c0 + w], start=True, stop=True)
                else:
                    _, nt, _ = lat[kind]
                    for j in range(nt):
                        k = square_at(kind, c, j)
                        pe.wait_ge(S["lat_sq"], k + 1)
                        ins = mm(dst, ones[:, :], lsq[:, k % 2, 0:w], start=(j == 0), stop=(j == nt - 1))
                        if j < nt - 1:
                            ins.then_inc(S["lsq_used"], 1)
                ins.then_inc(S["proj_done"], 1)

            def turn_v(s):
                _, layer, u = s
                pe.wait_ge(S["proj_evac"], last_turn("vn" if layer else "v0", u) + 1)
                v = bufs(layer)["vt"]
                for k, tiles in enumerate(V_TILES):
                    t = T_TURN[s, k]
                    if t >= 2:
                        pe.wait_ge(S["tr_lo"], t - 1)
                    for j, tile in enumerate(tiles):
                        c0, _ = (0, META) if tile == 0 else (META + 128 * (tile - 1), 128)
                        ins = nc.tensor.transpose(TR[t % 2][:, 128 * j:128 * j + 128], v[:, c0:c0 + 128], eye[:, :])
                    ins.then_inc(S["tr_done"], 1)

            def scores(t):
                g, i, slot = TSTEPS[t]
                layer, kind, u, head, _ = GROUPS[g]
                q0, rows = query_cols(i)
                n = keys_of(i)
                chunks = score_chunks(i)
                if slot == 0 and g == unit_groups(layer, u)[0]:
                    pe.wait_ge(S["proj_evac"], last_turn("qn" if layer else "q0", u) + 1)
                for m in range(2 if kind == "A" else 1):
                    for c, (c0, w) in enumerate(chunks):
                        b = S_CHUNK[t, m, c]
                        if b >= SBANKS:
                            pe.wait_ge(S["s_free_" + S_OWNER[b - SBANKS]], S_FREED[b - SBANKS])
                        dst = SC[b % SBANKS][:, 0:w]
                        qc = slice(q0, q0 + 128)
                        last = c == len(chunks) - 1 and not (i == META_Q and kind == "A")
                        if kind == "C":
                            prods = [(qh[:, a, qc], kh[:, u % 2, b_, c0:c0 + w]) for a, b_ in ((0, 0), (0, 1), (1, 0))]
                            prods += [(qpe[:, u % 2, a, qc], kpe[:, c0:c0 + w]) for a in (0, 1)]
                        else:
                            j = m if kind == "A" else head
                            prods = [(qst[:, j, a, qc], kst[:, u % 2, j, c0:c0 + w]) for a in (0, 1)]
                        for k, (l, r) in enumerate(prods):
                            ins = mm(dst, l, r, start=(k == 0), stop=(k == len(prods) - 1 and not last))
                        if last:
                            d = w - 128 if i != META_Q else 0
                            dw = 128 if i != META_Q else META
                            ins = mm(SC[b % SBANKS][:, d:d + dw], eyebf[:, :],
                                     mask[:, 1 if kind == "B" else 0, 0:dw], start=False, stop=True)
                        ins.then_inc(S["s_done"], 1)

            def values(s):
                g = s[1]
                layer, kind, u, head, blocks = GROUPS[g]
                B = bufs(layer)
                turns = turns_of(blocks)
                w_all = META if blocks == [META_Q] else 256

                def turn(k):
                    t = T_TURN[s, k]
                    if k == 0:
                        pe.wait_ge(S["p_ready"], GROUP_STEPS[g][-1] + 1)
                    if t >= 2:
                        pe.wait_ge(S["tr_lo"], t - 1)
                    dst = TR[t % 2]
                    at = 0
                    for tile in turns[k]:
                        for slot, i in enumerate(blocks):
                            if i != META_Q and tile > i + 1:
                                continue
                            if tile == 0:
                                rows = META if i == META_Q else 128
                                wd = META if i == META_Q else 128
                                ins = nc.tensor.transpose(dst[0:META, at:at + wd], B["pb"][0:rows, g % 2, slot, 0:META],
                                                          eye[0:rows, 0:rows])
                                at += wd
                            else:
                                k0 = META + 128 * (tile - 1)
                                ins = nc.tensor.transpose(dst[:, at:at + 128], B["pb"][:, g % 2, slot, k0:k0 + 128], eye[:, :])
                                at += 128
                    ins.then_inc(S["tr_done"], 1)

                def product(k):
                    t, r = T_TURN[s, k], RING[g, k]
                    pe.wait_ge(S["tr_lo"], t + 1)
                    if k == 0 and g >= 1:
                        pe.wait_ge(S["o_evac"], g)
                    at = 0
                    for tile in turns[k]:
                        wide = w_all if (tile == 0 or tile <= blocks[0] + 1) else 128
                        o0 = w_all - wide
                        rows = META if tile == 0 else 128
                        vv = B["vtok"]
                        if kind == "B":
                            prods = [(vv[0:rows, u % 2, head, tile, :], 0), (vv[0:rows, u % 2, head, tile, :], 1)]
                        else:
                            prods = [(vv[0:rows, u % 2, a, tile, :], b_) for a, b_ in ((0, 0), (1, 0), (0, 1))]
                        final = k == len(turns) - 1 and tile == turns[k][-1]
                        for j, (l, h) in enumerate(prods):
                            ins = mm(PO[:, o0:o0 + wide], l, B["ring"][0:rows, r % NRING, h, at:at + wide],
                                     start=(k == 0 and tile == turns[0][0] and j == 0),
                                     stop=(final and j == len(prods) - 1))
                        at += wide
                    ins.then_inc(S["pv_done"], 1)

                turn(0)
                for k in range(1, len(turns)):
                    turn(k)
                    product(k - 1)
                product(len(turns) - 1)

            def out_block(s):
                _, layer, b = s
                n = O_AT[s]
                ys = ysp1 if layer else ysp
                pe.wait_ge(S["y_split"], n + 1)
                if b == 0:
                    pe.wait_ge(S["w_ready"], WEIGHT_AT[("wo1" if layer else "wo0"), KD - 1] + 1)
                if n >= 2:
                    pe.wait_ge(S["y_evac"], n - 1)
                for half in range(2):
                    dst = bank[2 * (n % 2) + half]
                    for k in range(KD):
                        for a, c in ((0, 0), (0, 1), (1, 0)):
                            ins = mm(dst[:, :], ys[:, n % 2, a, k, :], wok[:, c, k, 512 * half:512 * half + 512],
                                     start=(k == 0 and a == 0 and c == 0), stop=(k == KD - 1 and a == 1))
                ins.then_inc(S["y_done"], 1)

            def turn_h(s):
                _, layer, b = s
                n = O_AT[s]
                rows = META if b == META_Q else 128
                pe.wait_ge(S["h_ready"], n + 1)
                for k in range(2):
                    t = T_TURN[s, k]
                    pe.wait_ge(S["tr_lo"], t - 1)
                    for j in range(4):
                        ins = nc.tensor.transpose(TR[t % 2][:, 128 * j:128 * j + rows],
                                                  res[0:rows, n % 2, 128 * (4 * k + j):128 * (4 * k + j) + 128],
                                                  eye[0:rows, 0:rows])
                    ins.then_inc(S["tr_done"], 1)

            pe.wait_ge(S["const_pool"], 4)
            pe.wait_ge(S["consts"], 16 * N_CONSTS)
            waiting = []
            for s in PLAN:
                if s[0] == "P":
                    (norm_sum if s[1] in NORMS else project)(s)
                elif s[0] == "VT":
                    turn_v(s)
                elif s[0] == "S":
                    scores(s[1])
                elif s[0] == "V":
                    values(s)
                elif s[0] == "O":
                    out_block(s)
                    if s[1] == 0:
                        if waiting:
                            turn_h(waiting.pop())
                        waiting.append(s)
                elif s[0] == "OT":
                    turn_h(waiting.pop())


def kernel(**inputs):
    import ml_dtypes
    import concourse.bacc as _bacc
    from concourse.bass_utils import run_bass_kernel_spmd as _run

    a = {k: np.asarray(v) for k, v in inputs.items()}

    def tiles(w):
        k = w.shape[0] // 128
        return w.reshape(k, 128, w.shape[1]).transpose(1, 0, 2).reshape(128, -1)

    h = np.concatenate([a["meta"], a["x"][0]], 0)
    ht = h.T.reshape(KD, 128, TOK).transpose(1, 0, 2)
    w_in = a["ev_w_in"][0]
    part = {"A": [0, 512, 1024, 1536], "B": [2048, 2560, 3072, 3584]}
    w0 = np.stack([np.stack([tiles(w_in[:, o + 128 * (u % 4):o + 128 * (u % 4) + 128])
                             for o in part["A" if u < A_UNITS else "B"]]) for u in range(UNITS)])
    w_od = a["od_w_in"][0]
    starts = [128 * j for j in range(QL_T + KVL_T)]
    w1 = [tiles(w_od[:, o:o + 128]) for o in starts]
    pe_cols = w_od[:, 768:832]
    w1.append(tiles(np.concatenate([pe_cols, pe_cols], 1)))
    w1 += [tiles(w_od[:, 832 + 128 * h_:960 + 128 * h_]) for h_ in range(HEADS)]
    w1 = np.stack(w1)
    wuq = a["od_w_uq"][0]
    wuq_n = np.stack([tiles(wuq[:, 192 * h_:192 * h_ + 128]) for h_ in range(HEADS)])
    wuq_r = np.stack([tiles(np.concatenate([wuq[:, 192 * h_ + 128:192 * h_ + 192] for h_ in (2 * j, 2 * j + 1)], 1))
                      for j in range(HEADS // 2)])
    wkv = a["od_w_ukv"][0]
    wukv = np.stack([np.stack([tiles(wkv[:, 256 * h_ + 128 * z:256 * h_ + 128 * z + 128]) for z in range(2)])
                     for h_ in range(HEADS)])
    wo0 = a["ev_w_out"][0].reshape(KD, 128, D).transpose(1, 0, 2)
    wo1 = a["od_w_out"][0].reshape(KD, 128, D).transpose(1, 0, 2)
    lam = np.stack([a["ev_lam_q1"][0], a["ev_lam_k1"][0], a["ev_lam_q2"][0], a["ev_lam_k2"][0]])[None]
    r, c = np.arange(128)[:, None], np.arange(TOK)[None, :]
    dist = -np.abs(128 * (NB - 1) + META + r - c).astype(np.float16)
    k = np.arange(128)[None, :]
    masks = np.stack([np.where((k // CHUNK) > (r // CHUNK), MASKED, 0.0), np.where(k >= r, MASKED, 0.0)], 1)\
        .astype(ml_dtypes.bfloat16)
    eyeb = np.eye(128).astype(ml_dtypes.bfloat16)
    inv = (np.float32(10000.0) ** (-np.arange(32, dtype=np.float32) / np.float32(32))).astype(np.float32)
    ang = np.arange(TOK, dtype=np.float32)[None, :] * inv[:, None]
    cos, sin = np.cos(ang), np.sin(ang)
    rope = np.stack([np.tile(cos, (4, 1)), np.tile(np.concatenate([-sin, sin], 0), (2, 1))], 1).astype(np.float32)
    arrays = dict(ht=ht, x=a["x"][0], meta=a["meta"], w0=w0, w1=w1, wuq_n=wuq_n, wuq_r=wuq_r, wukv=wukv,
                  wo0=wo0, wo1=wo1, lng=a["ln_g"], lnb=a["ln_b"], lam=lam, subln=a["ev_subln"].reshape(128, 1),
                  qnorm=a["od_q_norm"][0].reshape(QL_T, 128).T, kvnorm=a["od_kv_norm"][0].reshape(KVL_T, 128).T,
                  dist=dist, masks=masks, eyeb=eyeb, rope=rope)
    nc = _bacc.Bacc("TRN2", target_bir_lowering=False, num_devices=1)
    feed, args = {}, {}
    for name, v in arrays.items():
        v = np.ascontiguousarray(v)
        feed["in_" + name] = v
        args[name] = nc.dram_tensor("in_" + name, v.shape, mybir.dt.from_np(v.dtype), kind="ExternalInput").ap()
    args["out"] = nc.dram_tensor("out_0", (SEQ, D), F32, kind="ExternalOutput").ap()
    args["lam"] = args["lam"].to_broadcast([128, 4, DH])
    trunk_kernel(nc, **args)
    r_ = _run(nc, [feed], core_ids=[0])
    return r_.results[0]["out_0"].reshape(1, SEQ, D)
```

```python
import concourse.bass as bass
from concourse import mybir
from contextlib import ExitStack
import math
import numpy as np

F32 = mybir.dt.float32
F32R = mybir.dt.float32r
BF16 = mybir.dt.bfloat16
F16 = mybir.dt.float16
ALU = mybir.AluOpType
ACT = mybir.ActivationFunctionType
AX_X = mybir.AxisListType.X

META, SEQ, D = 16, 1024, 1024
TOK = META + SEQ
KD = D // 128
CHUNK = 64
CHUNKS = [(0, 352), (352, 344), (696, 344)]
X_PIECES = [(k0, c0, w) for c0, w in CHUNKS for k0 in (0, KD // 2)]
NB = SEQ // 128
A_UNITS, B_UNITS, HEADS = 4, 4, 8
UNITS = A_UNITS + B_UNITS
DH = 64
SCALE64 = DH ** -0.5
SLOPES = [2.0 ** (-8.0 * (h + 1) / A_UNITS) for h in range(A_UNITS)]
SCALE192 = 192 ** -0.5
LAM_INIT = 0.8 - 0.6 * math.exp(0.0)
ALPHA = 4.0 ** 0.25
LN_EPS, RMS_EPS = 1e-5, 1e-6
QL_T, KVL_T = 4, 2
MASKED = -1.0e30
NRING = 3
SBANKS = 3
META_Q = NB


def keys_of(i):
    return META if i == META_Q else META + 128 * (i + 1)


def score_chunks(i):
    n = keys_of(i)
    if n <= 512:
        return [(0, n)]
    if n <= 1024:
        return [(0, n // 2), (n // 2, n // 2)]
    return list(CHUNKS)


def query_cols(i):
    return (0, META) if i == META_Q else (META + 128 * i, 128)


def turns_of(blocks):
    if blocks == [META_Q]:
        return [[0]]
    top = blocks[-1] + 1
    return [[0]] + [[a, a + 1] for a in range(1, top, 2)]


def maps_of(kind):
    return 2 if kind == "A" else 1


def merged(*streams):
    placed = []
    for n, (steps, begin, end) in enumerate(streams):
        for k, step in enumerate(steps):
            placed.append((begin + (end - begin) * (k + 0.5) / len(steps), n, k, step))
    return [p[3] for p in sorted(placed, key=lambda p: p[:3])]


def make_plan():
    plan = []
    groups = []
    tsteps = []

    def group_list(layer, u):
        x = [[2 * j, 2 * j + 1] for j in range(NB // 2)]
        if layer == 1:
            return [(1, "C", u, 0, b) for b in x]
        if u < A_UNITS:
            return [(0, "A", u, 0, b) for b in [[META_Q]] + x]
        return [(0, "B", u, m, b) for m in range(2) for b in [[META_Q]] + x]

    def proj(kind, u):
        return [("P", kind, u, c) for c in range(len(CHUNKS))]

    def score_steps(gid):
        out, late = [], []
        for slot, i in enumerate(groups[gid][4]):
            t = len(tsteps)
            tsteps.append((gid, i, slot))
            for m in range(maps_of(groups[gid][1])):
                out += [("S", t, m, c) for c in range(len(score_chunks(i)))] + [("E", t, m)]
            out += late
            late = [("C", t)]
        return out, late

    def value_steps(gid):
        n = len(turns_of(groups[gid][4]))
        out = [("T", gid, 0)]
        for k in range(1, n):
            out += [("T", gid, k), ("X", gid, k - 1)]
        return out + [("X", gid, n - 1), ("Y", gid)]

    def final_steps(layer, u):
        return [("SQ", u)] + proj("rms0", u) + [("F", u)] if layer == 0 and u < A_UNITS else []

    def run_layer(layer, fills, q_next):
        before = None
        for u in range(UNITS):
            gl = group_list(layer, u)
            early, second, fill = fills(u)
            total = sum(keys_of(i) for g in gl for i in g[4])
            done = placed = 0
            for gi, g in enumerate(gl):
                gid = len(groups)
                groups.append(g)
                s_steps, s_late = score_steps(gid)
                v_steps = value_steps(before) if before is not None else []
                done += sum(keys_of(i) for i in g[4])
                p = SPREAD[g[1]]
                if gi == 0:
                    keys_first = done
                    plan.extend(merged((s_steps, p[0], 1.0), (v_steps, 0.0, p[1]), (early, 0.0, 1.0)))
                    plan.extend(s_late)
                    if u >= 1:
                        plan.extend(final_steps(layer, u - 1))
                    before = gid
                    continue
                upto = min(len(fill), math.ceil(len(fill) * (done - keys_first) / (total - keys_first) * p[6]))
                part = fill[placed:upto]
                placed = max(placed, upto)
                if gi == 1:
                    plan.extend(merged((s_steps, 0.0, 1.0), (second, 0.0, 0.8), (v_steps, 0.85, 1.0),
                                       (part, 0.8, 1.0)))
                    plan.extend(s_late)
                elif gi == len(gl) - 1:
                    plan.extend(merged((s_steps, 0.0, p[4]), (v_steps, p[2], 1.0), (part, 0.0, p[4]),
                                       (q_next(u), p[4], 1.0), (s_late, p[5], 1.0)))
                else:
                    plan.extend(merged((s_steps, 0.0, p[3]), (v_steps, p[2], 1.0), (part, 0.0, 1.0)))
                    plan.extend(s_late)
                before = gid
        plan.extend([("YL", layer, 0), ("YL", layer, 1)] + value_steps(before))

    for kind in ("k0", "v0", "q0"):
        plan.extend(proj(kind, 0))
    plan.append(("VT", 0, 0))

    def fills0(u):
        if u + 1 == UNITS:
            return [], proj("g0", u), [("WO", 0)]
        return proj("k0", u + 1), proj("g0", u), proj("v0", u + 1) + [("VT", 0, u + 1)]

    run_layer(0, fills0, lambda u: proj("q0", u + 1) if u + 1 < UNITS else [])
    for b in [META_Q] + list(range(NB)):
        plan.append(("O", 0, b))
    plan.extend(proj("cq", 0)[:2])
    plan.append(("OT", 0))
    plan.extend(proj("cq", 0)[2:])
    for j in range(1, QL_T):
        plan.extend(proj("cq", j))
    for j in range(KVL_T):
        plan.extend(proj("ckv", j))
    plan.extend(proj("kpe", 0))
    plan.extend(proj("g1", 0))
    plan.extend(proj("ncq", 0))
    plan.extend(proj("g1", 1))
    plan.extend(proj("nckv", 0))
    for h in range(2, HEADS):
        plan.extend(proj("g1", h))
    for kind in ("kn", "vn", "qr", "qn"):
        plan.extend(proj(kind, 0))
    plan.append(("VT", 1, 0))

    def fills1(u):
        if u + 1 == HEADS:
            return [], [("L", u)], [("WO", 1)]
        return proj("kn", u + 1), [("L", u)], proj("vn", u + 1) + [("VT", 1, u + 1)]

    run_layer(1, fills1, lambda u: (proj("qr", u + 1) if (u + 1) % 2 == 0 else []) + proj("qn", u + 1)
              if u + 1 < HEADS else [])
    for b in range(NB):
        plan.append(("O", 1, b))
    return plan, groups, tsteps


SPREAD = {"A": [0.15, 0.95, 0.15, 0.9, 0.6, 0.85, 1.1],
          "B": [0.15, 0.95, 0.15, 0.9, 0.6, 0.85, 1.1],
          "C": [0.15, 0.95, 0.15, 0.9, 0.6, 0.85, 1.1]}


PLAN, GROUPS, TSTEPS = make_plan()
NORMS = ("rms0", "ncq", "nckv")
KT_OF = {"q0": KD, "k0": KD, "v0": KD, "g0": KD, "cq": KD, "ckv": KD, "kpe": KD, "g1": KD,
         "kn": KVL_T, "vn": KVL_T, "qn": QL_T, "qr": QL_T}
PROJ = [s for s in PLAN if s[0] == "P"]
PTURN = {s: n for n, s in enumerate(PROJ)}
N_CONSTS = 7
TILES = []
for _s in PROJ:
    if _s[1] not in NORMS and _s[3] == 0:
        TILES.append(_s[1:3])
TILE_AT = {s: n for n, s in enumerate(TILES)}
_l0 = sum(1 for k, _ in TILES if k[1] == "0")
O_STEPS = [s for s in PLAN if s[0] == "O"]
O_AT = {s: n for n, s in enumerate(O_STEPS)}
WEIGHTS = TILES[:_l0] + [("wo0", k) for k in range(KD)] + [("y", n) for n in range(NB + 1)] \
    + TILES[_l0:] + [("wo1", k) for k in range(KD)] + [("y", n) for n in range(NB + 1, 2 * NB + 1)]
WEIGHT_AT = {s: n for n, s in enumerate(WEIGHTS)}
STATIONARY = [s for s in WEIGHTS if s[0] not in ("wo0", "wo1")]
SLOT = {s: n % 2 for n, s in enumerate(STATIONARY)}
NO_HI = ("v0", "vn", "cq", "ckv")


def count_before(items, good):
    out, n = {}, 0
    for s in items:
        n += bool(good(s))
        out[s] = n
    return out


HI_COUNT = count_before(PROJ, lambda s: s[1] not in NO_HI)
S_CHUNK, _n = {}, 0
S_OWNER = []
for _s in PLAN:
    if _s[0] == "S":
        S_CHUNK[_s[1:]] = len(S_OWNER)
        S_OWNER.append("dve" if GROUPS[TSTEPS[_s[1]][0]][1] == "A" else "act")
S_FREED = [S_OWNER[:n + 1].count(S_OWNER[n]) for n in range(len(S_OWNER))]
MAPS_DONE = {}
STATS_DONE = {}
for _s in PLAN:
    if _s[0] == "E":
        _kind = GROUPS[TSTEPS[_s[1]][0]][1]
        if _kind == "A":
            MAPS_DONE[_s[1:]] = len(MAPS_DONE) + 1
        if _kind != "B":
            STATS_DONE[_s[1:]] = len(STATS_DONE) + 1
T_TURN, RING, _t, _r = {}, {}, 0, 0
for _s in PLAN:
    if _s[0] == "VT":
        for _k in range(3):
            T_TURN[_s, _k] = _t
            _t += 1
    if _s[0] == "T":
        T_TURN[_s[1], _s[2]] = _t
        RING[_s[1], _s[2]] = _r
        _t, _r = _t + 1, _r + 1
    if _s[0] == "O" and _s[1] == 0:
        for _k in range(2):
            T_TURN[_s, _k] = _t
            _t += 1
B_GROUPS = [g for g in range(len(GROUPS)) if GROUPS[g][1] == "B"]
GROUP_STEPS = {g: [t for t in range(len(TSTEPS)) if TSTEPS[t][0] == g] for g in range(len(GROUPS))}
FIRST_C = min(t for t in range(len(TSTEPS)) if GROUPS[TSTEPS[t][0]][1] == "C")
LAST_T = {g: T_TURN[g, len(turns_of(GROUPS[g][4])) - 1] for g in range(len(GROUPS))}
V_TILES = [[0, 1, 2], [3, 4, 5], [6, 7, 8]]
STORES = [s for s in PLAN if s[0] == "F" or (s[0] == "Y" and GROUPS[s[1]][1] != "A")]
STORE_AT = {s: n for n, s in enumerate(STORES)}


def make_fill():
    fill = [None] * len(PLAN)
    start = 0
    for at, s in enumerate(PLAN):
        if s[0] == "O":
            start = at + 1
        if s[0] != "P":
            continue
        spots = [n for n in range(start, at) if PLAN[n][0] in ("S", "T", "X")]
        if s[1] not in NORMS and spots:
            left = 3 * KT_OF[s[1]] - 1
            for k, n in enumerate(spots):
                take = -(-left // (len(spots) - k + 1))
                fill[n] = (s, take)
                left -= take
        start = at + 1
    return fill


FILL = make_fill()
O_AT = {s: n for n, s in enumerate(O_STEPS)}
G1_STORES = HEADS


def square_at(kind, c, j):
    return QL_T * c + j if kind == "ncq" else QL_T * len(CHUNKS) + KVL_T * c + j


def square_used(k):
    n_cq = QL_T * len(CHUNKS)
    kind, nt, c, j = ("ncq", QL_T, *divmod(k, QL_T)) if k < n_cq else ("nckv", KVL_T, *divmod(k - n_cq, KVL_T))
    if j == nt - 1:
        return "proj_done", PTURN[("P", kind, 0, c)] + 1
    before = c * (nt - 1) + (0 if kind == "ncq" else len(CHUNKS) * (QL_T - 1))
    return "lsq_used", before + j + 1


def unit_groups(layer, u):
    return [g for g in range(len(GROUPS)) if GROUPS[g][0] == layer and GROUPS[g][2] == u]


def q_scale(u):
    return SCALE64 / SLOPES[u] if u < A_UNITS else 1.0


def last_turn(kind, u):
    return PTURN[("P", kind, u, len(CHUNKS) - 1)]


def trunk_kernel(nc, ht, x, meta, w0, wo0, w1, wuq_n, wuq_r, wukv, wo1, lng, lnb, lam, subln,
                 qnorm, kvnorm, dist, masks, eyeb, rope, out):
    yd = nc.dram_tensor("y_scratch", (2, UNITS, 128, TOK), F32, kind="Internal").ap()
    gd = nc.dram_tensor("gate_scratch", (HEADS, 128, TOK), F32, kind="Internal").ap()
    hd = nc.dram_tensor("h1_scratch", (SEQ, D), F32, kind="Internal").ap()

    ctx = ExitStack()
    with ctx:
        def sem(name):
            return ctx.enter_context(nc.semaphore(name))

        def sb(name, shape, dt, where=ctx):
            return where.enter_context(nc.sbuf_tensor(name, shape, dt))

        big = sb("big", [128, 2, KD, TOK], F32R)
        wraw = sb("wraw", [128, 2, KD * 128], F32)
        wsp = sb("wsp", [128, 2, 2, KD, 128], F32R)
        eye = sb("eye", [128, 128], F32)
        ones = sb("ones", [128, 128], F32)
        eyebf = sb("eyebf", [128, 128], BF16)
        mask = sb("mask", [128, 2, 128], BF16)
        stat = sb("stat", [128, 4, 16], F32)
        small = sb("small", [128, 64], F32)
        lamv = sb("lamv", [128, 4, DH], F32)
        eps = sb("eps", [128, 2], F32)
        rmsg = sb("rmsg", [128, 8], F32)
        wok = big[:, :, :, 0:D]

        st = ExitStack()
        kst = sb("kst", [128, 2, 2, TOK], F32R, st)
        qst = sb("qst", [128, 2, 2, TOK], F32R, st)
        vt = sb("vt", [128, TOK], F32, st)
        gate = sb("gate", [128, TOK], F32, st)
        ot = sb("ot", [128, TOK], F32, st)
        sq = sb("sq", [128, TOK], F32, st)
        otmp = sb("otmp", [64, 256], F32, st)
        distt = sb("distt", [128, TOK], F16, st)
        st2 = ExitStack()
        xin = sb("xin", [128, KD, TOK], F32, st2)
        st2.close()
        vtok = sb("vtok", [128, 2, 2, 9, 128], F32R, st)
        ring = sb("ring", [128, NRING, 2, 512], F32R, st)
        tb = sb("tb", [128, 2, 2, TOK], F32, st)
        pb = sb("pb", [128, 2, 2, TOK], F32, st)
        st.close()
        st = ExitStack()
        h1t = sb("h1t", [128, 2, KD, TOK], F32R, st)
        st2 = ExitStack()
        xres = sb("xres", [128, 2, D], F32, st2)
        res = sb("res", [128, 2, D], F32, st2)
        lngb = sb("lngb", [128, 2, D], F32, st2)
        st2.close()
        st2 = ExitStack()
        lraw = sb("lraw", [128, QL_T + KVL_T, TOK], F32, st2)
        gtmp = sb("gtmp", [128, 2, TOK], F32, st2)
        st2.close()
        st.close()
        st = ExitStack()
        kh = sb("kh", [128, 2, 2, TOK], F32R, st)
        qh = sb("qh", [128, 2, TOK], F32R, st)
        qpe = sb("qpe", [128, 2, 2, TOK], F32R, st)
        vtok1 = sb("vtok1", [128, 2, 2, 9, 128], F32R, st)
        vt1 = sb("vt1", [128, TOK], F32, st)
        gate1 = sb("gate1", [128, TOK], F32, st)
        ot1 = sb("ot1", [128, TOK], F32, st)
        ring1 = sb("ring1", [128, NRING, 2, 512], F32R, st)
        pb1 = sb("pb1", [128, 2, 2, TOK], F32, st)
        ropet = sb("ropet", [128, 2, TOK], F32, st)
        kpe = sb("kpe", [128, TOK], F32R, st)
        rtmp = sb("rtmp", [128, 2, 352], F32, st)
        lsq = rtmp
        st.close()
        st = ExitStack()
        xres1 = sb("xres1", [128, 2, D], F32, st)
        res1 = sb("res1", [128, 2, D], F32, st)
        lngb1 = sb("lngb1", [128, 2, D], F32, st)
        st.close()

        bank = [ctx.enter_context(nc.psum_tensor(f"bank{n}", [128, 512], F32)) for n in range(8)]
        PJ, SC, TR, PO = bank[0:2], bank[2:5], bank[5:7], bank[7]

        lat = {"ncq": (0, QL_T, 1), "nckv": (QL_T, KVL_T, 1 + QL_T)}
        L0T = dict(ring=ring, pb=pb, vtok=vtok, vt=vt, gate=gate, ot=ot)
        L1T = dict(ring=ring1, pb=pb1, vtok=vtok1, vt=vt1, gate=gate1, ot=ot1)

        def bufs(layer):
            return L1T if layer else L0T

        names = """consts const_dve const_pool x_in_0 x_in_1 x_in_2 x_in_3 x_in_4 x_in_5 x_split w_raw_0 w_raw_1 w_ready w_used proj_done proj_hi
            proj_evac s_done s_free_dve s_free_act max_ready exp_done p_ready tr_done tr_hi tr_lo
            pv_done o_done o_tmp o_evac sq_done unit_done y_stored_0 y_stored_1 act_step dve_step pool_step
            g_done g_stored_0 g_stored_1 g_loaded res_in_0 res_in_1 y_done y_evac
            res_used ln_mid ln_mid2 ln_norm ln_scaled h_ready h_stored_0 h_stored_1 lnp_in lam_exp rope_in
            lat_sq lsq_used x_hi ln_stats ln_rstd""".split()
        S = {n: sem(n) for n in names}

        def out_bank(n, half):
            return bank[2 * ((n + 1) % 2) + half]

        def slot(name, n):
            return S[f"{name}_{n % 2}"]

        def arrived(eng, name, n):
            eng.wait_ge(slot(name, n), 16 * (n // 2 + 1))

        def all_arrived(eng, name, count):
            for n in range(max(count - 2, 0), count):
                arrived(eng, name, n)

        block = ctx.enter_context(nc.Block())
        lo_hi = lambda ap: ap.bitcast(F32)

        def rhs_of(kind):
            if kind in ("q0", "k0", "v0", "g0"):
                return big, 0
            if kind in ("cq", "ckv", "kpe", "g1"):
                return h1t, 0
            return (big, 0) if kind in ("qn", "qr") else (big, QL_T)

        def w_src(kind, u):
            if kind in ("q0", "k0", "v0", "g0"):
                return w0[u, "qkvg".index(kind[0])]
            if kind == "cq":
                return w1[u]
            if kind == "ckv":
                return w1[QL_T + u]
            if kind == "kpe":
                return w1[QL_T + KVL_T]
            if kind == "g1":
                return w1[QL_T + KVL_T + 1 + u]
            if kind == "qn":
                return wuq_n[u]
            if kind == "qr":
                return wuq_r[u // 2]
            return wukv[u, 0 if kind == "kn" else 1]

        LAST0 = last_turn("g0", UNITS - 1)
        LAST_IN1 = last_turn("g1", HEADS - 1)
        LAST1 = last_turn("qn", HEADS - 1)

        def store_of(layer, b):
            blocks = [0, 1] if b == META_Q else [b // 2 * 2, b // 2 * 2 + 1]
            g = [g for g in unit_groups(layer, UNITS - 1) if GROUPS[g][4] == blocks][-1]
            return STORE_AT["Y", g]

        def group_cols(g):
            blocks = GROUPS[g][4]
            return (0, META) if blocks == [META_Q] else (META + 128 * blocks[0], 256)

        @block.sync
        def _(sp):
            def weights(upto):
                while issued[0] <= min(upto, len(WEIGHTS) - 1):
                    n = issued[0]
                    kind, u = WEIGHTS[n]
                    if n >= 2:
                        sp.wait_ge(S["w_ready"], n - 1)
                    if kind == "y":
                        _, layer, b = O_STEPS[u]
                        c0, _ = query_cols(b)
                        for k in (1, 0):
                            arrived(sp, "y_stored", store_of(layer, b) - k)
                        dst = wraw[:, n % 2, :].rearrange("p (k c) -> p k c", k=KD)
                        src = yd[layer, :, :, c0:c0 + 128].rearrange("u p c -> p u c")
                    elif kind in ("wo0", "wo1"):
                        dst, src = wraw[:, n % 2, :], (wo1 if kind == "wo1" else wo0)[:, u, :]
                    else:
                        dst, src = wraw[:, n % 2, 0:KT_OF[kind] * 128], w_src(kind, u)
                    sp.dma_start(dst, src).then_inc(slot("w_raw", n), 16)
                    issued[0] += 1

            issued = [0]
            weights(0)
            for n, (k0, c0, w) in enumerate(X_PIECES):
                sp.dma_start(xin[:, k0:k0 + KD // 2, c0:c0 + w], ht[:, k0:k0 + KD // 2, c0:c0 + w])\
                    .then_inc(S[f"x_in_{n}"], 16)
            sp.dma_start(eyebf[:, :], eyeb).then_inc(S["consts"], 16)
            sp.dma_start(mask[:, :, :], masks).then_inc(S["consts"], 16)
            sp.dma_start(distt[:, :], dist).then_inc(S["consts"], 16)
            sp.dma_start(lamv[:, :, :], lam).then_inc(S["consts"], 16)
            sp.dma_start(rmsg[:, 0:1], subln).then_inc(S["consts"], 16)
            sp.dma_start(rmsg[:, 1:5], qnorm).then_inc(S["consts"], 16)
            sp.dma_start(rmsg[:, 5:7], kvnorm).then_inc(S["consts"], 16)

            weights(1)
            for s in PLAN:
                if s[0] == "P":
                    if s[1] not in NORMS and s[3] == 0:
                        weights(WEIGHT_AT[s[1:3]] + 2)
                    if s == ("P", "cq", 0, 0):
                        sp.wait_ge(S["tr_lo"], T_TURN[("O", 0, NB - 1), 1] + 1)
                        all_arrived(sp, "h_stored", NB)
                        sp.dma_start(ropet[:, :, :], rope).then_inc(S["rope_in"], 16)
                    if s[1] == "g1" and s[3] == len(CHUNKS) - 1:
                        sp.wait_ge(S["proj_evac"], PTURN[s] + 1)
                        sp.dma_start(gd[s[2]], gtmp[:, s[2] % 2, :]).then_inc(slot("g_stored", s[2]), 16)
                if s in STORE_AT:
                    if s[0] == "F":
                        u = s[1]
                        sp.wait_ge(S["unit_done"], u + 1)
                        dst, src = yd[0, u], ot[:, :]
                    else:
                        layer, kind, u, head, _ = GROUPS[s[1]]
                        c0, w = group_cols(s[1])
                        rows = slice(DH * head, DH * head + DH) if kind == "B" else slice(0, 128)
                        sp.wait_ge(S["o_evac"], s[1] + 1)
                        dst, src = yd[layer, u, rows, c0:c0 + w], bufs(layer)["ot"][rows, c0:c0 + w]
                    sp.dma_start(dst, src).then_inc(slot("y_stored", STORE_AT[s]), 16)
                if s[0] == "L":
                    if s[1] == 0:
                        all_arrived(sp, "g_stored", HEADS)
                    else:
                        sp.wait_ge(S["o_evac"], unit_groups(1, s[1] - 1)[-1] + 1)
                    sp.dma_start(gate1[:, :], gd[s[1]]).then_inc(S["g_loaded"], 16)
                if s[0] == "YL":
                    weights(WEIGHT_AT["y", (NB + 1) * s[1] + s[2]])
                if s[0] == "WO":
                    weights(WEIGHT_AT[("wo1" if s[1] else "wo0"), KD - 1])
                if s[0] == "O" and O_AT[s] in (0, NB + 1):
                    layer = s[1]
                    all_arrived(sp, "y_stored", STORE_AT["Y", unit_groups(layer, UNITS - 1)[-1]] + 1)
                    g_, b_ = (lngb1 if layer else lngb)[:, 0, :], (lngb1 if layer else lngb)[:, 1, :]
                    sp.dma_start(g_, lng[layer:layer + 1, :].to_broadcast([128, D])).then_inc(S["lnp_in"], 16)
                    sp.dma_start(b_, lnb[layer:layer + 1, :].to_broadcast([128, D])).then_inc(S["lnp_in"], 16)
                if s[0] == "O":
                    layer, b = s[1], s[2]
                    n = O_AT[s]
                    rows = META if b == META_Q else 128
                    xr = xres1 if layer else xres
                    weights(WEIGHT_AT["y", n] + 1)
                    if n - (NB + 1) * layer >= 2:
                        sp.wait_ge(S["y_evac"], n - 1)
                    if layer:
                        all_arrived(sp, "h_stored", NB)
                    src = (hd[128 * b:128 * b + 128, :] if layer else
                           meta[:, :] if b == META_Q else x[128 * b:128 * b + 128, :])
                    sp.dma_start(xr[0:rows, n % 2, :], src).then_inc(slot("res_in", n), 16)
            all_arrived(sp, "h_stored", 2 * NB)


        @block.gpsimd
        def _(pool):
            step = [0]

            def tick(ins):
                step[0] += 1
                ins.then_inc(S["pool_step"], 1)
                return step[0]

            nc.gpsimd.memset(ones[:, :], 1.0).then_inc(S["const_pool"], 1)
            nc.gpsimd.memset(eps[:, 0:1], RMS_EPS).then_inc(S["const_pool"], 1)
            nc.gpsimd.memset(eps[:, 1:2], LN_EPS).then_inc(S["const_pool"], 1)
            pool.wait_ge(S["pool_step"], tick(nc.gpsimd.memset(eye[:, :], 0.0)))
            nc.gpsimd.affine_select(out=eye[:, :], in_=eye[:, :], compare_op=ALU.not_equal, fill=1.0,
                                    base=0, pattern=[[-1, 128]], channel_multiplier=1)\
                .then_inc(S["const_pool"], 1)

            def split(hi, lo, raw):
                pool.wait_ge(S["pool_step"], tick(nc.gpsimd.tensor_scalar(hi, raw, 1.0, 1.0, ALU.mult, ALU.mult)))
                return nc.gpsimd.tensor_tensor(lo, raw, lo_hi(hi), ALU.subtract)

            def split_weights(upto):
                while split_[0] <= min(upto, len(WEIGHTS) - 1):
                    n = split_[0]
                    kind, u = WEIGHTS[n]
                    arrived(pool, "w_raw", n)
                    if kind in ("wo0", "wo1"):
                        if u == 0:
                            pool.wait_ge(S["proj_done"], (LAST1 if kind == "wo1" else LAST0) + 1)
                        split(wok[:, 0, u, :], wok[:, 1, u, :], wraw[:, n % 2, :]).then_inc(S["w_ready"], 1)
                    else:
                        kt, i = KT_OF.get(kind, KD), STATIONARY.index((kind, u))
                        if i >= 2:
                            before = STATIONARY[i - 2]
                            if before[0] == "y":
                                pool.wait_ge(S["y_done"], before[1] + 1)
                            else:
                                pool.wait_ge(S["proj_done"], last_turn(*before) + 1)
                        split(wsp[:, i % 2, 0, 0:kt, :], wsp[:, i % 2, 1, 0:kt, :],
                              wraw[:, n % 2, 0:kt * 128].rearrange("p (k c) -> p k c", k=kt)).then_inc(S["w_ready"], 1)
                    split_[0] += 1

            split_ = [0]
            split_weights(0)
            for s in PLAN:
                if s[0] == "P" and s[1] not in NORMS and s[3] == 0:
                    split_weights(WEIGHT_AT[s[1:3]] + 1)
                if s[0] == "WO":
                    split_weights(WEIGHT_AT[("wo1" if s[1] else "wo0"), KD - 1])
                if s[0] == "YL":
                    split_weights(WEIGHT_AT["y", (NB + 1) * s[1] + s[2]])
                if s[0] == "O":
                    layer, b = s[1], s[2]
                    n = O_AT[s]
                    split_weights(WEIGHT_AT["y", n] + 1)
                    rs = res1 if layer else res
                    lg = lngb1 if layer else lngb
                    rows = META if b == META_Q else 128
                    pool.wait_ge(S["ln_scaled"], n + 1)
                    nc.gpsimd.tensor_tensor(rs[0:rows, n % 2, :], rs[0:rows, n % 2, :], lg[0:rows, 1, :],
                                            ALU.add).then_inc(S["h_ready"], 1)

        def p_free(eng, g):
            if g >= 2:
                eng.wait_ge(S["tr_done"], LAST_T[g - 2] + 1)

        def turn_extent(g, k):
            blocks = GROUPS[g][4]
            tiles = turns_of(blocks)[k]
            if blocks == [META_Q]:
                return META, META
            if tiles == [0]:
                return META, 256
            return 128, (384 if tiles[-1] == blocks[-1] + 1 else 512)

        def v_parts(s, k, part):
            _, layer, u = s
            tiles = V_TILES[k]
            a, b = tiles[0], tiles[-1] + 1
            src = TR[T_TURN[s, k] % 2][:, 0:384].rearrange("p (t d) -> p t d", t=3)
            v = bufs(layer)["vtok"]
            if layer == 1 or u < A_UNITS:
                return [(v[:, u % 2, part, a:b, :], v[:, u % 2, 0, a:b, :], src)]
            return [(v[:, u % 2, m, a:b, DH * part:DH * part + DH], v[:, u % 2, m, a:b, 0:DH],
                     src[:, :, DH * m:DH * m + DH]) for m in range(2)]

        @block.scalar
        def _(act):
            A = nc.scalar.activation

            def split_x():
                for n, (k0, c0, w) in enumerate(X_PIECES):
                    act.wait_ge(S[f"x_in_{n}"], 16)
                    ks = slice(k0, k0 + KD // 2)
                    A(big[:, 0, ks, c0:c0 + w], xin[:, ks, c0:c0 + w], ACT.Copy).then_inc(S["x_hi"], 1)

            def evacuate(s):
                _, kind, u, c = s
                if kind in NO_HI:
                    return
                turn = PTURN[s]
                c0, w = CHUNKS[c]
                cc = slice(c0, c0 + w)
                src = PJ[turn % 2]
                if kind in ("ncq", "nckv"):
                    t0, nt, _ = lat[kind]
                    if c == 0:
                        act.wait_ge(S["proj_evac"], last_turn(*(("cq", QL_T - 1) if kind == "ncq" else ("ckv", KVL_T - 1))) + 1)
                        act.wait_ge(S["proj_evac"], last_turn("kpe", 0) + 1)
                    for j in range(nt):
                        k = square_at(kind, c, j)
                        if k >= 2:
                            name, value = square_used(k - 2)
                            act.wait_ge(S[name], value)
                        A(lsq[:, k % 2, 0:w], lraw[:, t0 + j, cc], ACT.Square).then_inc(S["lat_sq"], 1)
                act.wait_ge(S["proj_done"], turn + 1)
                if kind == "k0":
                    for m in range(2):
                        ins = A(kst[0:64, u % 2, m, cc], src[64 * m:64 * m + 64, 0:w], ACT.Copy)
                elif kind == "q0":
                    for m in range(2):
                        for z in range(2):
                            ins = A(qst[64 * z:64 * z + 64, m, 0, cc], src[64 * m:64 * m + 64, 0:w],
                                    ACT.Copy, scale=q_scale(u))
                elif kind == "g0":
                    if c == 0 and u >= 1:
                        if u - 1 < A_UNITS:
                            act.wait_ge(S["unit_done"], u)
                        else:
                            act.wait_ge(S["o_evac"], unit_groups(0, u - 1)[-1] + 1)
                    ins = A(gate[:, cc], src[:, 0:w], ACT.Sigmoid)
                elif kind == "g1":
                    if c == 0 and u >= 2:
                        arrived(act, "g_stored", u - 2)
                    ins = A(gtmp[:, u % 2, cc], src[:, 0:w], ACT.Sigmoid)
                elif kind == "rms0":
                    ins = A(sq[:, cc], src[:, 0:w], ACT.Sqrt, bias=eps[:, 0:1], scale=1.0 / 128)
                elif kind in ("ncq", "nckv"):
                    ins = A(src[:, 0:w], src[:, 0:w], ACT.Sqrt, bias=eps[:, 0:1], scale=1.0 / (128 * lat[kind][1]))
                elif kind in ("kpe", "qr"):
                    if turn >= 1:
                        act.wait_ge(S["proj_evac"], turn)
                    for z in range(4):
                        a = 32 * (z ^ 1)
                        ins = A(rtmp[32 * z:32 * z + 32, 0, 0:w], src[a:a + 32, 0:w], ACT.Copy)
                elif kind == "kn":
                    ins = A(kh[:, u % 2, 0, cc], src[:, 0:w], ACT.Copy)
                elif kind == "qn":
                    ins = A(qh[:, 0, cc], src[:, 0:w], ACT.Copy)
                ins.then_inc(S["proj_hi"], 1)

            def turned_v(s):
                _, layer, u = s
                for k in range(3):
                    if k == 0 and u >= 2:
                        g = unit_groups(layer, u - 2)[-1]
                        act.wait_ge(S["pv_done"], RING[g, len(turns_of(GROUPS[g][4])) - 1] + 1)
                    act.wait_ge(S["tr_done"], T_TURN[s, k] + 1)
                    for dst, _, src in v_parts(s, k, 0):
                        ins = A(dst, src, ACT.Copy)
                    ins.then_inc(S["tr_hi"], 1)

            def sigmoids(t, c):
                g, i, slot = TSTEPS[t]
                if GROUPS[g][1] != "B":
                    return
                rows = META if i == META_Q else 128
                c0, w = score_chunks(i)[c]
                if c == 0 and t >= 2:
                    act.wait_ge(S["p_ready"], t - 1)
                b = S_CHUNK[t, 0, c]
                act.wait_ge(S["s_done"], b + 1)
                src = SC[b % SBANKS][0:rows, 0:w]
                A(tb[0:rows, t % 2, 0, c0:c0 + w], src, ACT.Sigmoid, scale=-SCALE64)
                A(tb[0:rows, t % 2, 1, c0:c0 + w], src, ACT.Sigmoid, scale=SCALE64).then_inc(S["s_free_act"], 1)

            def exps(t, m):
                g, i, slot = TSTEPS[t]
                layer, kind, u, head, _ = GROUPS[g]
                if kind == "B":
                    return
                n = keys_of(i)
                rows = META if i == META_Q else 128
                st_ = lambda a, b: stat[0:rows, t % 4, a:b]
                if kind == "C":
                    if t == FIRST_C:
                        all_arrived(act, "g_stored", HEADS)
                    p_free(act, g)
                act.wait_ge(S["max_ready"], STATS_DONE[t, m])
                if kind == "A":
                    A(tb[0:rows, t % 2, m, 0:n], tb[0:rows, t % 2, m, 0:n], ACT.Exp, bias=st_(6 + m, 7 + m),
                      scale=SLOPES[u], accum_out=st_(8 + m, 9 + m)).then_inc(S["exp_done"], 1)
                    return
                for c, (c0, w) in enumerate(score_chunks(i)):
                    b = S_CHUNK[t, 0, c]
                    A(pb1[:, g % 2, slot, c0:c0 + w], SC[b % SBANKS][:, 0:w], ACT.Exp, bias=st_(6, 7),
                      scale=SCALE192, accum_out=st_(8 + c, 9 + c)).then_inc(S["s_free_act"], 1)

            def turned_weights(g, k):
                R = bufs(GROUPS[g][0])["ring"]
                t, r = T_TURN[g, k], RING[g, k]
                rows, w = turn_extent(g, k)
                if r >= NRING:
                    act.wait_ge(S["pv_done"], r - NRING + 1)
                act.wait_ge(S["tr_done"], t + 1)
                A(R[0:rows, r % NRING, 0, 0:w], TR[t % 2][0:rows, 0:w], ACT.Copy).then_inc(S["tr_hi"], 1)

            def output(g):
                _, kind, _, _, blocks = GROUPS[g]
                if kind != "B":
                    return
                w = META if blocks == [META_Q] else 256
                act.wait_ge(S["pv_done"], RING[g, len(turns_of(blocks)) - 1] + 1)
                act.wait_ge(S["o_evac"], g)
                A(otmp[:, 0:w], PO[64:128, 0:w], ACT.Copy).then_inc(S["o_tmp"], 1)

            def norm_block(s):
                _, layer, b = s
                n = O_AT[s]
                rows = META if b == META_Q else 128
                o = 32 * (n % 2)
                rs = res1 if layer else res
                act.wait_ge(S["ln_stats"], n + 1)
                A(small[0:rows, o + 14:o + 15], small[0:rows, o + 13:o + 14], ACT.Sqrt, bias=eps[0:rows, 1:2])\
                    .then_inc(S["ln_mid"], 1)
                act.wait_ge(S["ln_rstd"], n + 1)
                A(rs[0:rows, n % 2, :], rs[0:rows, n % 2, :], ACT.Identity, scale=small[0:rows, o + 15:o + 16],
                  bias=small[0:rows, o + 16:o + 17]).then_inc(S["ln_norm"], 1)

            def store_block(s):
                _, layer, b = s
                if b == META_Q:
                    return
                n = O_AT[s]
                act.wait_ge(S["h_ready"], n + 1)
                dst = out if layer else hd
                act.dma_start(dst[128 * b:128 * b + 128, :], (res1 if layer else res)[:, n % 2, :])\
                    .then_inc(slot("h_stored", NB * layer + b), 16)

            def turned_h(s):
                b = s[2]
                c0, w = query_cols(b)
                for k in range(2):
                    t = T_TURN[s, k]
                    act.wait_ge(S["tr_done"], t + 1)
                    A(h1t[:, 0, 4 * k:4 * k + 4, c0:c0 + w],
                      TR[t % 2][:, :].rearrange("p (j c) -> p j c", j=4)[:, :, 0:w], ACT.Copy).then_inc(S["tr_hi"], 1)

            act.wait_ge(S["const_pool"], 4)
            split_x()
            act.wait_ge(S["lam_exp"], 1)
            A(small[:, 60:62], small[:, 62:64], ACT.Exp).then_inc(S["act_step"], 1)
            last = None
            for s in PLAN:
                if s[0] == "P":
                    evacuate(s)
                elif s[0] == "VT":
                    turned_v(s)
                elif s[0] == "S":
                    sigmoids(s[1], s[3])
                elif s[0] == "E":
                    exps(*s[1:])
                elif s[0] == "T":
                    turned_weights(*s[1:])
                elif s[0] == "Y":
                    output(s[1])
                elif s[0] == "SQ":
                    act.wait_ge(S["o_evac"], unit_groups(0, s[1])[-1] + 1)
                    if s[1] >= 1:
                        act.wait_ge(S["proj_evac"], last_turn("rms0", s[1] - 1) + 1)
                    A(sq[:, :], ot[:, :], ACT.Square).then_inc(S["sq_done"], 1)
                elif s[0] == "O":
                    norm_block(s)
                    if last is not None:
                        store_block(last)
                        if s[1] == 0:
                            turned_h(last)
                    last = s
                elif s[0] == "OT":
                    store_block(last)
                    turned_h(last)
                    last = None
            store_block(last)

        @block.vector
        def _(dve):
            V = nc.vector
            step = [0]

            def then(ins):
                step[0] += 1
                ins.then_inc(S["dve_step"], 1)
                dve.wait_ge(S["dve_step"], step[0])

            def constants():
                dve.wait_ge(S["consts"], 16 * N_CONSTS)
                for j in range(2):
                    then(V.tensor_tensor_reduce(out=lamv[:, 2 * j, :], in0=lamv[:, 2 * j, :], in1=lamv[:, 2 * j + 1, :],
                                                scale=1.0, scalar=0.0, op0=ALU.mult, op1=ALU.add,
                                                accum_out=small[:, 62 + j:63 + j]))
                then(V.tensor_scalar(rmsg[:, 0:1], rmsg[:, 0:1], 1.0 - LAM_INIT, None, ALU.mult))
                V.tensor_scalar(rmsg[:, 7:8], rmsg[:, 0:1], 0.0, None, ALU.mult).then_inc(S["lam_exp"], 1)

            def negative_lambda():
                dve.wait_ge(S["act_step"], 1)
                then(V.tensor_tensor(small[:, 58:59], small[:, 61:62], small[:, 60:61], ALU.subtract))
                then(V.tensor_scalar(small[:, 59:60], small[:, 58:59], -LAM_INIT, None, ALU.add))

            def split_x():
                for n, (k0, c0, w) in enumerate(X_PIECES):
                    dve.wait_ge(S["x_hi"], n + 1)
                    ks = slice(k0, k0 + KD // 2)
                    V.tensor_tensor(big[:, 1, ks, c0:c0 + w], xin[:, ks, c0:c0 + w], lo_hi(big[:, 0, ks, c0:c0 + w]),
                                    ALU.subtract).then_inc(S["x_split"], 1)

            def rotate(turn, cc, w):
                src = PJ[turn % 2][:, 0:w]
                dve.wait_ge(S["rope_in"], 16)
                V.tensor_tensor(rtmp[:, 1, 0:w], src, ropet[:, 0, cc], ALU.mult)
                then(V.tensor_tensor(rtmp[:, 0, 0:w], rtmp[:, 0, 0:w], ropet[:, 1, cc], ALU.mult))
                then(V.tensor_tensor(rtmp[:, 1, 0:w], rtmp[:, 0, 0:w], rtmp[:, 1, 0:w], ALU.add))

            def evacuate(s):
                _, kind, u, c = s
                turn = PTURN[s]
                c0, w = CHUNKS[c]
                cc = slice(c0, c0 + w)
                src = PJ[turn % 2]
                if kind in NO_HI:
                    dve.wait_ge(S["proj_done"], turn + 1)
                else:
                    dve.wait_ge(S["proj_hi"], HI_COUNT[s])
                if kind == "k0":
                    for m in range(2):
                        ins = V.tensor_tensor(kst[64:128, u % 2, m, cc], src[64 * m:64 * m + 64, 0:w],
                                              lo_hi(kst[0:64, u % 2, m, cc]), ALU.subtract)
                elif kind == "q0":
                    for m in range(2):
                        for z in range(2):
                            ins = V.scalar_tensor_tensor(
                                out=qst[64 * z:64 * z + 64, m, 1, cc], in0=src[64 * m:64 * m + 64, 0:w],
                                scalar=q_scale(u), in1=lo_hi(qst[0:64, m, 0, cc]), op0=ALU.mult, op1=ALU.subtract)
                elif kind in ("v0", "vn"):
                    ins = V.tensor_copy((vt1 if kind == "vn" else vt)[:, cc], src[:, 0:w])
                elif kind == "g0":
                    ins = V.tensor_tensor(gate[:, cc], src[:, 0:w], gate[:, cc], ALU.mult)
                elif kind == "g1":
                    ins = V.tensor_tensor(gtmp[:, u % 2, cc], src[:, 0:w], gtmp[:, u % 2, cc], ALU.mult)
                elif kind == "rms0":
                    then(V.reciprocal(sq[:, cc], sq[:, cc]))
                    ins = V.scalar_tensor_tensor(out=ot[:, cc], in0=ot[:, cc], scalar=rmsg[:, 0:1], in1=sq[:, cc],
                                                 op0=ALU.mult, op1=ALU.mult)
                elif kind in ("cq", "ckv"):
                    if (kind, u, c) == ("cq", 1, 0):
                        all_arrived(dve, "h_stored", NB)
                    ins = V.tensor_copy(lraw[:, u + (QL_T if kind == "ckv" else 0), cc], src[:, 0:w])
                elif kind in ("ncq", "nckv"):
                    t0, nt, gain = lat[kind]
                    then(V.reciprocal(src[:, 0:w], src[:, 0:w]))
                    for j in range(t0, t0 + nt):
                        last = V.scalar_tensor_tensor(out=lraw[:, j, cc], in0=lraw[:, j, cc],
                                                      scalar=rmsg[:, 1 + j:2 + j], in1=src[:, 0:w],
                                                      op0=ALU.mult, op1=ALU.mult)
                    then(last)
                    for j in range(t0, t0 + nt):
                        last = V.tensor_copy(big[:, 0, j, cc], lraw[:, j, cc])
                    then(last)
                    for j in range(t0, t0 + nt):
                        ins = V.tensor_tensor(big[:, 1, j, cc], lraw[:, j, cc], lo_hi(big[:, 0, j, cc]), ALU.subtract)
                elif kind == "kpe":
                    rotate(turn, cc, w)
                    then(V.tensor_copy(kpe[:, cc], rtmp[:, 1, 0:w]))
                    ins = V.tensor_tensor(kpe[64:128, cc], rtmp[64:128, 1, 0:w], lo_hi(kpe[64:128, cc]), ALU.subtract)
                elif kind == "qr":
                    rotate(turn, cc, w)
                    for h in range(2):
                        for z in range(2):
                            last = V.tensor_copy(qpe[64 * z:64 * z + 64, h, 0, cc], rtmp[64 * h:64 * h + 64, 1, 0:w])
                    then(last)
                    for h in range(2):
                        for z in range(2):
                            ins = V.tensor_tensor(qpe[64 * z:64 * z + 64, h, 1, cc], rtmp[64 * h:64 * h + 64, 1, 0:w],
                                                  lo_hi(qpe[64 * h:64 * h + 64, h, 0, cc]), ALU.subtract)
                elif kind == "kn":
                    ins = V.tensor_tensor(kh[:, u % 2, 1, cc], src[:, 0:w], lo_hi(kh[:, u % 2, 0, cc]), ALU.subtract)
                elif kind == "qn":
                    ins = V.tensor_tensor(qh[:, 1, cc], src[:, 0:w], lo_hi(qh[:, 0, cc]), ALU.subtract)
                ins.then_inc(S["proj_evac"], 1)

            def turned_v(s):
                for k in range(3):
                    dve.wait_ge(S["tr_hi"], T_TURN[s, k] + 1)
                    for dst, hi, src in v_parts(s, k, 1):
                        ins = V.tensor_tensor(dst, src, lo_hi(hi), ALU.subtract)
                    ins.then_inc(S["tr_lo"], 1)

            def scores(t, m, c):
                g, i, slot = TSTEPS[t]
                kind = GROUPS[g][1]
                if kind == "B":
                    return
                rows = META if i == META_Q else 128
                mx = stat[0:rows, t % 4, 3 * m + c:3 * m + c + 1]
                chunks = score_chunks(i)
                c0, w = chunks[c]
                b = S_CHUNK[t, m, c]
                dve.wait_ge(S["s_done"], b + 1)
                src = SC[b % SBANKS][0:rows, 0:w]
                if kind == "A":
                    if m == 0 and c == 0 and t >= 2:
                        dve.wait_ge(S["p_ready"], t - 1)
                    d0 = 128 * (NB - 1) + META if i == META_Q else 128 * (NB - 1 - i)
                    V.tensor_tensor_reduce(out=tb[0:rows, t % 2, m, c0:c0 + w], in0=src,
                                           in1=distt[0:rows, d0 + c0:d0 + c0 + w], scale=1.0, scalar=-3.0e38,
                                           op0=ALU.add, op1=ALU.max, accum_out=mx).then_inc(S["s_free_dve"], 1)
                else:
                    then(V.reduce_max(mx, src, AX_X))

            def maxima(t, m):
                g, i, slot = TSTEPS[t]
                layer, kind, u, head, _ = GROUPS[g]
                if kind == "B":
                    return
                rows = META if i == META_Q else 128
                n = len(score_chunks(i))
                st_ = lambda a, b: stat[0:rows, t % 4, a:b]
                if kind == "A":
                    dve.wait_ge(S["s_free_dve"], S_FREED[S_CHUNK[t, m, n - 1]])
                nm, mx = st_(6 + m, 7 + m), st_(3 * m, 3 * m + 1)
                if n > 1:
                    then(V.reduce_max(nm, st_(3 * m, 3 * m + n), AX_X))
                    mx = nm
                V.tensor_scalar(nm, mx, -(SLOPES[u] if kind == "A" else SCALE192), None, ALU.mult)\
                    .then_inc(S["max_ready"], 1)

            def weights(t):
                g, i, slot = TSTEPS[t]
                layer, kind, u, head, _ = GROUPS[g]
                n = keys_of(i)
                rows = META if i == META_Q else 128
                st_ = lambda a, b: stat[0:rows, t % 4, a:b]
                P = bufs(layer)["pb"][0:rows, g % 2, slot, :]
                chunks = score_chunks(i)
                if kind != "C":
                    p_free(dve, g)
                if kind == "A":
                    dve.wait_ge(S["exp_done"], MAPS_DONE[t, 1])
                    then(V.reciprocal(st_(12, 14), st_(8, 10)))
                    V.tensor_scalar(P[:, 0:n], tb[0:rows, t % 2, 0, 0:n], st_(12, 13), None, ALU.mult)
                    then(V.tensor_scalar(st_(14, 15), st_(13, 14), small[0:rows, 59:60], None, ALU.mult))
                    V.scalar_tensor_tensor(out=P[:, 0:n], in0=tb[0:rows, t % 2, 1, 0:n], scalar=st_(14, 15), in1=P[:, 0:n],
                                           op0=ALU.mult, op1=ALU.add).then_inc(S["p_ready"], 1)
                elif kind == "B":
                    dve.wait_ge(S["s_free_act"], S_FREED[S_CHUNK[t, 0, len(chunks) - 1]])
                    skip = tb[0:rows, t % 2, 0, :]
                    V.memset(P[:, n - 1:n], 1.0)
                    then(V.tensor_tensor_scan(P[:, 0:n - 1][:, ::-1], skip[:, 1:n][:, ::-1], skip[:, 1:n][:, ::-1], 1.0,
                                              ALU.mult, ALU.bypass))
                    V.tensor_tensor(P[:, 0:n], P[:, 0:n], tb[0:rows, t % 2, 1, 0:n], ALU.mult).then_inc(S["p_ready"], 1)
                else:
                    dve.wait_ge(S["s_free_act"], S_FREED[S_CHUNK[t, 0, len(chunks) - 1]])
                    if len(chunks) > 1:
                        then(V.reduce_sum(st_(12, 13), st_(8, 8 + len(chunks)), AX_X))
                        then(V.reciprocal(st_(13, 14), st_(12, 13)))
                    else:
                        then(V.reciprocal(st_(13, 14), st_(8, 9)))
                    V.tensor_scalar(P[:, 0:n], P[:, 0:n], st_(13, 14), None, ALU.mult).then_inc(S["p_ready"], 1)

            def turned_weights(g, k):
                R = bufs(GROUPS[g][0])["ring"]
                t, r = T_TURN[g, k], RING[g, k]
                rows, w = turn_extent(g, k)
                dve.wait_ge(S["tr_hi"], t + 1)
                V.tensor_tensor(R[0:rows, r % NRING, 1, 0:w], TR[t % 2][0:rows, 0:w],
                                lo_hi(R[0:rows, r % NRING, 0, 0:w]), ALU.subtract).then_inc(S["tr_lo"], 1)

            def output(g):
                layer, kind, u, head, blocks = GROUPS[g]
                B = bufs(layer)
                c0, w = group_cols(g)
                O = B["ot"]
                if kind == "A":
                    if u >= 1 and g == unit_groups(0, u)[0]:
                        arrived(dve, "y_stored", STORE_AT["F", u - 1])
                    dve.wait_ge(S["pv_done"], RING[g, len(turns_of(blocks)) - 1] + 1)
                    V.tensor_copy(O[:, c0:c0 + w], PO[:, 0:w]).then_inc(S["o_evac"], 1)
                    return
                n = STORE_AT["Y", g]
                arrived(dve, "y_stored", n - 2)
                if kind == "B":
                    if g == unit_groups(0, A_UNITS)[0]:
                        arrived(dve, "y_stored", STORE_AT["F", A_UNITS - 1])
                    rows = slice(DH * head, DH * head + DH)
                    dve.wait_ge(S["o_tmp"], B_GROUPS.index(g) + 1)
                    then(V.tensor_tensor(O[rows, c0:c0 + w], PO[0:64, 0:w], otmp[:, 0:w], ALU.add))
                    V.tensor_tensor(O[rows, c0:c0 + w], O[rows, c0:c0 + w], gate[rows, c0:c0 + w], ALU.mult)\
                        .then_inc(S["o_evac"], 1)
                else:
                    dve.wait_ge(S["g_loaded"], 16 * (u + 1))
                    dve.wait_ge(S["pv_done"], RING[g, len(turns_of(blocks)) - 1] + 1)
                    V.tensor_tensor(O[:, c0:c0 + w], PO[:, 0:w], gate1[:, c0:c0 + w], ALU.mult).then_inc(S["o_evac"], 1)

            def gated(s):
                u = s[1]
                dve.wait_ge(S["proj_evac"], last_turn("rms0", u) + 1)
                V.tensor_tensor(ot[:, :], ot[:, :], gate[:, :], ALU.mult).then_inc(S["unit_done"], 1)

            def norm_block(s):
                _, layer, b = s
                n = O_AT[s]
                rows = META if b == META_Q else 128
                o = 32 * (n % 2)
                rs, xr, lg = (res1, xres1, lngb1) if layer else (res, xres, lngb)
                base = (NB + 1) * layer
                arrived(dve, "res_in", n)
                dve.wait_ge(S["y_done"], n + 1)
                if n - base >= 2:
                    before = O_STEPS[n - 2]
                    if before[2] != META_Q:
                        arrived(dve, "h_stored", NB * layer + before[2])
                    if layer == 0:
                        dve.wait_ge(S["tr_done"], T_TURN[before, 1] + 1)
                for half in range(2):
                    hs = slice(512 * half, 512 * half + 512)
                    ins = V.scalar_tensor_tensor(out=rs[0:rows, n % 2, hs], in0=xr[0:rows, n % 2, hs], scalar=ALPHA,
                                                 in1=out_bank(n, half)[0:rows, :], op0=ALU.mult, op1=ALU.add)
                ins.then_inc(S["y_evac"], 1)
                dve.wait_ge(S["y_evac"], n + 1)
                for half in range(2):
                    ins = V.bn_stats(small[0:rows, o + 6 * half:o + 6 * half + 6], rs[0:rows, n % 2, 512 * half:512 * half + 512])
                then(ins)
                V.bn_aggr(small[0:rows, o + 12:o + 14], small[0:rows, o:o + 12]).then_inc(S["ln_stats"], 1)
                dve.wait_ge(S["ln_mid"], n + 1)
                then(V.reciprocal(small[0:rows, o + 15:o + 16], small[0:rows, o + 14:o + 15]))
                V.scalar_tensor_tensor(out=small[0:rows, o + 16:o + 17], in0=small[0:rows, o + 12:o + 13], scalar=-1.0,
                                       in1=small[0:rows, o + 15:o + 16], op0=ALU.mult, op1=ALU.mult).then_inc(S["ln_rstd"], 1)
                dve.wait_ge(S["ln_norm"], n + 1)
                dve.wait_ge(S["lnp_in"], 32 * (layer + 1))
                V.tensor_tensor(rs[0:rows, n % 2, :], rs[0:rows, n % 2, :], lg[0:rows, 0, :], ALU.mult)\
                    .then_inc(S["ln_scaled"], 1)

            def turned_h(s):
                b = s[2]
                c0, w = query_cols(b)
                for k in range(2):
                    t = T_TURN[s, k]
                    dve.wait_ge(S["tr_hi"], t + 1)
                    V.tensor_tensor(h1t[:, 1, 4 * k:4 * k + 4, c0:c0 + w],
                                    TR[t % 2][:, :].rearrange("p (j c) -> p j c", j=4)[:, :, 0:w],
                                    lo_hi(h1t[:, 0, 4 * k:4 * k + 4, c0:c0 + w]), ALU.subtract).then_inc(S["tr_lo"], 1)

            split_x()
            constants()
            negative_lambda()
            last = None
            for s in PLAN:
                if s[0] == "P":
                    evacuate(s)
                elif s[0] == "VT":
                    turned_v(s)
                elif s[0] == "S":
                    scores(*s[1:])
                elif s[0] == "E":
                    maxima(*s[1:])
                elif s[0] == "C":
                    weights(s[1])
                elif s[0] == "T":
                    turned_weights(*s[1:])
                elif s[0] == "Y":
                    output(s[1])
                elif s[0] == "F":
                    gated(s)
                elif s[0] == "O":
                    norm_block(s)
                    if s[1] == 0 and last is not None:
                        turned_h(last)
                    last = s
                elif s[0] == "OT":
                    turned_h(last)
                    last = None

        @block.tensor
        def _(pe):
            mm = nc.tensor.matmul

            def project(s):
                _, kind, u, c = s
                turn = PTURN[s]
                kt = KT_OF[kind]
                c0, w = CHUNKS[c]
                rhs, k0 = rhs_of(kind)
                if c == 0:
                    pe.wait_ge(S["w_ready"], WEIGHT_AT[kind, u] + 1)
                if kind == "cq" and u == 0:
                    pe.wait_ge(S["tr_lo"], T_TURN[("O", 0, (c0 + w - 1 - META) // 128), 1] + 1)
                if turn >= 2:
                    pe.wait_ge(S["proj_evac"], turn - 1)
                if (kind, u, c) == ("cq", 0, 0):
                    pe.wait_ge(S["y_evac"], NB)
                if (kind, u, c) in (("kn", 0, 0), ("qr", 0, 0)):
                    pe.wait_ge(S["proj_evac"], last_turn("nckv" if kind == "kn" else "ncq", 0) + 1)
                dst = PJ[turn % 2][:, 0:w]
                for k in range(kt):
                    if turn < len(CHUNKS) and k % (KD // 2) == 0:
                        pe.wait_ge(S["x_split"], 2 * turn + k // (KD // 2) + 1)
                    for a, b in ((0, 0), (0, 1), (1, 0)):
                        last = k == kt - 1 and a == 1
                        ins = mm(dst, wsp[:, SLOT[kind, u], a, k, :], rhs[:, b, k0 + k, c0:c0 + w],
                                 start=(k == 0 and a == 0 and b == 0), stop=last)
                        if last:
                            ins.then_inc(S["proj_done"], 1)
                        else:
                            yield

            def norm_sum(s):
                _, kind, u, c = s
                turn = PTURN[s]
                c0, w = CHUNKS[c]
                if turn >= 2:
                    pe.wait_ge(S["proj_evac"], turn - 1)
                dst = PJ[turn % 2][:, 0:w]
                if kind == "rms0":
                    pe.wait_ge(S["sq_done"], u + 1)
                    ins = mm(dst, ones[:, :], sq[:, c0:c0 + w], start=True, stop=True)
                else:
                    _, nt, _ = lat[kind]
                    for j in range(nt):
                        k = square_at(kind, c, j)
                        pe.wait_ge(S["lat_sq"], k + 1)
                        ins = mm(dst, ones[:, :], lsq[:, k % 2, 0:w], start=(j == 0), stop=(j == nt - 1))
                        if j < nt - 1:
                            ins.then_inc(S["lsq_used"], 1)
                ins.then_inc(S["proj_done"], 1)

            def turn_v(s):
                _, layer, u = s
                if s == ("VT", 0, 0):
                    pe.wait_ge(S["const_pool"], 4)
                    pe.wait_ge(S["consts"], 16 * N_CONSTS)
                pe.wait_ge(S["proj_evac"], last_turn("vn" if layer else "v0", u) + 1)
                v = bufs(layer)["vt"]
                for k, tiles in enumerate(V_TILES):
                    t = T_TURN[s, k]
                    if t >= 2:
                        pe.wait_ge(S["tr_lo"], t - 1)
                    for j, tile in enumerate(tiles):
                        c0, _ = (0, META) if tile == 0 else (META + 128 * (tile - 1), 128)
                        ins = nc.tensor.transpose(TR[t % 2][:, 128 * j:128 * j + 128], v[:, c0:c0 + 128], eye[:, :])
                    ins.then_inc(S["tr_done"], 1)

            def scores(t, m, c):
                g, i, slot = TSTEPS[t]
                layer, kind, u, head, _ = GROUPS[g]
                q0, rows = query_cols(i)
                chunks = score_chunks(i)
                c0, w = chunks[c]
                if slot == 0 and m == 0 and c == 0 and g == unit_groups(layer, u)[0]:
                    pe.wait_ge(S["proj_evac"], last_turn("qn" if layer else "q0", u) + 1)
                b = S_CHUNK[t, m, c]
                if b >= SBANKS:
                    pe.wait_ge(S["s_free_" + S_OWNER[b - SBANKS]], S_FREED[b - SBANKS])
                dst = SC[b % SBANKS][:, 0:w]
                qc = slice(q0, q0 + 128)
                masked = c == len(chunks) - 1 and not (i == META_Q and kind == "A")
                if kind == "C":
                    prods = [(qh[:, a, qc], kh[:, u % 2, b_, c0:c0 + w]) for a, b_ in ((0, 0), (0, 1), (1, 0))]
                    prods += [(qpe[:, u % 2, a, qc], kpe[:, c0:c0 + w]) for a in (0, 1)]
                else:
                    j = m if kind == "A" else head
                    prods = [(qst[:, j, a, qc], kst[:, u % 2, j, c0:c0 + w]) for a in (0, 1)]
                for k, (l, r) in enumerate(prods):
                    ins = mm(dst, l, r, start=(k == 0), stop=(k == len(prods) - 1 and not masked))
                if masked:
                    dw = META if i == META_Q else 128
                    ins = mm(SC[b % SBANKS][:, w - dw:w], eyebf[:, :],
                             mask[:, 1 if kind == "B" else 0, 0:dw], start=False, stop=True)
                ins.then_inc(S["s_done"], 1)

            def turn_weights(g, k):
                layer, kind, u, head, blocks = GROUPS[g]
                weights = bufs(layer)["pb"]
                t = T_TURN[g, k]
                if k == 0:
                    pe.wait_ge(S["p_ready"], GROUP_STEPS[g][-1] + 1)
                if t >= 2:
                    pe.wait_ge(S["tr_lo"], t - 1)
                at = 0
                for tile in turns_of(blocks)[k]:
                    for slot, i in enumerate(blocks):
                        if i != META_Q and tile > i + 1:
                            continue
                        rows = META if i == META_Q else 128
                        k0, wide = (0, META) if tile == 0 else (META + 128 * (tile - 1), 128)
                        ins = nc.tensor.transpose(TR[t % 2][0:wide, at:at + rows],
                                                  weights[0:rows, g % 2, slot, k0:k0 + wide], eye[0:rows, 0:rows])
                        at += rows
                ins.then_inc(S["tr_done"], 1)

            def product(g, k):
                layer, kind, u, head, blocks = GROUPS[g]
                B = bufs(layer)
                turns = turns_of(blocks)
                w_all = META if blocks == [META_Q] else 256
                t, r = T_TURN[g, k], RING[g, k]
                pe.wait_ge(S["tr_lo"], t + 1)
                if k == 0 and g >= 1:
                    pe.wait_ge(S["o_evac"], g)
                at = 0
                for tile in turns[k]:
                    wide = w_all if (tile == 0 or tile <= blocks[0] + 1) else 128
                    o0 = w_all - wide
                    rows = META if tile == 0 else 128
                    v = B["vtok"]
                    if kind == "B":
                        prods = [(v[0:rows, u % 2, head, tile, :], 0), (v[0:rows, u % 2, head, tile, :], 1)]
                    else:
                        prods = [(v[0:rows, u % 2, a, tile, :], b_) for a, b_ in ((0, 0), (1, 0), (0, 1))]
                    final = k == len(turns) - 1 and tile == turns[k][-1]
                    for j, (l, h) in enumerate(prods):
                        ins = mm(PO[:, o0:o0 + wide], l, B["ring"][0:rows, r % NRING, h, at:at + wide],
                                 start=(k == 0 and tile == turns[0][0] and j == 0),
                                 stop=(final and j == len(prods) - 1))
                    at += wide
                ins.then_inc(S["pv_done"], 1)

            def out_block(s):
                _, layer, b = s
                n = O_AT[s]
                pe.wait_ge(S["w_ready"], WEIGHT_AT["y", n] + 1)
                if n in (0, NB + 1):
                    pe.wait_ge(S["w_ready"], WEIGHT_AT[("wo1" if layer else "wo0"), KD - 1] + 1)
                if n - (NB + 1) * layer >= 2:
                    pe.wait_ge(S["y_evac"], n - 1)
                elif n % 2 == 1:
                    pe.wait_ge(S["proj_evac"], (LAST1 if layer else LAST0) + 1)
                else:
                    for b_ in (-1, -2, -3):
                        x_ = len(S_OWNER) + b_ if layer else S_CHUNK[FIRST_C, 0, 0] + b_
                        pe.wait_ge(S["s_free_" + S_OWNER[x_]], S_FREED[x_])
                for half in range(2):
                    dst = out_bank(n, half)
                    for k in range(KD):
                        for a, c in ((0, 0), (0, 1), (1, 0)):
                            ins = mm(dst[:, :], wsp[:, SLOT["y", n], a, k, :], wok[:, c, k, 512 * half:512 * half + 512],
                                     start=(k == 0 and a == 0 and c == 0), stop=(k == KD - 1 and a == 1))
                ins.then_inc(S["y_done"], 1)

            def turn_h(s):
                _, layer, b = s
                n = O_AT[s]
                rows = META if b == META_Q else 128
                pe.wait_ge(S["h_ready"], n + 1)
                for k in range(2):
                    t = T_TURN[s, k]
                    pe.wait_ge(S["tr_lo"], t - 1)
                    for j in range(4):
                        ins = nc.tensor.transpose(TR[t % 2][:, 128 * j:128 * j + rows],
                                                  res[0:rows, n % 2, 128 * (4 * k + j):128 * (4 * k + j) + 128],
                                                  eye[0:rows, 0:rows])
                    ins.then_inc(S["tr_done"], 1)

            waiting = []
            ahead = None

            def advance(count):
                for _ in range(count):
                    next(ahead, None)

            for at, s in enumerate(PLAN):
                if FILL[at] and ahead is None:
                    ahead = project(FILL[at][0])
                if s[0] == "P":
                    if s[1] in NORMS:
                        norm_sum(s)
                    else:
                        for _ in ahead or project(s):
                            pass
                        ahead = None
                elif s[0] == "VT":
                    turn_v(s)
                elif s[0] == "S":
                    scores(*s[1:])
                elif s[0] == "T":
                    turn_weights(*s[1:])
                elif s[0] == "X":
                    product(*s[1:])
                elif s[0] == "O":
                    out_block(s)
                    if s[1] == 0:
                        if waiting:
                            turn_h(waiting.pop())
                        waiting.append(s)
                elif s[0] == "OT":
                    turn_h(waiting.pop())
                if FILL[at]:
                    advance(FILL[at][1])


def kernel(**inputs):
    import ml_dtypes
    import concourse.bacc as _bacc
    from concourse.bass_utils import run_bass_kernel_spmd as _run

    a = {k: np.asarray(v) for k, v in inputs.items()}

    def tiles(w):
        k = w.shape[0] // 128
        return w.reshape(k, 128, w.shape[1]).transpose(1, 0, 2).reshape(128, -1)

    h = np.concatenate([a["meta"], a["x"][0]], 0)
    ht = h.T.reshape(KD, 128, TOK).transpose(1, 0, 2)
    w_in = a["ev_w_in"][0]
    part = {"A": [0, 512, 1024, 1536], "B": [2048, 2560, 3072, 3584]}
    w0 = np.stack([np.stack([tiles(w_in[:, o + 128 * (u % 4):o + 128 * (u % 4) + 128])
                             for o in part["A" if u < A_UNITS else "B"]]) for u in range(UNITS)])
    w_od = a["od_w_in"][0]
    starts = [128 * j for j in range(QL_T + KVL_T)]
    w1 = [tiles(w_od[:, o:o + 128]) for o in starts]
    pe_cols = w_od[:, 768:832]
    w1.append(tiles(np.concatenate([pe_cols, pe_cols], 1)))
    w1 += [tiles(w_od[:, 832 + 128 * h_:960 + 128 * h_]) for h_ in range(HEADS)]
    w1 = np.stack(w1)
    wuq = a["od_w_uq"][0]
    wuq_n = np.stack([tiles(wuq[:, 192 * h_:192 * h_ + 128]) for h_ in range(HEADS)])
    wuq_r = np.stack([tiles(np.concatenate([wuq[:, 192 * h_ + 128:192 * h_ + 192] for h_ in (2 * j, 2 * j + 1)], 1))
                      for j in range(HEADS // 2)])
    wkv = a["od_w_ukv"][0]
    wukv = np.stack([np.stack([tiles(wkv[:, 256 * h_ + 128 * z:256 * h_ + 128 * z + 128]) for z in range(2)])
                     for h_ in range(HEADS)])
    wo0 = a["ev_w_out"][0].reshape(KD, 128, D).transpose(1, 0, 2)
    wo1 = a["od_w_out"][0].reshape(KD, 128, D).transpose(1, 0, 2)
    lam = np.stack([a["ev_lam_q1"][0], a["ev_lam_k1"][0], a["ev_lam_q2"][0], a["ev_lam_k2"][0]])[None]
    r, c = np.arange(128)[:, None], np.arange(TOK)[None, :]
    dist = -np.abs(128 * (NB - 1) + META + r - c).astype(np.float16)
    k = np.arange(128)[None, :]
    masks = np.stack([np.where((k // CHUNK) > (r // CHUNK), MASKED, 0.0), np.where(k >= r, MASKED, 0.0)], 1)\
        .astype(ml_dtypes.bfloat16)
    eyeb = np.eye(128).astype(ml_dtypes.bfloat16)
    inv = (np.float32(10000.0) ** (-np.arange(32, dtype=np.float32) / np.float32(32))).astype(np.float32)
    ang = np.arange(TOK, dtype=np.float32)[None, :] * inv[:, None]
    cos, sin = np.cos(ang), np.sin(ang)
    rope = np.stack([np.tile(cos, (4, 1)), np.tile(np.concatenate([-sin, sin], 0), (2, 1))], 1).astype(np.float32)
    arrays = dict(ht=ht, x=a["x"][0], meta=a["meta"], w0=w0, w1=w1, wuq_n=wuq_n, wuq_r=wuq_r, wukv=wukv,
                  wo0=wo0, wo1=wo1, lng=a["ln_g"], lnb=a["ln_b"], lam=lam, subln=a["ev_subln"].reshape(128, 1),
                  qnorm=a["od_q_norm"][0].reshape(QL_T, 128).T, kvnorm=a["od_kv_norm"][0].reshape(KVL_T, 128).T,
                  dist=dist, masks=masks, eyeb=eyeb, rope=rope)
    nc = _bacc.Bacc("TRN2", target_bir_lowering=False, num_devices=1)
    feed, args = {}, {}
    for name, v in arrays.items():
        v = np.ascontiguousarray(v)
        feed["in_" + name] = v
        args[name] = nc.dram_tensor("in_" + name, v.shape, mybir.dt.from_np(v.dtype), kind="ExternalInput").ap()
    args["out"] = nc.dram_tensor("out_0", (SEQ, D), F32, kind="ExternalOutput").ap()
    args["lam"] = args["lam"].to_broadcast([128, 4, DH])
    trunk_kernel(nc, **args)
    r_ = _run(nc, [feed], core_ids=[0])
    return r_.results[0]["out_0"].reshape(1, SEQ, D)
```

```python
import concourse.bass as bass
from concourse import mybir
from collections import namedtuple
from contextlib import ExitStack
import math
import numpy as np

F32 = mybir.dt.float32
F32R = mybir.dt.float32r
BF16 = mybir.dt.bfloat16
F16 = mybir.dt.float16
ALU = mybir.AluOpType
ACT = mybir.ActivationFunctionType
AX_X = mybir.AxisListType.X

META, SEQ, D = 16, 1024, 1024
TOK = META + SEQ
KD = D // 128
CHUNK = 64
CHUNKS = [(0, 352), (352, 344), (696, 344)]
X_PIECES = [(k0, c0, w) for c0, w in CHUNKS for k0 in (0, KD // 2)]
NB = SEQ // 128
A_UNITS, B_UNITS, HEADS = 4, 4, 8
UNITS = A_UNITS + B_UNITS
DH = 64
SCALE64 = DH ** -0.5
SLOPES = [2.0 ** (-8.0 * (h + 1) / A_UNITS) for h in range(A_UNITS)]
SCALE192 = 192 ** -0.5
LAM_INIT = 0.8 - 0.6 * math.exp(0.0)
ALPHA = 4.0 ** 0.25
LN_EPS, RMS_EPS = 1e-5, 1e-6
QL_T, KVL_T = 4, 2
MASKED = -1.0e30
NRING = 3
SCORE_BANKS = ((2, 3), (2, 3, 4))
TURN_BANKS = ((4, 5, 6), (5, 6), (5, 6))
META_Q = NB


def keys_of(i):
    return META if i == META_Q else META + 128 * (i + 1)


def score_chunks(i):
    n = keys_of(i)
    if n <= 512:
        return [(0, n)]
    if n <= 1024:
        return [(0, n // 2), (n // 2, n // 2)]
    return list(CHUNKS)


def query_cols(i):
    return (0, META) if i == META_Q else (META + 128 * i, 128)


def turns_of(blocks):
    if blocks == [META_Q]:
        return [[0]]
    top = blocks[-1] + 1
    return [[0]] + [[a, a + 1] for a in range(1, top, 2)]


def maps_of(kind):
    return 2 if kind == "A" else 1


def merged(*streams, later={}):
    placed = []
    for n, (steps, begin, end) in enumerate(streams):
        for k, step in enumerate(steps):
            placed.append((begin + (end - begin) * (k + 0.5 + later.get(step[0], 0)) / len(steps), n, k, step))
    return [p[3] for p in sorted(placed, key=lambda p: p[:3])]


def make_plan():
    plan = []
    groups = []
    windows = []
    tsteps = []

    def group_list(layer, u):
        x = [[2 * j, 2 * j + 1] for j in range(NB // 2)]
        if layer == 1:
            return [(1, "C", u, 0, b) for b in x]
        if u < A_UNITS:
            return [(0, "A", u, 0, b) for b in [[META_Q]] + x]
        up = [[META_Q]] + x
        return [(0, "B", u, m, b) for b in up for m in range(2)]

    def proj(kind, u):
        return [("P", kind, u, c) for c in range(len(CHUNKS))]

    def score_steps(gid):
        out, late = [], []
        for slot, i in enumerate(groups[gid][4]):
            t = len(tsteps)
            tsteps.append((gid, i, slot))
            for m in range(maps_of(groups[gid][1])):
                out += [("S", t, m, c) for c in range(len(score_chunks(i)))] + [("M", t, m), ("E", t, m)]
            out += late
            late = [("C", t)]
        return out, late

    def value_steps(gid):
        n = len(turns_of(groups[gid][4]))
        lag = len(TURN_BANKS[groups[gid][0]]) - 1
        out = []
        for k in range(n + lag):
            out += [("T", gid, k)] * (k < n) + [("X", gid, k - lag)] * (k >= lag)
        return out + [("Y", gid)]

    def between(a, b):
        return [step for pair in zip(a, b) for step in pair]

    def run_layer(layer, fills, q_next):
        before = None
        for u in range(UNITS):
            gl = group_list(layer, u)
            early, second, fill = fills(u)
            placed = 0
            for gi, g in enumerate(gl):
                gid = len(groups)
                groups.append(g)
                windows.append(WINDOWS[g[1]][gi])
                w = Window(*windows[-1])
                s_steps, s_late = score_steps(gid)
                v_steps = value_steps(before) if before is not None else []
                own = early if gi == 0 else second if gi == 1 else q_next(u) if gi == len(gl) - 1 else []
                upto = len(fill) if gi == len(gl) - 1 else min(len(fill), math.ceil(len(fill) * w.filled))
                plan.extend(merged((s_steps, w.s_from, w.s_to), (v_steps, w.v_from, w.v_to),
                                   (own, w.own_from, w.own_to), (fill[placed:upto], w.fill_from, w.fill_to),
                                   (s_late, w.last_c, max(w.last_c, 1.0)), later={"E": w.e_later, "C": w.c_later}))
                placed = max(placed, upto)
                before = gid
        plan.extend([("YL", layer, 0), ("YL", layer, 1)] + value_steps(before))

    plan.extend(proj("k0", 0) + proj("v0", 0) + proj("q0", 0)[:1] + [("VT", 0, 0)])

    def fills0(u):
        q_rest, gate = proj("q0", u)[1:], proj("g0", u)
        if u + 1 == UNITS:
            return q_rest, gate, [("WO", 0, k) for k in range(KD)]
        k, v = proj("k0", u + 1), proj("v0", u + 1) + [("VT", 0, u + 1)]
        if 1 <= u <= A_UNITS:
            norm = proj("rms0", u - 1)
            n = len(gate) if u == A_UNITS else 1
            return (q_rest + k[:1], [("SQ", u - 1)] + between(k[1:], norm) + [norm[2], ("F", u - 1)] + gate[:n], gate[n:] + v)
        return q_rest + k, gate, v

    run_layer(0, fills0, lambda u: proj("q0", u + 1)[:1] if u + 1 < UNITS else [])
    for b in [META_Q] + list(range(NB)):
        plan.append(("O", 0, b))
    plan.extend(proj("cq", 0)[:2])
    plan.append(("OT", 0))
    plan.extend(proj("cq", 0)[2:])
    for j in range(1, QL_T):
        plan.extend(proj("cq", j))
    for j in range(KVL_T):
        plan.extend(proj("ckv", j))
    plan.extend(proj("kpe", 0))
    norms = proj("ncq", 0) + proj("nckv", 0)
    gates = [step for h in range(HEADS) for step in proj("g1", h)]
    for n, step in enumerate(gates[:3 * len(norms)]):
        plan.append(step)
        if n % 3 == 2:
            plan.append(norms[n // 3])
    plan.extend(gates[3 * len(norms):] + proj("kn", 0) + proj("vn", 0))
    plan.extend([("P", "qr", 0, 0), ("P", "qn", 0, 0), ("VT", 1, 0)])

    def queries(u, chunks):
        qn = proj("qn", u)[chunks]
        return between(proj("qr", u)[chunks], qn) if u % 2 == 0 else qn

    def fills1(u):
        q_rest = queries(u, slice(1, None))
        if u + 1 == HEADS:
            return q_rest, [("L", u)], [("WO", 1, k) for k in range(KD)]
        return q_rest + proj("kn", u + 1), [("L", u)], proj("vn", u + 1) + [("VT", 1, u + 1)]

    run_layer(1, fills1, lambda u: queries(u + 1, slice(0, 1)) if u + 1 < HEADS else [])
    for b in range(NB):
        plan.append(("O", 1, b))
    return plan, groups, windows, tsteps


Window = namedtuple("Window", "s_from s_to v_from v_to own_from own_to fill_from fill_to last_c filled "
                              "c_share e_share e_later c_later")
WINDOWS = {"A": [[0.108, 0.931, 0.0, 1.0, 0.0, 0.99, 0.093, 1.0, 2.0, 0.0, 0.522, 1.999, 1.104, -1.901],
                 [0.0, 0.946, 0.82, 1.0, 0.0, 0.71, 0.72, 1.0, 2.0, 0.042, 1.49, 0.673, 0.107, -1.901],
                 [0.002, 0.856, 0.33, 1.0, 0.0, 0.99, 0.045, 1.0, 1.984, 0.274, 1.49, 0.453, 0.0, -1.112],
                 [0.002, 0.856, 0.312, 1.0, 0.0, 0.99, 0.0, 1.0, 1.983, 0.567, 1.49, 0.572, 0.18, -2.0],
                 [0.002, 0.357, 0.316, 1.0, 0.36, 0.375, 0.018, 0.411, 0.851, 1.0, 1.14, 0.453, 0.107, -0.744]],
           "B": [[0.269, 1.0, 0.0, 0.911, 0.007, 1.0, 0.459, 1.0, 1.893, 0.0, 0.879, 0.349, 0.09, 0.454],
                 [0.0, 0.999, 0.529, 1.0, 0.007, 1.0, 0.989, 1.0, 2.0, 0.0, 0.879, 0.0, 0.09, -0.019],
                 [0.0, 0.729, 0.514, 1.0, 0.223, 1.0, 0.472, 1.0, 1.984, 0.0, 0.879, 0.0, 0.09, 0.066],
                 [0.0, 0.729, 0.513, 1.0, 0.007, 1.0, 0.472, 1.0, 2.0, 0.016, 0.66, 0.0, 0.09, 0.054],
                 [0.0, 0.729, 0.382, 1.0, 0.0, 1.0, 0.472, 1.0, 2.0, 0.083, 1.049, 0.0, 1.113, -0.578],
                 [0.0, 0.796, 0.37, 1.0, 0.007, 0.888, 0.478, 1.0, 2.0, 0.221, 0.314, 0.303, 0.09, -0.019],
                 [0.0, 0.729, 0.489, 1.0, 0.007, 1.0, 0.472, 1.0, 1.909, 0.454, 0.66, 0.405, 0.09, -0.019],
                 [0.0, 0.729, 0.345, 1.0, 0.102, 1.0, 0.472, 1.0, 1.973, 0.539, 1.198, 1.136, 0.093, -0.019],
                 [0.0, 0.729, 0.333, 1.0, 0.007, 1.0, 0.401, 1.0, 2.0, 0.755, 0.879, 0.0, 0.09, -0.044],
                 [0.0, 0.702, 0.352, 0.896, 0.296, 0.495, 0.523, 0.828, 0.517, 0.922, 3.052, 0.232, 0.249, -0.019]],
           "C": [[0.0, 1.0, 0.087, 1.0, 0.0, 0.952, 0.011, 1.0, 1.66, 0.0, 1.993, 1.694, 0.306, -2.0],
                 [0.011, 1.0, 0.775, 1.0, 0.0, 0.78, 0.586, 1.0, 1.985, 0.258, 6.406, 0.173, 0.293, -0.131],
                 [0.0, 0.885, 0.055, 1.0, 0.025, 1.0, 0.0, 0.937, 2.0, 0.563, 1.374, 0.042, 0.602, 0.713],
                 [0.0, 0.395, 0.055, 1.0, 0.072, 0.302, 0.004, 0.612, 0.58, 1.0, 3.798, 0.042, 0.047, -0.25]]}


PLAN, GROUPS, GROUP_WINDOW, TSTEPS = make_plan()
NORMS = ("rms0", "ncq", "nckv")
KT_OF = {"q0": KD, "k0": KD, "v0": KD, "g0": KD, "cq": KD, "ckv": KD, "kpe": KD, "g1": KD,
         "kn": KVL_T, "vn": KVL_T, "qn": QL_T, "qr": QL_T}
PROJ = [s for s in PLAN if s[0] == "P"]
PTURN = {s: n for n, s in enumerate(PROJ)}
N_CONSTS = 7
TILES = []
for _s in PROJ:
    if _s[1] not in NORMS and _s[3] == 0:
        TILES.append(_s[1:3])
TILE_AT = {s: n for n, s in enumerate(TILES)}
_l0 = sum(1 for k, _ in TILES if k[1] == "0")
O_STEPS = [s for s in PLAN if s[0] == "O"]
O_AT = {s: n for n, s in enumerate(O_STEPS)}
WEIGHTS = TILES[:_l0] + [("wo0", k) for k in range(KD)] + [("y", n) for n in range(NB + 1)] \
    + TILES[_l0:] + [("wo1", k) for k in range(KD)] + [("y", n) for n in range(NB + 1, 2 * NB + 1)]
WEIGHT_AT = {s: n for n, s in enumerate(WEIGHTS)}
STATIONARY = [s for s in WEIGHTS if s[0] not in ("wo0", "wo1")]
SLOT = {s: n % 2 for n, s in enumerate(STATIONARY)}
NO_HI = ("v0", "vn", "cq", "ckv")


def chunk_of(i):
    q0, _ = query_cols(i)
    return next(c for c, (c0, w) in enumerate(CHUNKS) if q0 + 128 <= c0 + w)


LATENTS = ("ncq", "nckv")
TURN_BEFORE, TURN_BANK = {}, {}
_bank_turns = {}
for _s in PROJ:
    if _s[1] in LATENTS:
        TURN_BANK[_s] = 2 + _s[3]
    else:
        TURN_BANK[_s] = _bank_turns.get("rotation", 0) % 2
        _bank_turns["rotation"] = _bank_turns.get("rotation", 0) + 1
    TURN_BEFORE[_s] = _bank_turns.get(TURN_BANK[_s])
    _bank_turns[TURN_BANK[_s]] = PTURN[_s]


def count_before(items, good):
    out, n = {}, 0
    for s in items:
        n += bool(good(s))
        out[s] = n
    return out


Q_COPY = count_before(PROJ, lambda s: s[1] in ("q0", "qr"))
HI_COUNT = count_before(PROJ, lambda s: s[1] not in NO_HI)
S_CHUNK = {}
S_OWNER = []
for _s in PLAN:
    if _s[0] == "S":
        S_CHUNK[_s[1:]] = len(S_OWNER)
        S_OWNER.append("dve" if GROUPS[TSTEPS[_s[1]][0]][1] == "A" else "act")
S_FREED = [S_OWNER[:n + 1].count(S_OWNER[n]) for n in range(len(S_OWNER))]
MAPS_DONE = {}
STATS_DONE = {}
for _s in PLAN:
    if _s[0] == "E":
        _kind = GROUPS[TSTEPS[_s[1]][0]][1]
        if _kind == "A":
            MAPS_DONE[_s[1:]] = len(MAPS_DONE) + 1
        if _kind != "B":
            STATS_DONE[_s[1:]] = len(STATS_DONE) + 1
S_BANK, S_BEFORE, _had = [], [], {}
for _s in PLAN:
    if _s[0] == "S":
        _layer = GROUPS[TSTEPS[_s[1]][0]][0]
        _b = SCORE_BANKS[_layer][len(S_BANK) % len(SCORE_BANKS[_layer])]
        S_BEFORE.append(_had.get(_b))
        _had[_b] = len(S_BANK)
        S_BANK.append(_b)
T_TURN, RING, _t, _r = {}, {}, 0, 0
for _s in PLAN:
    if _s[0] == "VT":
        for _k in range(3):
            T_TURN[_s, _k] = _t
            _t += 1
    if _s[0] == "T":
        T_TURN[_s[1], _s[2]] = _t
        RING[_s[1], _s[2]] = _r
        _t, _r = _t + 1, _r + 1
    if _s[0] == "O" and _s[1] == 0:
        for _k in range(2):
            T_TURN[_s, _k] = _t
            _t += 1
T_BANK, T_BEFORE, _had = [], [], {}
for _s, _k in sorted(T_TURN, key=T_TURN.get):
    _layer = GROUPS[_s][0] if isinstance(_s, int) else 2 if _s[0] == "O" else _s[1]
    _b = TURN_BANKS[_layer][len(T_BANK) % len(TURN_BANKS[_layer])]
    T_BEFORE.append(_had.get(_b))
    _had[_b] = len(T_BANK)
    T_BANK.append(_b)
B_GROUPS = [g for g in range(len(GROUPS)) if GROUPS[g][1] == "B"]
GROUP_STEPS = {g: [t for t in range(len(TSTEPS)) if TSTEPS[t][0] == g] for g in range(len(GROUPS))}
P_OWNER = ["pool" if GROUPS[g][1] == "B" and slot == 0 and i != META_Q and GROUPS[g][2] < UNITS - 1 else "dve"
           for g, i, slot in TSTEPS]
P_COUNT = [P_OWNER[:t + 1].count(P_OWNER[t]) for t in range(len(TSTEPS))]
FIRST_C = min(t for t in range(len(TSTEPS)) if GROUPS[TSTEPS[t][0]][1] == "C")
LAST_T = {g: T_TURN[g, len(turns_of(GROUPS[g][4])) - 1] for g in range(len(GROUPS))}
V_TILES = [[0, 1, 2], [3, 4, 5], [6, 7, 8]]
STORES = [s for s in PLAN if s[0] == "F" or (s[0] == "Y" and GROUPS[s[1]][1] != "A")]
STORE_AT = {s: n for n, s in enumerate(STORES)}


def share(s):
    if s[0] in ("S", "T", "X"):
        return 1
    if s[0] in ("C", "E"):
        w = Window(*GROUP_WINDOW[TSTEPS[s[1]][0]])
        return w.c_share if s[0] == "C" else w.e_share
    return 0


def make_fill():
    fill = [None] * len(PLAN)
    start = 0
    for at, s in enumerate(PLAN):
        if s[0] == "O":
            start = at + 1
        if s[0] != "P":
            continue
        spots = [(n, share(PLAN[n])) for n in range(start, at) if share(PLAN[n])]
        if s[1] not in NORMS and spots:
            left, weight = 3 * KT_OF[s[1]] - 1, 1 + sum(w for _, w in spots)
            for n, w in spots:
                take = math.ceil(left * w / weight)
                fill[n] = (s, take)
                left -= take
                weight -= w
        start = at + 1
    return fill


FILL = make_fill()


def square_at(kind, c, j):
    return QL_T * c + j if kind == "ncq" else QL_T * len(CHUNKS) + KVL_T * c + j


def square_used(k):
    n_cq = QL_T * len(CHUNKS)
    kind, nt, c, j = ("ncq", QL_T, *divmod(k, QL_T)) if k < n_cq else ("nckv", KVL_T, *divmod(k - n_cq, KVL_T))
    if j == nt - 1:
        return "proj_done", PTURN[("P", kind, 0, c)] + 1
    before = c * (nt - 1) + (0 if kind == "ncq" else len(CHUNKS) * (QL_T - 1))
    return "lsq_used", before + j + 1


def unit_groups(layer, u):
    return [g for g in range(len(GROUPS)) if GROUPS[g][0] == layer and GROUPS[g][2] == u]


def q_scale(u):
    return SCALE64 / SLOPES[u] if u < A_UNITS else 1.0


def last_turn(kind, u):
    return PTURN[("P", kind, u, len(CHUNKS) - 1)]


def trunk_kernel(nc, ht, x, meta, w0, wo0, w1, wuq_n, wuq_r, wukv, wo1, lng, lnb, lam, subln,
                 qnorm, kvnorm, dist, masks, eyeb, rope, out):
    yd = nc.dram_tensor("y_scratch", (2, UNITS, 128, TOK), F32, kind="Internal").ap()
    gd = nc.dram_tensor("gate_scratch", (HEADS, 128, TOK), F32, kind="Internal").ap()
    hd = nc.dram_tensor("h1_scratch", (SEQ, D), F32, kind="Internal").ap()

    ctx = ExitStack()
    with ctx:
        def sem(name):
            return ctx.enter_context(nc.semaphore(name))

        def sb(name, shape, dt, where=ctx):
            return where.enter_context(nc.sbuf_tensor(name, shape, dt))

        big = sb("big", [128, 2, KD, TOK], F32R)
        wraw = sb("wraw", [128, 2, KD * 128], F32)
        wsp = sb("wsp", [128, 2, 2, KD, 128], F32R)
        eye = sb("eye", [128, 128], F32)
        ones = sb("ones", [128, 128], F32)
        eyebf = sb("eyebf", [128, 128], BF16)
        mask = sb("mask", [128, 2, 128], BF16)
        stat = sb("stat", [128, 4, 16], F32)
        small = sb("small", [128, 64], F32)
        lamv = sb("lamv", [128, 4, DH], F32)
        eps = sb("eps", [128, 2], F32)
        rmsg = sb("rmsg", [128, 8], F32)
        wok = big[:, :, :, 0:D]

        st = ExitStack()
        kst = sb("kst", [128, 2, 2, TOK], F32R, st)
        qst = sb("qst", [128, 2, 2, TOK], F32R, st)
        vt = sb("vt", [128, TOK], F32, st)
        gate = sb("gate", [128, TOK], F32, st)
        ot = sb("ot", [128, TOK], F32, st)
        sq = sb("sq", [128, TOK], F32, st)
        otmp = sb("otmp", [64, 256], F32, st)
        distt = sb("distt", [128, TOK], F16, st)
        st2 = ExitStack()
        xin = sb("xin", [128, KD, TOK], F32, st2)
        st2.close()
        vtok = sb("vtok", [128, 2, 2, 9, 128], F32R, st)
        ring = sb("ring", [128, NRING, 2, 512], F32R, st)
        tb = sb("tb", [128, 2, 2, TOK], F32, st)
        pb = sb("pb", [128, 2, 2, TOK], F32, st)
        st.close()
        st = ExitStack()
        h1t = sb("h1t", [128, 2, KD, TOK], F32R, st)
        st2 = ExitStack()
        xres = sb("xres", [128, 2, D], F32, st2)
        res = sb("res", [128, 2, D], F32, st2)
        lngb = sb("lngb", [128, 2, D], F32, st2)
        st2.close()
        st2 = ExitStack()
        lraw = sb("lraw", [128, QL_T + KVL_T, TOK], F32, st2)
        gtmp = sb("gtmp", [128, 2, TOK], F32, st2)
        st2.close()
        st.close()
        st = ExitStack()
        kh = sb("kh", [128, 2, 2, TOK], F32R, st)
        qh = sb("qh", [128, 2, TOK], F32R, st)
        qpe = sb("qpe", [128, 2, 2, TOK], F32R, st)
        vtok1 = sb("vtok1", [128, 2, 2, 9, 128], F32R, st)
        vt1 = sb("vt1", [128, TOK], F32, st)
        gate1 = sb("gate1", [128, TOK], F32, st)
        ot1 = sb("ot1", [128, TOK], F32, st)
        ring1 = sb("ring1", [128, NRING, 2, 512], F32R, st)
        pb1 = sb("pb1", [128, 2, 2, TOK], F32, st)
        ropet = sb("ropet", [128, 2, TOK], F32, st)
        kpe = sb("kpe", [128, TOK], F32R, st)
        rtmp = sb("rtmp", [128, 2, 352], F32, st)
        lsq = rtmp
        st.close()
        st = ExitStack()
        xres1 = sb("xres1", [128, 2, D], F32, st)
        res1 = sb("res1", [128, 2, D], F32, st)
        lngb1 = sb("lngb1", [128, 2, D], F32, st)
        st.close()

        bank = [ctx.enter_context(nc.psum_tensor(f"bank{n}", [128, 512], F32)) for n in range(8)]
        PO = bank[7]

        lat = {"ncq": (0, QL_T, 1), "nckv": (QL_T, KVL_T, 1 + QL_T)}
        L0T = dict(ring=ring, pb=pb, vtok=vtok, vt=vt, gate=gate, ot=ot)
        L1T = dict(ring=ring1, pb=pb1, vtok=vtok1, vt=vt1, gate=gate1, ot=ot1)

        def bufs(layer):
            return L1T if layer else L0T

        names = """consts const_pool x_in_0 x_in_1 x_in_2 x_in_3 x_in_4 x_in_5 x_hi x_split
            w_raw_0 w_raw_1 w_ready proj_done proj_hi proj_evac q_copied lat_sq lsq_used lat_split
            s_done s_free_dve s_free_act max_ready exp_done scanned p_ready_dve p_ready_pool
            tr_done tr_hi tr_lo pv_done o_tmp o_evac sq_done unit_done y_stored_0 y_stored_1
            g_stored_0 g_stored_1 g_loaded lam_exp rope_in lnp_in res_in_0 res_in_1
            y_done y_evac ln_stats ln_mid ln_rstd ln_norm ln_scaled h_ready h_stored_0 h_stored_1
            act_step dve_step pool_step""".split()
        S = {n: sem(n) for n in names}

        def out_bank(n, half):
            return bank[2 * ((n + 1) % 2) + half]

        def slot(name, n):
            return S[f"{name}_{n % 2}"]

        def arrived(eng, name, n):
            eng.wait_ge(slot(name, n), 16 * (n // 2 + 1))

        def all_arrived(eng, name, count):
            for n in range(max(count - 2, 0), count):
                arrived(eng, name, n)

        block = ctx.enter_context(nc.Block())
        lo_hi = lambda ap: ap.bitcast(F32)

        def rhs_of(kind):
            if kind in ("q0", "k0", "v0", "g0"):
                return big, 0
            if kind in ("cq", "ckv", "kpe", "g1"):
                return h1t, 0
            return (big, 0) if kind in ("qn", "qr") else (big, QL_T)

        def w_src(kind, u):
            if kind in ("q0", "k0", "v0", "g0"):
                return w0[u, "qkvg".index(kind[0])]
            if kind == "cq":
                return w1[u]
            if kind == "ckv":
                return w1[QL_T + u]
            if kind == "kpe":
                return w1[QL_T + KVL_T]
            if kind == "g1":
                return w1[QL_T + KVL_T + 1 + u]
            if kind == "qn":
                return wuq_n[u]
            if kind == "qr":
                return wuq_r[u // 2]
            return wukv[u, 0 if kind == "kn" else 1]

        LAST0 = last_turn("g0", UNITS - 1)
        LAST1 = last_turn("qn", HEADS - 1)

        def store_of(layer, b):
            blocks = [0, 1] if b == META_Q else [b // 2 * 2, b // 2 * 2 + 1]
            g = [g for g in unit_groups(layer, UNITS - 1) if GROUPS[g][4] == blocks][-1]
            return STORE_AT["Y", g]

        def group_cols(g):
            blocks = GROUPS[g][4]
            return (0, META) if blocks == [META_Q] else (META + 128 * blocks[0], 256)

        @block.sync
        def _(sp):
            def weights(upto):
                while issued[0] <= min(upto, len(WEIGHTS) - 1):
                    n = issued[0]
                    kind, u = WEIGHTS[n]
                    if n >= 2:
                        sp.wait_ge(S["w_ready"], n - 1)
                    if kind == "y":
                        _, layer, b = O_STEPS[u]
                        c0, _ = query_cols(b)
                        for k in (1, 0):
                            arrived(sp, "y_stored", store_of(layer, b) - k)
                        dst = wraw[:, n % 2, :].rearrange("p (k c) -> p k c", k=KD)
                        src = yd[layer, :, :, c0:c0 + 128].rearrange("u p c -> p u c")
                    elif kind in ("wo0", "wo1"):
                        dst, src = wraw[:, n % 2, :], (wo1 if kind == "wo1" else wo0)[:, u, :]
                    else:
                        dst, src = wraw[:, n % 2, 0:KT_OF[kind] * 128], w_src(kind, u)
                    sp.dma_start(dst, src).then_inc(slot("w_raw", n), 16)
                    issued[0] += 1

            issued = [0]
            weights(0)
            for n, (k0, c0, w) in enumerate(X_PIECES):
                sp.dma_start(xin[:, k0:k0 + KD // 2, c0:c0 + w], ht[:, k0:k0 + KD // 2, c0:c0 + w])\
                    .then_inc(S[f"x_in_{n}"], 16)
            sp.dma_start(eyebf[:, :], eyeb).then_inc(S["consts"], 16)
            sp.dma_start(mask[:, :, :], masks).then_inc(S["consts"], 16)
            sp.dma_start(distt[:, :], dist).then_inc(S["consts"], 16)
            sp.dma_start(lamv[:, :, :], lam).then_inc(S["consts"], 16)
            sp.dma_start(rmsg[:, 0:1], subln).then_inc(S["consts"], 16)
            sp.dma_start(rmsg[:, 1:5], qnorm).then_inc(S["consts"], 16)
            sp.dma_start(rmsg[:, 5:7], kvnorm).then_inc(S["consts"], 16)

            weights(1)
            for s in PLAN:
                if s[0] == "P":
                    if s[1] not in NORMS and s[3] == 0:
                        weights(WEIGHT_AT[s[1:3]] + 2)
                    if s == ("P", "cq", 0, 0):
                        sp.wait_ge(S["tr_lo"], T_TURN[("O", 0, NB - 1), 1] + 1)
                        all_arrived(sp, "h_stored", NB)
                        sp.dma_start(ropet[:, :, :], rope).then_inc(S["rope_in"], 16)
                    if s[1] == "g1" and s[3] == len(CHUNKS) - 1:
                        sp.wait_ge(S["proj_evac"], PTURN[s] + 1)
                        sp.dma_start(gd[s[2]], gtmp[:, s[2] % 2, :]).then_inc(slot("g_stored", s[2]), 16)
                if s in STORE_AT:
                    if s[0] == "F":
                        u = s[1]
                        sp.wait_ge(S["unit_done"], u + 1)
                        dst, src = yd[0, u], ot[:, :]
                    else:
                        layer, kind, u, head, _ = GROUPS[s[1]]
                        c0, w = group_cols(s[1])
                        rows = slice(DH * head, DH * head + DH) if kind == "B" else slice(0, 128)
                        sp.wait_ge(S["o_evac"], s[1] + 1)
                        dst, src = yd[layer, u, rows, c0:c0 + w], bufs(layer)["ot"][rows, c0:c0 + w]
                    sp.dma_start(dst, src).then_inc(slot("y_stored", STORE_AT[s]), 16)
                if s[0] == "L":
                    if s[1] == 0:
                        all_arrived(sp, "g_stored", HEADS)
                    else:
                        sp.wait_ge(S["o_evac"], unit_groups(1, s[1] - 1)[-1] + 1)
                    sp.dma_start(gate1[:, :], gd[s[1]]).then_inc(S["g_loaded"], 16)
                if s[0] == "YL":
                    weights(WEIGHT_AT["y", (NB + 1) * s[1] + s[2]])
                if s[0] == "WO":
                    weights(WEIGHT_AT[("wo1" if s[1] else "wo0"), s[2]])
                if s[0] == "O" and O_AT[s] in (0, NB + 1):
                    layer = s[1]
                    all_arrived(sp, "y_stored", STORE_AT["Y", unit_groups(layer, UNITS - 1)[-1]] + 1)
                    g_, b_ = (lngb1 if layer else lngb)[:, 0, :], (lngb1 if layer else lngb)[:, 1, :]
                    sp.dma_start(g_, lng[layer:layer + 1, :].to_broadcast([128, D])).then_inc(S["lnp_in"], 16)
                    sp.dma_start(b_, lnb[layer:layer + 1, :].to_broadcast([128, D])).then_inc(S["lnp_in"], 16)
                if s[0] == "O":
                    layer, b = s[1], s[2]
                    n = O_AT[s]
                    rows = META if b == META_Q else 128
                    xr = xres1 if layer else xres
                    weights(WEIGHT_AT["y", n] + 2)
                    if n - (NB + 1) * layer >= 2:
                        sp.wait_ge(S["y_evac"], n - 1)
                    if layer:
                        all_arrived(sp, "h_stored", NB)
                    src = (hd[128 * b:128 * b + 128, :] if layer else
                           meta[:, :] if b == META_Q else x[128 * b:128 * b + 128, :])
                    sp.dma_start(xr[0:rows, n % 2, :], src).then_inc(slot("res_in", n), 16)
            all_arrived(sp, "h_stored", 2 * NB)


        @block.gpsimd
        def _(pool):
            step = [0]

            def tick(ins):
                step[0] += 1
                ins.then_inc(S["pool_step"], 1)
                return step[0]

            nc.gpsimd.memset(ones[:, :], 1.0).then_inc(S["const_pool"], 1)
            nc.gpsimd.memset(eps[:, 0:1], RMS_EPS).then_inc(S["const_pool"], 1)
            nc.gpsimd.memset(eps[:, 1:2], LN_EPS).then_inc(S["const_pool"], 1)
            pool.wait_ge(S["pool_step"], tick(nc.gpsimd.memset(eye[:, :], 0.0)))
            nc.gpsimd.affine_select(out=eye[:, :], in_=eye[:, :], compare_op=ALU.not_equal, fill=1.0,
                                    base=0, pattern=[[-1, 128]], channel_multiplier=1)\
                .then_inc(S["const_pool"], 1)

            def split(hi, lo, raw):
                pool.wait_ge(S["pool_step"], tick(nc.gpsimd.tensor_scalar(hi, raw, 1.0, 1.0, ALU.mult, ALU.mult)))
                return nc.gpsimd.tensor_tensor(lo, raw, lo_hi(hi), ALU.subtract)

            def split_weights(upto):
                while split_[0] <= min(upto, len(WEIGHTS) - 1):
                    n = split_[0]
                    kind, u = WEIGHTS[n]
                    arrived(pool, "w_raw", n)
                    if kind in ("wo0", "wo1"):
                        if u == 0:
                            pool.wait_ge(S["proj_done"], (LAST1 if kind == "wo1" else LAST0) + 1)
                        split(wok[:, 0, u, :], wok[:, 1, u, :], wraw[:, n % 2, :]).then_inc(S["w_ready"], 1)
                    else:
                        kt, i = KT_OF.get(kind, KD), STATIONARY.index((kind, u))
                        if i >= 2:
                            before = STATIONARY[i - 2]
                            if before[0] == "y":
                                pool.wait_ge(S["y_done"], before[1] + 1)
                            else:
                                pool.wait_ge(S["proj_done"], last_turn(*before) + 1)
                        split(wsp[:, i % 2, 0, 0:kt, :], wsp[:, i % 2, 1, 0:kt, :],
                              wraw[:, n % 2, 0:kt * 128].rearrange("p (k c) -> p k c", k=kt)).then_inc(S["w_ready"], 1)
                    split_[0] += 1

            def copy_queries(s):
                _, kind, u, c = s
                c0, w = CHUNKS[c]
                cc = slice(c0, c0 + w)
                pool.wait_ge(S["proj_evac"], PTURN[s] + 1)
                pool.wait_ge(S["w_ready"], split_[0])
                q = qst if kind == "q0" else qpe
                for m in range(2):
                    a, b = (0, 64) if kind == "q0" or m == 0 else (64, 0)
                    ins = nc.gpsimd.tensor_scalar(q[b:b + 64, m, :, cc], lo_hi(q[a:a + 64, m, :, cc]), 1.0, 1.0,
                                                  ALU.mult, ALU.mult)
                    if m == 0:
                        pool.wait_ge(S["pool_step"], tick(ins))
                ins.then_inc(S["q_copied"], 1)
                pool.wait_ge(S["q_copied"], Q_COPY[s])

            split_ = [0]
            split_weights(0)
            for s in PLAN:
                if s[0] == "P" and s[1] not in NORMS and s[3] == 0:
                    split_weights(WEIGHT_AT[s[1:3]] + 1)
                if s[0] == "P" and s[1] in ("q0", "qr"):
                    copy_queries(s)
                if s[0] == "P" and s[1] in LATENTS:
                    (t0, nt, _), (c0, w) = lat[s[1]], CHUNKS[s[3]]
                    tiles, cc = slice(t0, t0 + nt), slice(c0, c0 + w)
                    pool.wait_ge(S["proj_evac"], PTURN[s] + 1)
                    split(big[:, 0, tiles, cc], big[:, 1, tiles, cc], lraw[:, tiles, cc]).then_inc(S["lat_split"], 1)
                if s[0] == "C" and P_OWNER[s[1]] == "pool":
                    t = s[1]
                    g, i, slot_ = TSTEPS[t]
                    n = keys_of(i)
                    pool.wait_ge(S["scanned"], P_COUNT[t])
                    nc.gpsimd.tensor_tensor(pb[:, g % 2, slot_, 0:n], pb[:, g % 2, slot_, 0:n],
                                            tb[:, t % 2, 1, 0:n], ALU.mult).then_inc(S["p_ready_pool"], 1)
                if s[0] == "WO":
                    split_weights(WEIGHT_AT[("wo1" if s[1] else "wo0"), s[2]])
                if s[0] == "YL":
                    split_weights(WEIGHT_AT["y", (NB + 1) * s[1] + s[2]])
                if s[0] == "O":
                    layer, b = s[1], s[2]
                    n = O_AT[s]
                    split_weights(WEIGHT_AT["y", n] + 2)
                    rs = res1 if layer else res
                    lg = lngb1 if layer else lngb
                    rows = META if b == META_Q else 128
                    pool.wait_ge(S["ln_scaled"], n + 1)
                    nc.gpsimd.tensor_tensor(rs[0:rows, n % 2, :], rs[0:rows, n % 2, :], lg[0:rows, 1, :],
                                            ALU.add).then_inc(S["h_ready"], 1)

        def p_ready(eng, t):
            eng.wait_ge(S["p_ready_" + P_OWNER[t]], P_COUNT[t])

        def p_free(eng, g):
            if g >= 2:
                eng.wait_ge(S["tr_done"], LAST_T[g - 2] + 1)

        def turn_extent(g, k):
            blocks = GROUPS[g][4]
            tiles = turns_of(blocks)[k]
            if blocks == [META_Q]:
                return META, META
            if tiles == [0]:
                return META, 256
            return 128, (384 if tiles[-1] == blocks[-1] + 1 else 512)

        def v_parts(s, k, part):
            _, layer, u = s
            tiles = V_TILES[k]
            a, b = tiles[0], tiles[-1] + 1
            src = bank[T_BANK[T_TURN[s, k]]][:, 0:384].rearrange("p (t d) -> p t d", t=3)
            v = bufs(layer)["vtok"]
            if layer == 1 or u < A_UNITS:
                return [(v[:, u % 2, part, a:b, :], v[:, u % 2, 0, a:b, :], src)]
            return [(v[:, u % 2, m, a:b, DH * part:DH * part + DH], v[:, u % 2, m, a:b, 0:DH],
                     src[:, :, DH * m:DH * m + DH]) for m in range(2)]

        @block.scalar
        def _(act):
            A = nc.scalar.activation

            def split_x():
                for n, (k0, c0, w) in enumerate(X_PIECES):
                    act.wait_ge(S[f"x_in_{n}"], 16)
                    ks = slice(k0, k0 + KD // 2)
                    A(big[:, 0, ks, c0:c0 + w], xin[:, ks, c0:c0 + w], ACT.Copy).then_inc(S["x_hi"], 1)

            def evacuate(s):
                _, kind, u, c = s
                if kind in NO_HI:
                    return
                turn = PTURN[s]
                c0, w = CHUNKS[c]
                cc = slice(c0, c0 + w)
                src = bank[TURN_BANK[s]]
                if kind in ("ncq", "nckv"):
                    t0, nt, _ = lat[kind]
                    if c == 0:
                        act.wait_ge(S["proj_evac"], last_turn(*(("cq", QL_T - 1) if kind == "ncq" else ("ckv", KVL_T - 1))) + 1)
                        act.wait_ge(S["proj_evac"], last_turn("kpe", 0) + 1)
                    for j in range(nt):
                        k = square_at(kind, c, j)
                        if k >= 2:
                            name, value = square_used(k - 2)
                            act.wait_ge(S[name], value)
                        A(lsq[:, k % 2, 0:w], lraw[:, t0 + j, cc], ACT.Square).then_inc(S["lat_sq"], 1)
                act.wait_ge(S["proj_done"], turn + 1)
                if kind == "k0":
                    for m in range(2):
                        ins = A(kst[0:64, u % 2, m, cc], src[64 * m:64 * m + 64, 0:w], ACT.Copy)
                elif kind == "q0":
                    for m in range(2):
                        ins = A(qst[0:64, m, 0, cc], src[64 * m:64 * m + 64, 0:w], ACT.Copy, scale=q_scale(u))
                elif kind == "g0":
                    if c == 0 and u >= 1:
                        if u - 1 < A_UNITS:
                            act.wait_ge(S["unit_done"], u)
                        else:
                            act.wait_ge(S["o_evac"], unit_groups(0, u - 1)[-1] + 1)
                    ins = A(gate[:, cc], src[:, 0:w], ACT.Sigmoid)
                elif kind == "g1":
                    if c == 0 and u >= 2:
                        arrived(act, "g_stored", u - 2)
                    ins = A(gtmp[:, u % 2, cc], src[:, 0:w], ACT.Sigmoid)
                elif kind == "rms0":
                    ins = A(sq[:, cc], src[:, 0:w], ACT.Sqrt, bias=eps[:, 0:1], scale=1.0 / 128)
                elif kind in ("ncq", "nckv"):
                    ins = A(src[:, 0:w], src[:, 0:w], ACT.Sqrt, bias=eps[:, 0:1], scale=1.0 / (128 * lat[kind][1]))
                elif kind in ("kpe", "qr"):
                    if turn >= 1:
                        act.wait_ge(S["proj_evac"], turn)
                    for z in range(4):
                        a = 32 * (z ^ 1)
                        ins = A(rtmp[32 * z:32 * z + 32, 0, 0:w], src[a:a + 32, 0:w], ACT.Copy)
                elif kind == "kn":
                    ins = A(kh[:, u % 2, 0, cc], src[:, 0:w], ACT.Copy)
                elif kind == "qn":
                    ins = A(qh[:, 0, cc], src[:, 0:w], ACT.Copy)
                ins.then_inc(S["proj_hi"], 1)

            def turned_v(s):
                _, layer, u = s
                for k in range(3):
                    if k == 0 and u >= 2:
                        g = unit_groups(layer, u - 2)[-1]
                        act.wait_ge(S["pv_done"], RING[g, len(turns_of(GROUPS[g][4])) - 1] + 1)
                    act.wait_ge(S["tr_done"], T_TURN[s, k] + 1)
                    for dst, _, src in v_parts(s, k, 0):
                        ins = A(dst, src, ACT.Copy)
                    ins.then_inc(S["tr_hi"], 1)

            def sigmoids(t, c):
                g, i, slot = TSTEPS[t]
                if GROUPS[g][1] != "B":
                    return
                rows = META if i == META_Q else 128
                c0, w = score_chunks(i)[c]
                if c == 0 and t >= 2:
                    p_ready(act, t - 2)
                b = S_CHUNK[t, 0, c]
                act.wait_ge(S["s_done"], b + 1)
                src = bank[S_BANK[b]][0:rows, 0:w]
                A(tb[0:rows, t % 2, 0, c0:c0 + w], src, ACT.Sigmoid, scale=-SCALE64)
                A(tb[0:rows, t % 2, 1, c0:c0 + w], src, ACT.Sigmoid, scale=SCALE64).then_inc(S["s_free_act"], 1)

            def exps(t, m):
                g, i, slot = TSTEPS[t]
                layer, kind, u, head, _ = GROUPS[g]
                if kind == "B":
                    return
                n = keys_of(i)
                rows = META if i == META_Q else 128
                st_ = lambda a, b: stat[0:rows, t % 4, a:b]
                if kind == "C":
                    if t == FIRST_C:
                        all_arrived(act, "g_stored", HEADS)
                    p_free(act, g)
                act.wait_ge(S["max_ready"], STATS_DONE[t, m])
                if kind == "A":
                    A(tb[0:rows, t % 2, m, 0:n], tb[0:rows, t % 2, m, 0:n], ACT.Exp, bias=st_(6 + m, 7 + m),
                      scale=SLOPES[u], accum_out=st_(8 + m, 9 + m)).then_inc(S["exp_done"], 1)
                    return
                for c, (c0, w) in enumerate(score_chunks(i)):
                    b = S_CHUNK[t, 0, c]
                    A(pb1[:, g % 2, slot, c0:c0 + w], bank[S_BANK[b]][:, 0:w], ACT.Exp, bias=st_(6, 7),
                      scale=SCALE192, accum_out=st_(8 + c, 9 + c)).then_inc(S["s_free_act"], 1)

            def turned_weights(g, k):
                R = bufs(GROUPS[g][0])["ring"]
                t, r = T_TURN[g, k], RING[g, k]
                rows, w = turn_extent(g, k)
                if r >= NRING:
                    act.wait_ge(S["pv_done"], r - NRING + 1)
                act.wait_ge(S["tr_done"], t + 1)
                A(R[0:rows, r % NRING, 0, 0:w], bank[T_BANK[t]][0:rows, 0:w], ACT.Copy).then_inc(S["tr_hi"], 1)

            def output(g):
                _, kind, _, _, blocks = GROUPS[g]
                if kind != "B":
                    return
                w = META if blocks == [META_Q] else 256
                act.wait_ge(S["pv_done"], RING[g, len(turns_of(blocks)) - 1] + 1)
                act.wait_ge(S["o_evac"], g)
                A(otmp[:, 0:w], PO[64:128, 0:w], ACT.Copy).then_inc(S["o_tmp"], 1)

            def norm_block(s):
                _, layer, b = s
                n = O_AT[s]
                rows = META if b == META_Q else 128
                o = 32 * (n % 2)
                rs = res1 if layer else res
                act.wait_ge(S["ln_stats"], n + 1)
                A(small[0:rows, o + 14:o + 15], small[0:rows, o + 13:o + 14], ACT.Sqrt, bias=eps[0:rows, 1:2])\
                    .then_inc(S["ln_mid"], 1)
                act.wait_ge(S["ln_rstd"], n + 1)
                A(rs[0:rows, n % 2, :], rs[0:rows, n % 2, :], ACT.Identity, scale=small[0:rows, o + 15:o + 16],
                  bias=small[0:rows, o + 16:o + 17]).then_inc(S["ln_norm"], 1)

            def store_block(s):
                _, layer, b = s
                if b == META_Q:
                    return
                n = O_AT[s]
                act.wait_ge(S["h_ready"], n + 1)
                dst = out if layer else hd
                act.dma_start(dst[128 * b:128 * b + 128, :], (res1 if layer else res)[:, n % 2, :])\
                    .then_inc(slot("h_stored", NB * layer + b), 16)

            def turned_h(s):
                b = s[2]
                c0, w = query_cols(b)
                for k in range(2):
                    t = T_TURN[s, k]
                    act.wait_ge(S["tr_done"], t + 1)
                    A(h1t[:, 0, 4 * k:4 * k + 4, c0:c0 + w],
                      bank[T_BANK[t]][:, :].rearrange("p (j c) -> p j c", j=4)[:, :, 0:w], ACT.Copy).then_inc(S["tr_hi"], 1)

            act.wait_ge(S["const_pool"], 4)
            split_x()
            act.wait_ge(S["lam_exp"], 1)
            A(small[:, 60:62], small[:, 62:64], ACT.Exp).then_inc(S["act_step"], 1)
            last = None
            for s in PLAN:
                if s[0] == "P":
                    evacuate(s)
                elif s[0] == "VT":
                    turned_v(s)
                elif s[0] == "S":
                    sigmoids(s[1], s[3])
                elif s[0] == "E":
                    exps(*s[1:])
                elif s[0] == "T":
                    turned_weights(*s[1:])
                elif s[0] == "Y":
                    output(s[1])
                elif s[0] == "SQ":
                    act.wait_ge(S["o_evac"], unit_groups(0, s[1])[-1] + 1)
                    if s[1] >= 1:
                        act.wait_ge(S["proj_evac"], last_turn("rms0", s[1] - 1) + 1)
                    A(sq[:, :], ot[:, :], ACT.Square).then_inc(S["sq_done"], 1)
                elif s[0] == "O":
                    norm_block(s)
                    if last is not None:
                        store_block(last)
                        if s[1] == 0:
                            turned_h(last)
                    last = s
                elif s[0] == "OT":
                    store_block(last)
                    turned_h(last)
                    last = None
            store_block(last)

        @block.vector
        def _(dve):
            V = nc.vector
            step = [0]

            def then(ins):
                step[0] += 1
                ins.then_inc(S["dve_step"], 1)
                dve.wait_ge(S["dve_step"], step[0])

            def constants():
                dve.wait_ge(S["consts"], 16 * N_CONSTS)
                for j in range(2):
                    then(V.tensor_tensor_reduce(out=lamv[:, 2 * j, :], in0=lamv[:, 2 * j, :], in1=lamv[:, 2 * j + 1, :],
                                                scale=1.0, scalar=0.0, op0=ALU.mult, op1=ALU.add,
                                                accum_out=small[:, 62 + j:63 + j]))
                then(V.tensor_scalar(rmsg[:, 0:1], rmsg[:, 0:1], 1.0 - LAM_INIT, None, ALU.mult))
                V.tensor_scalar(rmsg[:, 7:8], rmsg[:, 0:1], 0.0, None, ALU.mult).then_inc(S["lam_exp"], 1)

            def negative_lambda():
                dve.wait_ge(S["act_step"], 1)
                then(V.tensor_tensor(small[:, 58:59], small[:, 61:62], small[:, 60:61], ALU.subtract))
                then(V.tensor_scalar(small[:, 59:60], small[:, 58:59], -LAM_INIT, None, ALU.add))

            def split_x():
                for n, (k0, c0, w) in enumerate(X_PIECES):
                    dve.wait_ge(S["x_hi"], n + 1)
                    ks = slice(k0, k0 + KD // 2)
                    V.tensor_tensor(big[:, 1, ks, c0:c0 + w], xin[:, ks, c0:c0 + w], lo_hi(big[:, 0, ks, c0:c0 + w]),
                                    ALU.subtract).then_inc(S["x_split"], 1)

            def rotate(s, cc, w):
                src = bank[TURN_BANK[s]][:, 0:w]
                dve.wait_ge(S["rope_in"], 16)
                V.tensor_tensor(rtmp[:, 1, 0:w], src, ropet[:, 0, cc], ALU.mult)
                then(V.tensor_tensor(rtmp[:, 0, 0:w], rtmp[:, 0, 0:w], ropet[:, 1, cc], ALU.mult))
                then(V.tensor_tensor(rtmp[:, 1, 0:w], rtmp[:, 0, 0:w], rtmp[:, 1, 0:w], ALU.add))

            def evacuate(s):
                _, kind, u, c = s
                turn = PTURN[s]
                c0, w = CHUNKS[c]
                cc = slice(c0, c0 + w)
                src = bank[TURN_BANK[s]]
                if kind in NO_HI:
                    dve.wait_ge(S["proj_done"], turn + 1)
                else:
                    dve.wait_ge(S["proj_hi"], HI_COUNT[s])
                if kind == "k0":
                    for m in range(2):
                        ins = V.tensor_tensor(kst[64:128, u % 2, m, cc], src[64 * m:64 * m + 64, 0:w],
                                              lo_hi(kst[0:64, u % 2, m, cc]), ALU.subtract)
                elif kind == "q0":
                    for m in range(2):
                        ins = V.scalar_tensor_tensor(
                            out=qst[0:64, m, 1, cc], in0=src[64 * m:64 * m + 64, 0:w],
                            scalar=q_scale(u), in1=lo_hi(qst[0:64, m, 0, cc]), op0=ALU.mult, op1=ALU.subtract)
                elif kind in ("v0", "vn"):
                    ins = V.tensor_copy((vt1 if kind == "vn" else vt)[:, cc], src[:, 0:w])
                elif kind == "g0":
                    ins = V.tensor_tensor(gate[:, cc], src[:, 0:w], gate[:, cc], ALU.mult)
                elif kind == "g1":
                    ins = V.tensor_tensor(gtmp[:, u % 2, cc], src[:, 0:w], gtmp[:, u % 2, cc], ALU.mult)
                elif kind == "rms0":
                    then(V.reciprocal(sq[:, cc], sq[:, cc]))
                    ins = V.scalar_tensor_tensor(out=ot[:, cc], in0=ot[:, cc], scalar=rmsg[:, 0:1], in1=sq[:, cc],
                                                 op0=ALU.mult, op1=ALU.mult)
                elif kind in ("cq", "ckv"):
                    if (kind, u, c) == ("cq", 1, 0):
                        all_arrived(dve, "h_stored", NB)
                    ins = V.tensor_copy(lraw[:, u + (QL_T if kind == "ckv" else 0), cc], src[:, 0:w])
                elif kind in ("ncq", "nckv"):
                    t0, nt, gain = lat[kind]
                    then(V.reciprocal(src[:, 0:w], src[:, 0:w]))
                    for j in range(t0, t0 + nt):
                        ins = V.scalar_tensor_tensor(out=lraw[:, j, cc], in0=lraw[:, j, cc],
                                                     scalar=rmsg[:, 1 + j:2 + j], in1=src[:, 0:w],
                                                     op0=ALU.mult, op1=ALU.mult)
                elif kind == "kpe":
                    rotate(s, cc, w)
                    then(V.tensor_copy(kpe[:, cc], rtmp[:, 1, 0:w]))
                    ins = V.tensor_tensor(kpe[64:128, cc], rtmp[64:128, 1, 0:w], lo_hi(kpe[64:128, cc]), ALU.subtract)
                elif kind == "qr":
                    rotate(s, cc, w)
                    for h in range(2):
                        rows = slice(64 * h, 64 * h + 64)
                        last = V.tensor_copy(qpe[rows, h, 0, cc], rtmp[rows, 1, 0:w])
                    then(last)
                    for h in range(2):
                        rows = slice(64 * h, 64 * h + 64)
                        ins = V.tensor_tensor(qpe[rows, h, 1, cc], rtmp[rows, 1, 0:w], lo_hi(qpe[rows, h, 0, cc]),
                                              ALU.subtract)
                elif kind == "kn":
                    ins = V.tensor_tensor(kh[:, u % 2, 1, cc], src[:, 0:w], lo_hi(kh[:, u % 2, 0, cc]), ALU.subtract)
                elif kind == "qn":
                    ins = V.tensor_tensor(qh[:, 1, cc], src[:, 0:w], lo_hi(qh[:, 0, cc]), ALU.subtract)
                ins.then_inc(S["proj_evac"], 1)

            def turned_v(s):
                for k in range(3):
                    dve.wait_ge(S["tr_hi"], T_TURN[s, k] + 1)
                    for dst, hi, src in v_parts(s, k, 1):
                        ins = V.tensor_tensor(dst, src, lo_hi(hi), ALU.subtract)
                    ins.then_inc(S["tr_lo"], 1)

            def scores(t, m, c):
                g, i, slot = TSTEPS[t]
                kind = GROUPS[g][1]
                if kind == "B":
                    return
                rows = META if i == META_Q else 128
                mx = stat[0:rows, t % 4, 3 * m + c:3 * m + c + 1]
                chunks = score_chunks(i)
                c0, w = chunks[c]
                b = S_CHUNK[t, m, c]
                dve.wait_ge(S["s_done"], b + 1)
                src = bank[S_BANK[b]][0:rows, 0:w]
                if kind == "A":
                    if m == 0 and c == 0 and t >= 2:
                        p_ready(dve, t - 2)
                    d0 = 128 * (NB - 1) + META if i == META_Q else 128 * (NB - 1 - i)
                    V.tensor_tensor_reduce(out=tb[0:rows, t % 2, m, c0:c0 + w], in0=src,
                                           in1=distt[0:rows, d0 + c0:d0 + c0 + w], scale=1.0, scalar=-3.0e38,
                                           op0=ALU.add, op1=ALU.max, accum_out=mx).then_inc(S["s_free_dve"], 1)
                else:
                    step[0] += 1
                    V.reduce_max(mx, src, AX_X).then_inc(S["dve_step"], 1)

            def maxima(t, m):
                g, i, slot = TSTEPS[t]
                layer, kind, u, head, _ = GROUPS[g]
                if kind == "B":
                    return
                rows = META if i == META_Q else 128
                n = len(score_chunks(i))
                st_ = lambda a, b: stat[0:rows, t % 4, a:b]
                if kind == "A":
                    dve.wait_ge(S["s_free_dve"], S_FREED[S_CHUNK[t, m, n - 1]])
                else:
                    dve.wait_ge(S["dve_step"], step[0])
                nm, mx = st_(6 + m, 7 + m), st_(3 * m, 3 * m + 1)
                factor = SLOPES[u] if kind == "A" else SCALE192
                if n > 1:
                    mx = st_(3 * m, 3 * m + n)
                    V.tensor_tensor_reduce(out=mx, in0=mx, in1=mx, scale=-0.5 * factor, scalar=3.0e38, op0=ALU.add,
                                           op1=ALU.min, accum_out=nm).then_inc(S["max_ready"], 1)
                else:
                    V.tensor_scalar(nm, mx, -factor, None, ALU.mult).then_inc(S["max_ready"], 1)

            def weights(t):
                g, i, slot = TSTEPS[t]
                layer, kind, u, head, _ = GROUPS[g]
                n = keys_of(i)
                rows = META if i == META_Q else 128
                st_ = lambda a, b: stat[0:rows, t % 4, a:b]
                P = bufs(layer)["pb"][0:rows, g % 2, slot, :]
                chunks = score_chunks(i)
                if kind != "C":
                    p_free(dve, g)
                if kind == "A":
                    dve.wait_ge(S["exp_done"], MAPS_DONE[t, 1])
                    then(V.reciprocal(st_(12, 14), st_(8, 10)))
                    V.tensor_scalar(P[:, 0:n], tb[0:rows, t % 2, 0, 0:n], st_(12, 13), None, ALU.mult)
                    then(V.tensor_scalar(st_(14, 15), st_(13, 14), small[0:rows, 59:60], None, ALU.mult))
                    V.scalar_tensor_tensor(out=P[:, 0:n], in0=tb[0:rows, t % 2, 1, 0:n], scalar=st_(14, 15), in1=P[:, 0:n],
                                           op0=ALU.mult, op1=ALU.add).then_inc(S["p_ready_dve"], 1)
                elif kind == "B":
                    dve.wait_ge(S["s_free_act"], S_FREED[S_CHUNK[t, 0, len(chunks) - 1]])
                    skip = tb[0:rows, t % 2, 0, :]
                    V.memset(P[:, n - 1:n], 1.0)
                    scan = V.tensor_tensor_scan(P[:, 0:n - 1][:, ::-1], skip[:, 1:n][:, ::-1], skip[:, 1:n][:, ::-1], 1.0,
                                                ALU.mult, ALU.bypass)
                    if P_OWNER[t] == "pool":
                        scan.then_inc(S["scanned"], 1)
                        return
                    then(scan)
                    V.tensor_tensor(P[:, 0:n], P[:, 0:n], tb[0:rows, t % 2, 1, 0:n], ALU.mult)\
                        .then_inc(S["p_ready_dve"], 1)
                else:
                    dve.wait_ge(S["s_free_act"], S_FREED[S_CHUNK[t, 0, len(chunks) - 1]])
                    if len(chunks) > 1:
                        then(V.reduce_sum(st_(12, 13), st_(8, 8 + len(chunks)), AX_X))
                        then(V.reciprocal(st_(13, 14), st_(12, 13)))
                    else:
                        then(V.reciprocal(st_(13, 14), st_(8, 9)))
                    V.tensor_scalar(P[:, 0:n], P[:, 0:n], st_(13, 14), None, ALU.mult).then_inc(S["p_ready_dve"], 1)

            def turned_weights(g, k):
                R = bufs(GROUPS[g][0])["ring"]
                t, r = T_TURN[g, k], RING[g, k]
                rows, w = turn_extent(g, k)
                dve.wait_ge(S["tr_hi"], t + 1)
                V.tensor_tensor(R[0:rows, r % NRING, 1, 0:w], bank[T_BANK[t]][0:rows, 0:w],
                                lo_hi(R[0:rows, r % NRING, 0, 0:w]), ALU.subtract).then_inc(S["tr_lo"], 1)

            def output(g):
                layer, kind, u, head, blocks = GROUPS[g]
                B = bufs(layer)
                c0, w = group_cols(g)
                O = B["ot"]
                if kind == "A":
                    if u >= 1 and g == unit_groups(0, u)[0]:
                        arrived(dve, "y_stored", STORE_AT["F", u - 1])
                    dve.wait_ge(S["pv_done"], RING[g, len(turns_of(blocks)) - 1] + 1)
                    V.tensor_copy(O[:, c0:c0 + w], PO[:, 0:w]).then_inc(S["o_evac"], 1)
                    return
                n = STORE_AT["Y", g]
                arrived(dve, "y_stored", n - 2)
                if kind == "B":
                    if g == unit_groups(0, A_UNITS)[0]:
                        arrived(dve, "y_stored", STORE_AT["F", A_UNITS - 1])
                    rows = slice(DH * head, DH * head + DH)
                    dve.wait_ge(S["o_tmp"], B_GROUPS.index(g) + 1)
                    then(V.tensor_tensor(O[rows, c0:c0 + w], PO[0:64, 0:w], otmp[:, 0:w], ALU.add))
                    V.tensor_tensor(O[rows, c0:c0 + w], O[rows, c0:c0 + w], gate[rows, c0:c0 + w], ALU.mult)\
                        .then_inc(S["o_evac"], 1)
                else:
                    dve.wait_ge(S["g_loaded"], 16 * (u + 1))
                    dve.wait_ge(S["pv_done"], RING[g, len(turns_of(blocks)) - 1] + 1)
                    V.tensor_tensor(O[:, c0:c0 + w], PO[:, 0:w], gate1[:, c0:c0 + w], ALU.mult).then_inc(S["o_evac"], 1)

            def gated(s):
                u = s[1]
                dve.wait_ge(S["proj_evac"], last_turn("rms0", u) + 1)
                V.tensor_tensor(ot[:, :], ot[:, :], gate[:, :], ALU.mult).then_inc(S["unit_done"], 1)

            def norm_block(s):
                _, layer, b = s
                n = O_AT[s]
                rows = META if b == META_Q else 128
                o = 32 * (n % 2)
                rs, xr, lg = (res1, xres1, lngb1) if layer else (res, xres, lngb)
                arrived(dve, "res_in", n)
                dve.wait_ge(S["y_done"], n + 1)
                if n - (NB + 1) * layer >= 2:
                    before = O_STEPS[n - 2]
                    if before[2] != META_Q:
                        arrived(dve, "h_stored", NB * layer + before[2])
                    if layer == 0:
                        dve.wait_ge(S["tr_done"], T_TURN[before, 1] + 1)
                for half in range(2):
                    hs = slice(512 * half, 512 * half + 512)
                    ins = V.scalar_tensor_tensor(out=rs[0:rows, n % 2, hs], in0=xr[0:rows, n % 2, hs], scalar=ALPHA,
                                                 in1=out_bank(n, half)[0:rows, :], op0=ALU.mult, op1=ALU.add)
                ins.then_inc(S["y_evac"], 1)
                dve.wait_ge(S["y_evac"], n + 1)
                for half in range(2):
                    ins = V.bn_stats(small[0:rows, o + 6 * half:o + 6 * half + 6], rs[0:rows, n % 2, 512 * half:512 * half + 512])
                then(ins)
                V.bn_aggr(small[0:rows, o + 12:o + 14], small[0:rows, o:o + 12]).then_inc(S["ln_stats"], 1)
                dve.wait_ge(S["ln_mid"], n + 1)
                then(V.reciprocal(small[0:rows, o + 15:o + 16], small[0:rows, o + 14:o + 15]))
                V.scalar_tensor_tensor(out=small[0:rows, o + 16:o + 17], in0=small[0:rows, o + 12:o + 13], scalar=-1.0,
                                       in1=small[0:rows, o + 15:o + 16], op0=ALU.mult, op1=ALU.mult).then_inc(S["ln_rstd"], 1)
                dve.wait_ge(S["ln_norm"], n + 1)
                dve.wait_ge(S["lnp_in"], 32 * (layer + 1))
                V.tensor_tensor(rs[0:rows, n % 2, :], rs[0:rows, n % 2, :], lg[0:rows, 0, :], ALU.mult)\
                    .then_inc(S["ln_scaled"], 1)

            def turned_h(s):
                b = s[2]
                c0, w = query_cols(b)
                for k in range(2):
                    t = T_TURN[s, k]
                    dve.wait_ge(S["tr_hi"], t + 1)
                    V.tensor_tensor(h1t[:, 1, 4 * k:4 * k + 4, c0:c0 + w],
                                    bank[T_BANK[t]][:, :].rearrange("p (j c) -> p j c", j=4)[:, :, 0:w],
                                    lo_hi(h1t[:, 0, 4 * k:4 * k + 4, c0:c0 + w]), ALU.subtract).then_inc(S["tr_lo"], 1)

            split_x()
            constants()
            negative_lambda()
            last = None
            for s in PLAN:
                if s[0] == "P":
                    evacuate(s)
                elif s[0] == "VT":
                    turned_v(s)
                elif s[0] == "S":
                    scores(*s[1:])
                elif s[0] == "M":
                    maxima(*s[1:])
                elif s[0] == "C":
                    weights(s[1])
                elif s[0] == "T":
                    turned_weights(*s[1:])
                elif s[0] == "Y":
                    output(s[1])
                elif s[0] == "F":
                    gated(s)
                elif s[0] == "O":
                    norm_block(s)
                    if s[1] == 0 and last is not None:
                        turned_h(last)
                    last = s
                elif s[0] == "OT":
                    turned_h(last)
                    last = None

        @block.tensor
        def _(pe):
            mm = nc.tensor.matmul

            def project(s):
                _, kind, u, c = s
                turn = PTURN[s]
                kt = KT_OF[kind]
                c0, w = CHUNKS[c]
                rhs, k0 = rhs_of(kind)
                if c == 0:
                    pe.wait_ge(S["w_ready"], WEIGHT_AT[kind, u] + 1)
                if kind == "cq" and u == 0:
                    pe.wait_ge(S["tr_lo"], T_TURN[("O", 0, (c0 + w - 1 - META) // 128), 1] + 1)
                if TURN_BEFORE[s] is not None:
                    pe.wait_ge(S["proj_evac"], TURN_BEFORE[s] + 1)
                if (kind, u, c) == ("cq", 0, 0):
                    pe.wait_ge(S["y_evac"], NB)
                if (kind, u, c) == ("kn", 0, 0):
                    pe.wait_ge(S["lat_split"], 2 * len(CHUNKS))
                dst = bank[TURN_BANK[s]][:, 0:w]
                for k in range(kt):
                    if turn < len(CHUNKS) and k % (KD // 2) == 0:
                        pe.wait_ge(S["x_split"], 2 * turn + k // (KD // 2) + 1)
                    for a, b in ((0, 0), (0, 1), (1, 0)):
                        last = k == kt - 1 and a == 1
                        ins = mm(dst, wsp[:, SLOT[kind, u], a, k, :], rhs[:, b, k0 + k, c0:c0 + w],
                                 start=(k == 0 and a == 0 and b == 0), stop=last)
                        if last:
                            ins.then_inc(S["proj_done"], 1)
                        else:
                            yield

            def norm_sum(s):
                _, kind, u, c = s
                turn = PTURN[s]
                c0, w = CHUNKS[c]
                if TURN_BEFORE[s] is not None:
                    pe.wait_ge(S["proj_evac"], TURN_BEFORE[s] + 1)
                dst = bank[TURN_BANK[s]][:, 0:w]
                if kind == "rms0":
                    pe.wait_ge(S["sq_done"], u + 1)
                    ins = mm(dst, ones[:, :], sq[:, c0:c0 + w], start=True, stop=True)
                else:
                    _, nt, _ = lat[kind]
                    for j in range(nt):
                        k = square_at(kind, c, j)
                        pe.wait_ge(S["lat_sq"], k + 1)
                        ins = mm(dst, ones[:, :], lsq[:, k % 2, 0:w], start=(j == 0), stop=(j == nt - 1))
                        if j < nt - 1:
                            ins.then_inc(S["lsq_used"], 1)
                ins.then_inc(S["proj_done"], 1)

            def turn_v(s):
                _, layer, u = s
                if s == ("VT", 0, 0):
                    pe.wait_ge(S["const_pool"], 4)
                    pe.wait_ge(S["consts"], 16 * N_CONSTS)
                pe.wait_ge(S["proj_evac"], last_turn("vn" if layer else "v0", u) + 1)
                v = bufs(layer)["vt"]
                for k, tiles in enumerate(V_TILES):
                    t = T_TURN[s, k]
                    if T_BEFORE[t] is not None:
                        pe.wait_ge(S["tr_lo"], T_BEFORE[t] + 1)
                    for j, tile in enumerate(tiles):
                        c0, _ = (0, META) if tile == 0 else (META + 128 * (tile - 1), 128)
                        ins = nc.tensor.transpose(bank[T_BANK[t]][:, 128 * j:128 * j + 128], v[:, c0:c0 + 128], eye[:, :])
                    ins.then_inc(S["tr_done"], 1)

            def scores(t, m, c):
                g, i, slot = TSTEPS[t]
                layer, kind, u, head, _ = GROUPS[g]
                q0, rows = query_cols(i)
                chunks = score_chunks(i)
                c0, w = chunks[c]
                if m == 0 and c == 0 and head == 0:
                    cq = chunk_of(i)
                    if layer:
                        pe.wait_ge(S["proj_evac"], PTURN["P", "qn", u, cq] + 1)
                    pe.wait_ge(S["q_copied"], Q_COPY["P", "qr" if layer else "q0", u - u % 2 if layer else u, cq])
                b = S_CHUNK[t, m, c]
                if S_BEFORE[b] is not None:
                    pe.wait_ge(S["s_free_" + S_OWNER[S_BEFORE[b]]], S_FREED[S_BEFORE[b]])
                dst = bank[S_BANK[b]][:, 0:w]
                qc = slice(q0, q0 + 128)
                masked = c == len(chunks) - 1 and not (i == META_Q and kind == "A")
                if kind == "C":
                    prods = [(qh[:, a, qc], kh[:, u % 2, b_, c0:c0 + w]) for a, b_ in ((0, 0), (0, 1), (1, 0))]
                    prods += [(qpe[:, u % 2, a, qc], kpe[:, c0:c0 + w]) for a in (0, 1)]
                else:
                    j = m if kind == "A" else head
                    prods = [(qst[:, j, a, qc], kst[:, u % 2, j, c0:c0 + w]) for a in (0, 1)]
                for k, (l, r) in enumerate(prods):
                    ins = mm(dst, l, r, start=(k == 0), stop=(k == len(prods) - 1 and not masked))
                if masked:
                    dw = META if i == META_Q else 128
                    ins = mm(bank[S_BANK[b]][:, w - dw:w], eyebf[:, :],
                             mask[:, 1 if kind == "B" else 0, 0:dw], start=False, stop=True)
                ins.then_inc(S["s_done"], 1)

            def turn_weights(g, k):
                layer, kind, u, head, blocks = GROUPS[g]
                weights = bufs(layer)["pb"]
                t = T_TURN[g, k]
                if k == 0:
                    for t_ in GROUP_STEPS[g]:
                        p_ready(pe, t_)
                if T_BEFORE[t] is not None:
                    pe.wait_ge(S["tr_lo"], T_BEFORE[t] + 1)
                at = 0
                for tile in turns_of(blocks)[k]:
                    for slot, i in enumerate(blocks):
                        if i != META_Q and tile > i + 1:
                            continue
                        rows = META if i == META_Q else 128
                        k0, wide = (0, META) if tile == 0 else (META + 128 * (tile - 1), 128)
                        ins = nc.tensor.transpose(bank[T_BANK[t]][0:wide, at:at + rows],
                                                  weights[0:rows, g % 2, slot, k0:k0 + wide], eye[0:rows, 0:rows])
                        at += rows
                ins.then_inc(S["tr_done"], 1)

            def product(g, k):
                layer, kind, u, head, blocks = GROUPS[g]
                B = bufs(layer)
                turns = turns_of(blocks)
                w_all = META if blocks == [META_Q] else 256
                t, r = T_TURN[g, k], RING[g, k]
                pe.wait_ge(S["tr_hi"], t + 1)
                if k == 0 and g >= 1:
                    pe.wait_ge(S["o_evac"], g)
                for part in (0, 1):
                    if part == 1:
                        pe.wait_ge(S["tr_lo"], t + 1)
                    at = 0
                    for tile in turns[k]:
                        wide = w_all if (tile == 0 or tile <= blocks[0] + 1) else 128
                        o0 = w_all - wide
                        rows = META if tile == 0 else 128
                        v = B["vtok"]
                        if kind == "B":
                            prods = [v[0:rows, u % 2, head, tile, :]]
                        else:
                            prods = [v[0:rows, u % 2, a, tile, :] for a in ((0,) if part else (0, 1))]
                        for j, l in enumerate(prods):
                            ins = mm(PO[:, o0:o0 + wide], l, B["ring"][0:rows, r % NRING, part, at:at + wide],
                                     start=(k == 0 and tile == turns[0][0] and part == 0 and j == 0),
                                     stop=(k == len(turns) - 1 and tile == turns[k][-1] and part == 1))
                        at += wide
                ins.then_inc(S["pv_done"], 1)

            def out_block(s):
                _, layer, b = s
                n = O_AT[s]
                pe.wait_ge(S["w_ready"], WEIGHT_AT["y", n] + 1)
                if n in (0, NB + 1):
                    pe.wait_ge(S["w_ready"], WEIGHT_AT[("wo1" if layer else "wo0"), KD - 1] + 1)
                if n - (NB + 1) * layer >= 2:
                    pe.wait_ge(S["y_evac"], n - 1)
                elif n % 2 == 1:
                    pe.wait_ge(S["proj_evac"], (LAST1 if layer else LAST0) + 1)
                else:
                    for b_ in (-1, -2, -3):
                        x_ = len(S_OWNER) + b_ if layer else S_CHUNK[FIRST_C, 0, 0] + b_
                        pe.wait_ge(S["s_free_" + S_OWNER[x_]], S_FREED[x_])
                for half in range(2):
                    dst = out_bank(n, half)
                    for k in range(KD):
                        for a, c in ((0, 0), (0, 1), (1, 0)):
                            ins = mm(dst[:, :], wsp[:, SLOT["y", n], a, k, :], wok[:, c, k, 512 * half:512 * half + 512],
                                     start=(k == 0 and a == 0 and c == 0), stop=(k == KD - 1 and a == 1))
                ins.then_inc(S["y_done"], 1)

            def turn_h(s):
                _, layer, b = s
                n = O_AT[s]
                rows = META if b == META_Q else 128
                pe.wait_ge(S["h_ready"], n + 1)
                for k in range(2):
                    t = T_TURN[s, k]
                    pe.wait_ge(S["tr_lo"], T_BEFORE[t] + 1)
                    for j in range(4):
                        ins = nc.tensor.transpose(bank[T_BANK[t]][:, 128 * j:128 * j + rows],
                                                  res[0:rows, n % 2, 128 * (4 * k + j):128 * (4 * k + j) + 128],
                                                  eye[0:rows, 0:rows])
                    ins.then_inc(S["tr_done"], 1)

            waiting = []
            ahead = None

            def advance(count):
                for _ in range(count):
                    next(ahead, None)

            for at, s in enumerate(PLAN):
                if FILL[at] and ahead is None:
                    ahead = project(FILL[at][0])
                if s[0] == "P":
                    if s[1] in NORMS:
                        norm_sum(s)
                    else:
                        for _ in ahead or project(s):
                            pass
                        ahead = None
                elif s[0] == "VT":
                    turn_v(s)
                elif s[0] == "S":
                    scores(*s[1:])
                elif s[0] == "T":
                    turn_weights(*s[1:])
                elif s[0] == "X":
                    product(*s[1:])
                elif s[0] == "O":
                    out_block(s)
                    if s[1] == 0:
                        if waiting:
                            turn_h(waiting.pop())
                        waiting.append(s)
                elif s[0] == "OT":
                    turn_h(waiting.pop())
                if FILL[at]:
                    advance(FILL[at][1])


def kernel(**inputs):
    import ml_dtypes
    import concourse.bacc as _bacc
    from concourse.bass_utils import run_bass_kernel_spmd as _run

    a = {k: np.asarray(v) for k, v in inputs.items()}

    def tiles(w):
        k = w.shape[0] // 128
        return w.reshape(k, 128, w.shape[1]).transpose(1, 0, 2).reshape(128, -1)

    h = np.concatenate([a["meta"], a["x"][0]], 0)
    ht = h.T.reshape(KD, 128, TOK).transpose(1, 0, 2)
    w_in = a["ev_w_in"][0]
    part = {"A": [0, 512, 1024, 1536], "B": [2048, 2560, 3072, 3584]}
    w0 = np.stack([np.stack([tiles(w_in[:, o + 128 * (u % 4):o + 128 * (u % 4) + 128])
                             for o in part["A" if u < A_UNITS else "B"]]) for u in range(UNITS)])
    w_od = a["od_w_in"][0]
    starts = [128 * j for j in range(QL_T + KVL_T)]
    w1 = [tiles(w_od[:, o:o + 128]) for o in starts]
    pe_cols = w_od[:, 768:832]
    w1.append(tiles(np.concatenate([pe_cols, pe_cols], 1)))
    w1 += [tiles(w_od[:, 832 + 128 * h_:960 + 128 * h_]) for h_ in range(HEADS)]
    w1 = np.stack(w1)
    wuq = a["od_w_uq"][0]
    wuq_n = np.stack([tiles(wuq[:, 192 * h_:192 * h_ + 128]) for h_ in range(HEADS)])
    wuq_r = np.stack([tiles(np.concatenate([wuq[:, 192 * h_ + 128:192 * h_ + 192] for h_ in (2 * j, 2 * j + 1)], 1))
                      for j in range(HEADS // 2)])
    wkv = a["od_w_ukv"][0]
    wukv = np.stack([np.stack([tiles(wkv[:, 256 * h_ + 128 * z:256 * h_ + 128 * z + 128]) for z in range(2)])
                     for h_ in range(HEADS)])
    wo0 = a["ev_w_out"][0].reshape(KD, 128, D).transpose(1, 0, 2)
    wo1 = a["od_w_out"][0].reshape(KD, 128, D).transpose(1, 0, 2)
    lam = np.stack([a["ev_lam_q1"][0], a["ev_lam_k1"][0], a["ev_lam_q2"][0], a["ev_lam_k2"][0]])[None]
    r, c = np.arange(128)[:, None], np.arange(TOK)[None, :]
    dist = -np.abs(128 * (NB - 1) + META + r - c).astype(np.float16)
    k = np.arange(128)[None, :]
    masks = np.stack([np.where((k // CHUNK) > (r // CHUNK), MASKED, 0.0), np.where(k >= r, MASKED, 0.0)], 1)\
        .astype(ml_dtypes.bfloat16)
    eyeb = np.eye(128).astype(ml_dtypes.bfloat16)
    inv = (np.float32(10000.0) ** (-np.arange(32, dtype=np.float32) / np.float32(32))).astype(np.float32)
    ang = np.arange(TOK, dtype=np.float32)[None, :] * inv[:, None]
    cos, sin = np.cos(ang), np.sin(ang)
    rope = np.stack([np.tile(cos, (4, 1)), np.tile(np.concatenate([-sin, sin], 0), (2, 1))], 1).astype(np.float32)
    arrays = dict(ht=ht, x=a["x"][0], meta=a["meta"], w0=w0, w1=w1, wuq_n=wuq_n, wuq_r=wuq_r, wukv=wukv,
                  wo0=wo0, wo1=wo1, lng=a["ln_g"], lnb=a["ln_b"], lam=lam, subln=a["ev_subln"].reshape(128, 1),
                  qnorm=a["od_q_norm"][0].reshape(QL_T, 128).T, kvnorm=a["od_kv_norm"][0].reshape(KVL_T, 128).T,
                  dist=dist, masks=masks, eyeb=eyeb, rope=rope)
    nc = _bacc.Bacc("TRN2", target_bir_lowering=False, num_devices=1)
    feed, args = {}, {}
    for name, v in arrays.items():
        v = np.ascontiguousarray(v)
        feed["in_" + name] = v
        args[name] = nc.dram_tensor("in_" + name, v.shape, mybir.dt.from_np(v.dtype), kind="ExternalInput").ap()
    args["out"] = nc.dram_tensor("out_0", (SEQ, D), F32, kind="ExternalOutput").ap()
    args["lam"] = args["lam"].to_broadcast([128, 4, DH])
    trunk_kernel(nc, **args)
    r_ = _run(nc, [feed], core_ids=[0])
    return r_.results[0]["out_0"].reshape(1, SEQ, D)
```
